# Optimizing a Trainium2 kernel written in Bass

```python
import math
import jax, jax.numpy as jnp
from jax import lax
import numpy as np

D_MODEL = 1024
BATCH = 1
SEQ = 1024
DEPTH = 1

N_ATTN_HEADS = 8
ATTN_HEAD_DIM = 64
N_KV_GROUPS = 2
Q_LORA_RANK = 256
N_IDX_HEADS = 8
IDX_HEAD_DIM = 64
TOPK_MAX = 256
Q_BLOCK = 128
N_BUCKETS = 32
MAX_DISTANCE = 128
N_REC_HEADS = 4
REC_HEAD_DIM = 128
CHUNK = 64
FFN_HIDDEN = -(-8 * D_MODEL // (3 * 256)) * 256

ATTN_WIDTH = N_ATTN_HEADS * ATTN_HEAD_DIM
KV_WIDTH = N_KV_GROUPS * ATTN_HEAD_DIM
IDX_Q_WIDTH = N_IDX_HEADS * IDX_HEAD_DIM
REC_WIDTH = N_REC_HEADS * REC_HEAD_DIM
IN_SPLITS = [Q_LORA_RANK, KV_WIDTH, KV_WIDTH, IDX_HEAD_DIM, N_IDX_HEADS,
             REC_WIDTH, REC_WIDTH, REC_WIDTH, REC_WIDTH, 2 * D_MODEL]
IN_WIDTH = sum(IN_SPLITS)
IN_POINTS = [int(p) for p in np.cumsum(IN_SPLITS)[:-1]]
EPS = 1e-6

kernel_name = "hybrid_dsa_hgrn2_gated_block"

def rmsnorm(x, w):
    xf = x.astype(jnp.float32)
    y = xf * lax.rsqrt(jnp.mean(xf * xf, axis=-1, keepdims=True) + EPS)
    return (y * w.astype(jnp.float32)).astype(x.dtype)

def t5_bucket(n):
    max_exact = N_BUCKETS // 2
    nf = jnp.maximum(n, 1).astype(jnp.float32)
    large = max_exact + (jnp.log(nf / max_exact) / math.log(MAX_DISTANCE / max_exact)
                         * (N_BUCKETS - max_exact)).astype(jnp.int32)
    large = jnp.minimum(large, N_BUCKETS - 1)
    return jnp.where(n < max_exact, n, large)

def dsa_attention(q, k, v, qi, ki, wi, rel_bias):
    B, S = q.shape[0], q.shape[1]
    k_sel = min(TOPK_MAX, S // 4)
    nblk = S // Q_BLOCK
    R = N_ATTN_HEADS // N_KV_GROUPS
    key_pos = jnp.arange(S, dtype=jnp.int32)
    idx_scale = IDX_HEAD_DIM ** -0.5
    attn_scale = ATTN_HEAD_DIM ** -0.5
    wi = wi * (N_IDX_HEADS ** -0.5)

    def to_blocks(a):
        return a.reshape(B, nblk, Q_BLOCK, *a.shape[2:]).swapaxes(0, 1)

    def block(args):
        qb, qib, wib, start = args
        pos_q = start + jnp.arange(Q_BLOCK, dtype=jnp.int32)
        logits = jnp.einsum('bqhd,bsd->bqhs', qib, ki) * idx_scale
        score = jnp.einsum('bqhs,bqh->bqs', jax.nn.relu(logits), wib).astype(jnp.float32)
        causal = key_pos[None, :] <= pos_q[:, None]
        score = jnp.where(causal[None], score, -jnp.inf)
        _, idx = lax.top_k(score, k_sel)
        ksel = jax.vmap(lambda kb, ib: kb[ib])(k, idx)
        vsel = jax.vmap(lambda vb, ib: vb[ib])(v, idx)
        dist = pos_q[None, :, None] - idx
        valid = dist >= 0
        bias = rel_bias[t5_bucket(jnp.maximum(dist, 0))].astype(jnp.float32)
        bias = bias.reshape(B, Q_BLOCK, k_sel, N_KV_GROUPS, R).transpose(0, 1, 3, 4, 2)
        qg = qb.reshape(B, Q_BLOCK, N_KV_GROUPS, R, ATTN_HEAD_DIM)
        s = jnp.einsum('bqgrd,bqkgd->bqgrk', qg, ksel).astype(jnp.float32) * attn_scale + bias
        s = jnp.where(valid[:, :, None, None, :], s, -jnp.inf)
        p = jax.nn.softmax(s, axis=-1).astype(vsel.dtype)
        o = jnp.einsum('bqgrk,bqkgd->bqgrd', p, vsel)
        return o.reshape(B, Q_BLOCK, ATTN_WIDTH)

    starts = jnp.arange(nblk, dtype=jnp.int32) * Q_BLOCK
    out = lax.map(block, (to_blocks(q), to_blocks(qi), to_blocks(wi), starts))
    return out.swapaxes(0, 1).reshape(B, S, ATTN_WIDTH)

def hgrn2(q_raw, f_raw, i_raw, lb):
    B, S = q_raw.shape[0], q_raw.shape[1]
    n = S // CHUNK
    H, dk = N_REC_HEADS, REC_HEAD_DIM
    f = lb + (1.0 - lb) * jax.nn.sigmoid(f_raw.astype(jnp.float32))
    g = jnp.log(f)
    kk = 1.0 - f
    qq = jax.nn.silu(q_raw.astype(jnp.float32))
    vv = i_raw.astype(jnp.float32)

    def to_chunks(a):
        return a.reshape(B, n, CHUNK, H, dk).transpose(1, 0, 3, 2, 4)

    mask = jnp.tril(jnp.ones((CHUNK, CHUNK), dtype=bool))

    def step(state, inp):
        qc, kc, vc, gc = inp
        A = jnp.cumsum(gc, axis=-2)
        o_inter = jnp.einsum('bhtc,bhcv->bhtv', qc * jnp.exp(A), state)
        diff = A[:, :, :, None, :] - A[:, :, None, :, :]
        decay = jnp.exp(jnp.where(mask[:, :, None], diff, -jnp.inf))
        P = jnp.einsum('bhtc,bhsc,bhtsc->bhts', qc, kc, decay)
        o = o_inter + jnp.einsum('bhts,bhsv->bhtv', P, vc)
        A_last = A[:, :, -1:, :]
        new_state = jnp.exp(A_last[:, :, 0, :])[..., None] * state + \
            jnp.einsum('bhsc,bhsv->bhcv', kc * jnp.exp(A_last - A), vc)
        return new_state, o

    s0 = jnp.zeros((B, H, dk, dk), jnp.float32)
    _, o = lax.scan(step, s0, (to_chunks(qq), to_chunks(kk), to_chunks(vv), to_chunks(g)))
    return o.transpose(1, 0, 3, 2, 4).reshape(B, S, H, dk)

def setup_inputs(seed: int = 0) -> dict:
    key = jax.random.key(seed)
    ks = jax.random.split(key, 20)
    f32 = jnp.float32

    def w(k, shape, fan_in):
        return jax.random.normal(k, shape, f32) * (fan_in ** -0.5)

    def gain(k, shape):
        return 1.0 + 0.02 * jax.random.normal(k, shape, f32)

    return {
        "x": jax.random.normal(ks[0], (BATCH, SEQ, D_MODEL), f32),
        "c": jax.random.normal(ks[1], (BATCH, D_MODEL), f32),
        "w_ada": w(ks[2], (DEPTH, D_MODEL, 6 * D_MODEL), D_MODEL),
        "b_ada": 0.02 * jax.random.normal(ks[3], (DEPTH, 6 * D_MODEL), f32),
        "norm1_w": gain(ks[4], (DEPTH, D_MODEL)),
        "w_in": w(ks[5], (DEPTH, D_MODEL, IN_WIDTH), D_MODEL),
        "q_norm_w": gain(ks[6], (DEPTH, Q_LORA_RANK)),
        "w_uq": w(ks[7], (DEPTH, Q_LORA_RANK, ATTN_WIDTH), Q_LORA_RANK),
        "w_uq_idx": w(ks[8], (DEPTH, Q_LORA_RANK, IDX_Q_WIDTH), Q_LORA_RANK),
        "rel_bias": 0.5 * jax.random.normal(ks[9], (N_BUCKETS, N_ATTN_HEADS), f32),
        "lb_logits": 0.5 * jax.random.normal(ks[10], (DEPTH + 1, REC_WIDTH), f32),
        "rec_norm_w": gain(ks[11], (DEPTH, REC_HEAD_DIM)),
        "w_branch_attn": w(ks[12], (DEPTH, ATTN_WIDTH, D_MODEL), ATTN_WIDTH),
        "w_branch_rec": w(ks[13], (DEPTH, REC_WIDTH, D_MODEL), REC_WIDTH),
        "w_out": w(ks[14], (DEPTH, D_MODEL, D_MODEL), D_MODEL),
        "norm2_w": gain(ks[15], (DEPTH, D_MODEL)),
        "w_ffn_gate": w(ks[16], (DEPTH, D_MODEL, FFN_HIDDEN), D_MODEL),
        "w_ffn_up": w(ks[17], (DEPTH, D_MODEL, FFN_HIDDEN), D_MODEL),
        "w_ffn_down": w(ks[18], (DEPTH, FFN_HIDDEN, D_MODEL), FFN_HIDDEN),
        "final_norm_w": gain(ks[19], (D_MODEL,)),
    }

def reference(x, c, w_ada, b_ada, norm1_w, w_in, q_norm_w, w_uq, w_uq_idx, rel_bias,
              lb_logits, rec_norm_w, w_branch_attn, w_branch_rec, w_out, norm2_w,
              w_ffn_gate, w_ffn_up, w_ffn_down, final_norm_w):
    B, S, _ = x.shape
    lower_bounds = jnp.cumsum(jax.nn.softmax(lb_logits.astype(jnp.float32), axis=0), axis=0)
    c_act = jax.nn.silu(c)
    for layer in range(DEPTH):
        mod = (c_act @ w_ada[layer] + b_ada[layer])[:, None, :]
        sh1, sc1, g1, sh2, sc2, g2 = jnp.split(mod, 6, axis=-1)
        h = rmsnorm(x, norm1_w[layer]) * (1.0 + sc1) + sh1
        proj = h @ w_in[layer]
        cq, k, v, ki, wi, rq, rf, ri, rg, gates = jnp.split(proj, IN_POINTS, axis=-1)
        cq = rmsnorm(cq, q_norm_w[layer])
        q = (cq @ w_uq[layer]).reshape(B, S, N_ATTN_HEADS, ATTN_HEAD_DIM)
        qi = (cq @ w_uq_idx[layer]).reshape(B, S, N_IDX_HEADS, IDX_HEAD_DIM)
        k = k.reshape(B, S, N_KV_GROUPS, ATTN_HEAD_DIM)
        v = v.reshape(B, S, N_KV_GROUPS, ATTN_HEAD_DIM)
        attn = dsa_attention(q, k, v, qi, ki, wi, rel_bias)
        y_attn = attn @ w_branch_attn[layer]
        rec = hgrn2(rq, rf, ri, lower_bounds[layer]).astype(x.dtype)
        rec = rmsnorm(rec, rec_norm_w[layer]).reshape(B, S, REC_WIDTH) * jax.nn.silu(rg)
        y_rec = rec @ w_branch_rec[layer]
        g_attn, g_rec = jnp.split(jax.nn.sigmoid(gates), 2, axis=-1)
        mixed = (g_attn * y_attn + g_rec * y_rec) @ w_out[layer]
        x = x + g1 * mixed
        h2 = rmsnorm(x, norm2_w[layer]) * (1.0 + sc2) + sh2
        ffn = (jax.nn.silu(h2 @ w_ffn_gate[layer]) * (h2 @ w_ffn_up[layer])) @ w_ffn_down[layer]
        x = x + g2 * ffn
    return rmsnorm(x, final_norm_w)


_drawn_inputs = setup_inputs


def setup_inputs(seed=0):
    import zlib

    import numpy as np

    out = dict(_drawn_inputs(seed))
    spreads = {}
    factors = {'norm1_w': 5.87,
     'q_norm_w': 8.0,
     'lb_logits': 5.801,
     'rec_norm_w': 8.0,
     'norm2_w': 15.811,
     'final_norm_w': 7.777,
     'rel_bias': 6.254}
    for name, (base, spread) in spreads.items():
        noise = np.random.default_rng([zlib.crc32(name.encode()), seed]).standard_normal(out[name].shape)
        drawn = base * np.exp(spread * noise) if base else spread * noise
        out[name] = __import__('jax').numpy.asarray(drawn.astype(out[name].dtype))
    for name, factor in factors.items():
        out[name] = (out[name] * factor).astype(out[name].dtype)
    return out
```

```python
import math
from contextlib import ExitStack

import numpy as np

import concourse.bass as bass
from concourse import mybir

F32 = mybir.dt.float32
I32 = mybir.dt.int32
U8 = mybir.dt.uint8
ALU = mybir.AluOpType
ACT = mybir.ActivationFunctionType
AX = mybir.AxisListType

P = 128
SEQ = 1024
D = 1024
KD = D // P
NT = SEQ // P
HALF = 512
NH = 8
HD = 64
LORA = 256
NIH = 8
TOPK = 256
NB = 32
MAXD = 128
RH = 4
RW = RH * P
FF = 2816
KF = FF // P
EPS = 1e-6
C_CQ, C_K, C_V, C_KI, C_WI = 0, 256, 384, 512, 576
C_RQ, C_RF, C_RI, C_RG, C_GATE = 584, 1096, 1608, 2120, 2632

NONCAUSAL = -3.0e38
PICKED = -3.4e38
MASKED = -1.0e30

V_C, V_N1, V_N2, V_QN, V_RN, V_LB, V_BADA, V_END = 0, 8, 16, 24, 26, 27, 35, 83


class Ring:

    def __init__(self, slots):
        self.order, self.src, self.dst, self.slot, self.full, self.free = [], {}, {}, {}, {}, {}
        self.fills, self.last = [0] * slots, [(None, None)] * slots

    def add(self, name, slot, src, dst, done, over=None):
        self.order.append(name)
        self.src[name], self.dst[name], self.slot[name] = src, dst, slot
        self.fills[slot] += len(dst) if isinstance(dst, list) else 1
        self.full[name] = 16 * self.fills[slot]
        free = {}
        for s in over or [slot]:
            now, before = self.last[s]
            if now != done:
                now, before = done, now
            self.last[s] = (now, before)
            if before:
                free[before[0].name] = max(before, free.get(before[0].name, before), key=lambda x: x[1])
        self.free[name] = list(free.values())


def block_kernel(nc, T):
    ctx = ExitStack()
    with ctx:
        build(nc, ctx, T)


def build(nc, ctx, T):
    def sb(name, shape, dt=F32):
        return ctx.enter_context(nc.sbuf_tensor(name, shape, dt))

    def sem(name):
        return ctx.enter_context(nc.semaphore(name))

    arena = sb("arena", [P, 47616])

    def at(off, *dims):
        n = 1
        for d in dims:
            n *= d
        ap = arena[:, off:off + n]
        if len(dims) == 2:
            ap = ap.rearrange("p (a b) -> p a b", a=dims[0])
        if len(dims) == 3:
            ap = ap.rearrange("p (a b c) -> p a b c", a=dims[0], b=dims[1])
        return ap

    A0, B0, C0, D0, E0, F0, G0, H0 = 0, 8192, 12288, 16384, 20480, 25088, 29184, 43520
    hT = at(A0, KD, SEQ)
    x_tok = at(B0, NT, D)
    qT = at(B0, 4, SEQ)
    qiT = at(C0, 4, SEQ)
    kT = [at(D0, SEQ), at(D0 + 1024, SEQ)]
    kiT = at(D0 + 2048, SEQ)
    v_tok = at(D0 + 3072, NT, P)
    W_OFF = [sum(P * (j + 1) for j in range(b)) for b in range(NT)]
    W = [at(E0 + W_OFF[b], P * (b + 1)) for b in range(NT)]
    cq_tok = at(G0, NT, LORA)
    cqT = at(G0 + 2048, 2, SEQ)
    relu_buf = [at(G0 + 4096 + 1024 * i, SEQ) for i in range(2)]
    sq_junk = at(G0 + 6144, D)
    ri_tok = at(F0, NT, RW)
    rg_tok = at(C0, NT, RW)
    sgT = [at(G0 + 1024 * i, SEQ) for i in range(2)]
    rqT = [at(G0 + 2048 + 1024 * i, SEQ) for i in range(2)]
    kkT = at(G0 + 4096, SEQ)
    cumT = at(G0 + 5120, SEQ)
    expT = [at(G0 + 6144 + 1024 * i, SEQ) for i in range(2)]
    zT = [at(G0 + 8192 + 1024 * i, SEQ) for i in range(2)]
    bias_rev = at(G0 + 8192, NH, 256)
    flip = at(G0 + 10240, P)
    qaT = at(G0 + 10240, SEQ)
    mask_wide = at(G0 + 11264, 8, P)
    kl_tok = at(G0 + 11264, NT, P)
    pT_rec = at(G0 + 12288, NT, P)
    states = at(G0 + 13312, NT, P)
    recT = at(G0, RH, SEQ)
    o_sq = at(G0 + 4096, NT * RW)
    s_buf = [at(G0 + 4096 + 1024 * i, SEQ) for i in range(2)]
    p_buf = [at(G0 + 6144 + 1024 * i, SEQ) for i in range(2)]
    pT = [at(G0 + 8192 + 1024 * i, NT, P) for i in range(2)]
    near = [at(G0 + 10240 + 256 * i, 256) for i in range(2)]
    attn_tok = at(G0 + 10752, 512)
    g1_row = at(G0 + 11776, D)
    g2_row = at(G0 + 12800, D)
    attnT = at(A0, 4, SEQ)
    w_br = [at(F0, 4, D), at(A0 + 4096, 4, D)]
    gate_out = [at(D0 + 2048 + HALF * i, HALF) for i in range(2)]
    gate_in = [at(G0 + 4096 + 1024 * i, 2, HALF) for i in range(2)]
    y_tmp = [at(G0 + 6144 + 1024 * i, 2, HALF) for i in range(2)]
    mixT = at(B0, KD, SEQ)
    w_o = at(D0, KD, D)
    x1 = at(A0, NT, D)
    xn2 = at(G0, 4, D)
    h2T = [at(G0 + 4096, KD, HALF), at(B0, KD, HALF)]
    hidT = at(C0, KF, HALF)
    silu_buf = [at(G0 + 8192 + 512 * i, HALF) for i in range(2)]
    wd_ring = at(F0, 8, HALF)
    fin_row = at(G0 + 9216, D)
    ff_tmp = at(G0 + 10240, HALF)
    junk2 = at(G0 + 10752, D)

    ring_buf = at(H0, 4, 8, P)
    ring_flat = at(H0, 8, 512)
    ring_pair = [at(H0, 8, 256), at(H0 + 2048, 8, 256)]
    ring_uq = [at(H0 + 1024 * i, 2, 512) for i in range(4)]

    ident = sb("ident", [P, P])
    vrows = sb("vrows", [P, P])
    vcol = sb("vcol", [P, V_END])
    c_act = sb("c_act", [P, KD])
    c_wide = sb("c_wide", [P, KD, P])
    mod = sb("mod", [P, 32])
    gain1 = sb("gain1", [P, KD])
    gain2 = sb("gain2", [P, KD])
    lb = sb("lb", [P, RH])
    one_lb = sb("one_lb", [P, RH])
    lb_e = sb("lb_e", [P, 2 * RH])
    ss = sb("ss", [P, 64])
    rstd = sb("rstd", [P, 64])
    wi = sb("wi", [P, NT, NIH])
    top8 = sb("top8", [P, 8])
    scan_gate = sb("scan_gate", [P, SEQ])
    decay = sb("decay", [P, NT])
    lvl_mask = sb("lvl_mask", [P, 8, P], U8)
    bias8 = sb("bias8", [P, NH, 256])
    brow = sb("brow", [NH, 384])
    rb_sb = sb("rb_sb", [NB, NH])
    bk_sb = at(G0 + 7168, 384)[0:NB, :]
    nmax = sb("nmax", [P, 16])
    rsum = sb("rsum", [P, 16])
    rinv = sb("rinv", [P, 8])
    far_max = sb("far_max", [P, 2])

    pp = [ctx.enter_context(nc.psum_tensor(f"pp{i}", [P, 1024], F32)) for i in range(4)]
    bank = [pp[i // 2][:, (i % 2) * 512:(i % 2) * 512 + 512] for i in range(8)]

    bias_d = nc.dram_tensor("bias_rows", [NH, 384], F32, kind="Internal").ap()
    gates_d = nc.dram_tensor("gates_t", [2 * D, SEQ], F32, kind="Internal").ap()

    x_d = T["x"][0].rearrange("(t p) d -> t p d", p=P)
    out_d = T["out"][0].rearrange("(t p) d -> t p d", p=P)

    def wtile(w, c0, n=P):
        return w[:, c0:c0 + n].rearrange("(k p) c -> p k c", p=P)

    w_in = T["w_in"][0]
    w_ada = T["w_ada"][0]

    ring_full = [sem(f"ring_full{i}") for i in range(4)]
    vec_loaded = sem("vec_loaded")
    rb_loaded = sem("rb_loaded")
    x_loaded = [sem(f"x_loaded{t}") for t in range(NT)]
    mask_loaded = sem("mask_loaded")
    brow_stored = sem("brow_stored")
    bias_loaded = sem("bias_loaded")
    flip_ready = sem("flip_ready")
    bias_full = sem("bias_full")
    bias_ready = sem("bias_ready")
    ident_ready = sem("ident_ready")
    masks01 = sem("masks01")
    vt_full = sem("vt_full")
    vcol_ready = sem("vcol_ready")
    cact_ready = sem("cact_ready")
    cwide_ready = sem("cwide_ready")
    brow_full = sem("brow_full")
    brow_ready = sem("brow_ready")
    pj_full = sem("pj_full")
    pj_free = sem("pj_free")
    tr_full = sem("tr_full")
    tr_free = sem("tr_free")
    xsq_done = sem("xsq_done")
    std1_done = sem("std1_done")
    ssum1 = sem("ssum1")
    xn_ready = sem("xn_ready")
    gain1_ready = sem("gain1_ready")
    lbe_ready = sem("lbe_ready")
    lb_ready = sem("lb_ready")
    cqsq_done = sem("cqsq_done")
    ssum2 = sem("ssum2")
    std2_done = sem("std2_done")
    cqn_ready = sem("cqn_ready")
    sc_full = sem("sc_full")
    sc_relu = sem("sc_relu")
    sc_added = sem("sc_added")
    sc_masked = sem("sc_masked")
    topk_step = sem("topk_step")
    topk_pace = sem("topk_pace")
    topk_done = sem("topk_done")
    dve_step = sem("dve_step")
    act_step = sem("act_step")
    pool_step = sem("pool_step")
    ada_done = sem("ada_done")
    mod_copied = sem("mod_copied")
    gr_full = sem("gr_full")
    gb_loaded = sem("gb_loaded")
    gate_stored = [sem(f"gate_stored{i}") for i in range(2)]
    f_ready = sem("f_ready")
    kk_ready = sem("kk_ready")
    g_ready = sem("g_ready")
    cum_ready = sem("cum_ready")
    diff_ready = sem("diff_ready")
    exp_ready = sem("exp_ready")
    z_ready = sem("z_ready")
    kl_full = sem("kl_full")
    kl_free = sem("kl_free")
    u_full = sem("u_full")
    state_ready = sem("state_ready")
    lv_full = sem("lv_full")
    lv_free = sem("lv_free")
    ro_full = sem("ro_full")
    ro_free = sem("ro_free")
    osq_ready = sem("osq_ready")
    ssum3 = sem("ssum3")
    std3_done = sem("std3_done")
    on_ready = sem("on_ready")
    rt_full = sem("rt_full")
    rt_free = sem("rt_free")
    grow_ready = sem("grow_ready")
    bg_loaded = sem("bg_loaded")
    near_ready = sem("near_ready")
    s_full = sem("s_full")
    s_read = sem("s_read")
    p_ready = sem("p_ready")
    pt_full = sem("pt_full")
    pt_free = sem("pt_free")
    pv_full = sem("pv_full")
    o_read = sem("o_read")
    at_full = sem("at_full")
    attnT_ready = sem("attnT_ready")
    wbr_loaded = sem("wbr_loaded")
    wbr2_loaded = sem("wbr2_loaded")
    wo_loaded = [sem(f"wo_loaded{i}") for i in range(2)]
    gin_loaded = [sem(f"gin_loaded{i}") for i in range(2)]
    y_full = sem("y_full")
    mix_ready = sem("mix_ready")
    xr_loaded = [sem(f"xr_loaded{t}") for t in range(NT)]
    wo_full = sem("wo_full")
    x1_ready = sem("x1_ready")
    sq4_done = sem("sq4_done")
    ssum4 = sem("ssum4")
    std4_done = sem("std4_done")
    xn2_ready = sem("xn2_ready")
    mod2_ready = sem("mod2_ready")
    t2_full = sem("t2_full")
    t2_free = sem("t2_free")
    g_full = sem("g_full")
    up_full = sem("up_full")
    silu_ready = sem("silu_ready")
    hid_ready = sem("hid_ready")
    wd_full = [sem(f"wd_full{i}") for i in range(8)]
    wd_used = sem("wd_used")
    dn_full = sem("dn_full")
    x2_ready = sem("x2_ready")
    far_done = sem("far_done")
    std_done = sem("cum_std")
    sq5_done = sem("sq5_done")
    ssum5 = sem("ssum5")
    std5_done = sem("std5_done")
    y_ready = sem("y_ready")
    out_stored = sem("out_stored")
    fin_loaded = sem("fin_loaded")

    block = ctx.enter_context(nc.Block())

    G_A = 0
    G_B = G_A + NT
    G_UQI = G_B + 6
    G_UQ = G_UQI + 8
    G_RFQ = [G_UQ + 8, 0, 0, 0]
    G_RI = G_RFQ[0] + 4
    G_RFQ[1] = G_RI + 16
    G_RG = G_RFQ[1] + 4
    G_RFQ[2] = G_RG + 16
    G_GATE = [G_RFQ[2] + 4]
    G_RFQ[3] = G_GATE[0] + 8
    G_GATE += [G_RFQ[3] + 4 + 8 * q for q in range(3)]
    G_END = G_GATE[3] + 8

    ring = Ring(4)
    for j in range(16):
        ring.add(("ada", j), j % 4, wtile(w_ada, j * P), ring_buf[:, j % 4], (ada_done, j + 1))
    for s, (name, c0, n) in enumerate((("cq0", C_CQ, P), ("cq1", C_CQ + P, P), ("v", C_V, P), ("wi", C_WI, NIH))):
        ring.add(name, s, wtile(w_in, c0, n), ring_flat[:, :, s * P:s * P + n], (pj_full, G_A + NT), range(4))
    for s, (name, c0) in enumerate((("k0", C_K), ("k1", C_K + HD), ("ki", C_KI))):
        ring.add(name, s, wtile(w_in, c0, HD), [ring_buf[:, s, :, 0:HD], ring_buf[:, s, :, HD:P]], (pj_full, G_B + 2 * s + 2))
    ring.add("uqi", 3, T["w_uq_idx"][0].rearrange("(k p) c -> p k c", p=P), ring_uq[3], (pj_full, G_UQI + 8))
    ring.add("uq", 0, T["w_uq"][0].rearrange("(k p) c -> p k c", p=P), ring_uq[0], (pj_full, G_UQ + 8))

    def plan_rf_rq(h, s):
        ring.add(("rf", h), s, wtile(w_in, C_RF + h * P), ring_buf[:, s], (pj_full, G_RFQ[h] + 2))
        ring.add(("rq", h), s + 1, wtile(w_in, C_RQ + h * P), ring_buf[:, s + 1], (pj_full, G_RFQ[h] + 4))

    def plan_pair(name, w, c0, which, done):
        for m in range(2):
            ring.add((name, m), 2 * which + m, wtile(w, c0 + m * P), ring_pair[which][:, :, m * P:(m + 1) * P], done, (2 * which, 2 * which + 1))

    def plan_gates(q, s0):
        for j in range(4):
            s = (s0 + j) % 4
            ring.add(("gate", q, j), s, wtile(w_in, C_GATE + (4 * q + j) * P), ring_buf[:, s], (pj_full, G_GATE[q] + 2 * j + 2))

    plan_rf_rq(0, 2)
    for j in range(2):
        plan_pair(("ri", j), w_in, C_RI + 256 * j, j, (pj_full, G_RI + NT * (j + 1)))
    plan_rf_rq(1, 0)
    for j in range(2):
        plan_pair(("rg", j), w_in, C_RG + 256 * j, 1 - j, (pj_full, G_RG + NT * (j + 1)))
    plan_rf_rq(2, 2)
    plan_gates(0, 0)
    plan_rf_rq(3, 0)
    for q in range(1, 4):
        plan_gates(q, 2)
    for j in range(8):
        plan_pair(("g", j), w_ada, (2048 if j < 4 else 5120) + 256 * (j % 4), (j + 1) % 2, (gr_full, j + 1))
    for j in range(16):
        s = (j + 2) % 4
        ring.add(("ada", 16 + j), s, wtile(w_ada, (24 + j) * P), ring_buf[:, s], (ada_done, 17 + j))
    ff_fills = list(ring.fills)

    SCORED = list(range(TOPK // P, NT))
    TR_X, TR_CQ = 0, 16
    UNITS = 9
    ITEMS = [(b, h) for b in range(NT) for h in range(NH)]
    PT_GROUPS = [0]
    for b, h in ITEMS:
        PT_GROUPS.append(PT_GROUPS[-1] + (b + 4) // 4)

    @block.sync
    def _(sp):
        rows = [
            (V_C, T["c"].rearrange("o (r p) -> (o r) p", p=P), 8),
            (V_N1, T["norm1_w"].rearrange("o (r p) -> (o r) p", p=P), 8),
            (V_N2, T["norm2_w"].rearrange("o (r p) -> (o r) p", p=P), 8),
            (V_QN, T["q_norm_w"].rearrange("o (r p) -> (o r) p", p=P), 2),
            (V_RN, T["rec_norm_w"], 1),
            (V_LB, T["lb_logits"].rearrange("l (r p) -> (l r) p", p=P), 8),
            (V_BADA, T["b_ada"].rearrange("o (r p) -> (o r) p", p=P), 48),
        ]
        for r0, s, n in rows:
            sp.dma_start(vrows[r0:r0 + n, :], s).then_inc(vec_loaded, 16)
        for t in range(NT):
            sp.dma_start(x_tok[:, t, :], x_d[t]).then_inc(x_loaded[t], 16)
        sp.dma_start(mask_wide.bitcast(I32), T["level_masks"].rearrange("p (u t) -> p u t", u=8)).then_inc(mask_loaded, 16)

        def load(name):
            for signal, value in ring.free[name]:
                sp.wait_ge(signal, value)
            dst = ring.dst[name]
            for part in dst if isinstance(dst, list) else [dst]:
                sp.dma_start(part, ring.src[name]).then_inc(ring_full[ring.slot[name]], 16)

        def load_from(a, b):
            for name in ring.order[ring.order.index(a):ring.order.index(b)]:
                load(name)

        load_from(("ada", 0), ("ada", 4))
        sp.dma_start(rb_sb[:, :], T["rel_bias"]).then_inc(rb_loaded, 16)
        sp.dma_start(bk_sb, T["bucket_steps"]).then_inc(rb_loaded, 16)
        load_from(("ada", 4), "uq")
        sp.wait_ge(brow_ready, 1)
        sp.dma_start(bias_d, brow[:, :]).then_inc(brow_stored, 16)
        sp.wait_ge(brow_stored, 16)
        sp.dma_start(bias_rev, bass.AP(bias_d.tensor, 0, [[1, P], [384, NH], [1, 256]])).then_inc(bias_loaded, 16)
        load_from("uq", (("g", 2), 0))
        sp.wait_ge(ro_full, 2 * RH)
        for row, c0 in ((g1_row, 2 * D), (g2_row, 5 * D)):
            sp.dma_start(row, T["b_ada"][:, c0:c0 + D].broadcast_to([P, D])).then_inc(gb_loaded, 16)
        load_from((("g", 2), 0), ("ada", 31))
        load(("ada", 31))
        sp.wait_ge(rt_full, 2 * RH)
        sp.dma_start(w_br[0], T["w_branch_attn"][0].rearrange("(k p) c -> p k c", p=P)).then_inc(wbr_loaded, 16)
        sp.wait_ge(pj_full, G_END)
        sp.dma_start(w_br[1], T["w_branch_rec"][0].rearrange("(k p) c -> p k c", p=P)).then_inc(wbr_loaded, 16)
        gv = gates_d.rearrange("(g m p) t -> p m g t", g=2, p=P)
        sp.wait_ge(at_full, NT)
        for st in range(2):
            sp.wait_ge(gate_stored[st], 16 * 16)
        for n in range(16):
            m, hf = divmod(n, 2)
            if n >= 2:
                sp.wait_ge(mix_ready, n - 1)
            sp.dma_start(gate_in[n % 2], gv[:, m, :, hf * HALF:(hf + 1) * HALF]).then_inc(gin_loaded[n % 2], 16)
            if n in (1, 2):
                dh = n - 1
                sp.dma_start(w_o[:, :, dh * HALF:(dh + 1) * HALF], wtile(T["w_out"][0], dh * HALF, HALF)).then_inc(wo_loaded[dh], 16)
            if n == 2:
                sp.dma_start(fin_row, T["final_norm_w"].rearrange("(o d) -> o d", o=1).broadcast_to([P, D])).then_inc(fin_loaded, 16)
        sp.wait_ge(y_full, 32)
        for t in range(NT):
            sp.dma_start(x1[:, t, :], x_d[t]).then_inc(xr_loaded[t], 16)
        wg = T["w_ffn_gate"][0].rearrange("(k p) c -> p k c", p=P)
        wu = T["w_ffn_up"][0].rearrange("(k p) c -> p k c", p=P)
        wd = T["w_ffn_down"][0].rearrange("(f p) c -> p f c", p=P)
        for hf in range(2):
            def two_hidden(i):
                for j in range(2):
                    for w, used, s in ((wg, g_full, (2 + 2 * j) % 4), (wu, up_full, (3 + 2 * j) % 4)):
                        if isinstance(i, int) and hf == 0:
                            sp.wait_ge(ada_done, 32)
                        else:
                            sp.wait_ge(used, i * 2 + (hf * KF + j - 1))
                        sp.dma_start(ring_buf[:, s], w[:, :, bass.ds(i * 256 + j * P, P)]).then_inc(ring_full[s], 16)

            two_hidden(0)
            with sp.Fori(1, KF // 2) as i:
                two_hidden(i)
            for dh in range(2):
                for f in range(KF):
                    n = (hf * 2 + dh) * KF + f
                    if n >= 8:
                        q, g = divmod(n - 8, KF)
                        if g == KF - 1:
                            sp.wait_ge(dn_full, 4 * (q + 1))
                        else:
                            sp.wait_ge(wd_used, q * (KF - 1) + g + 1)
                    sp.dma_start(wd_ring[:, n % 8, :], wd[:, f, dh * HALF:(dh + 1) * HALF]).then_inc(wd_full[n % 8], 16)
                if hf == 1 and dh == 0:
                    for t in range(4):
                        sp.wait_ge(y_ready, t + 1)
                        sp.dma_start(out_d[t], x1[:, t, :]).then_inc(out_stored, 16)
        for t in range(4, NT):
            sp.wait_ge(y_ready, t + 1)
            sp.dma_start(out_d[t], x1[:, t, :]).then_inc(out_stored, 16)
        sp.wait_ge(out_stored, 16 * NT)

    @block.gpsimd
    def _(pool):
        pool.memset(ident[:, :], 0.0).then_inc(pool_step, 1)
        pool.wait_ge(pool_step, 1)
        pool.affine_select(out=ident[:, :], in_=ident[:, :], compare_op=ALU.not_equal, fill=1.0, base=0,
                           pattern=[[-1, P]], channel_multiplier=1).then_inc(ident_ready, 1)
        pool.memset(flip, 0.0).then_inc(pool_step, 1)
        pool.wait_ge(pool_step, 2)
        pool.affine_select(out=flip, in_=flip, compare_op=ALU.not_equal, fill=1.0, base=1 - P,
                           pattern=[[1, P]], channel_multiplier=1).then_inc(flip_ready, 1)
        pool.memset(arena[:, E0:E0 + 3 * P], 0.0).then_inc(pool_step, 1)
        pool.wait_ge(pool_step, 3)
        pool.affine_select(out=W[0], in_=W[0], compare_op=ALU.is_ge, fill=MASKED, base=0,
                           pattern=[[-1, P]], channel_multiplier=1).then_inc(masks01, 1)
        pool.affine_select(out=W[1], in_=W[1], compare_op=ALU.is_ge, fill=MASKED, base=P,
                           pattern=[[-1, 2 * P]], channel_multiplier=1).then_inc(masks01, 1)
        for n, b in enumerate(SCORED):
            pool.wait_ge(sc_added, NIH * (n + 1))
            diag = W[b][:, b * P:(b + 1) * P]
            pool.affine_select(out=diag, in_=diag, compare_op=ALU.is_ge, fill=NONCAUSAL, base=0,
                               pattern=[[-1, P]], channel_multiplier=1).then_inc(sc_masked, 1)
        for h in range(RH):
            pool.wait_ge(lb_ready, 1)
            pool.wait_ge(pj_free, G_RFQ[h] + 2)
            pool.tensor_scalar(sgT[h % 2], sgT[h % 2], one_lb[:, h:h + 1], lb[:, h:h + 1], ALU.mult, ALU.add).then_inc(f_ready, 1)
            pool.wait_ge(f_ready, h + 1)
            if h:
                pool.wait_ge(ro_full, 2 * h)
            pool.tensor_scalar(kkT, sgT[h % 2], -1.0, 1.0, ALU.mult, ALU.add).then_inc(kk_ready, 1)
            pool.wait_ge(cum_ready, h + 1)
            a3 = cumT.rearrange("p (c t) -> p c t", t=P)
            for u in range(1, UNITS):
                n = h * UNITS + u
                if n >= 2:
                    pool.wait_ge(z_ready, n - 1)
                e = expT[n % 2]
                if u == 1:
                    pool.tensor_tensor(e.rearrange("p (c t) -> p c t", t=P), a3[:, :, P - 1:P].broadcast_to([P, NT, P]), a3,
                                       ALU.subtract).then_inc(diff_ready, 1)
                    continue
                m = P >> (u - 1)
                a4 = cumT.rearrange("p (b two m) -> p b two m", two=2, m=m)
                e4 = e.rearrange("p (b two m) -> p b two m", two=2, m=m)
                nb = SEQ // (2 * m)
                ref = a4[:, :, 0, m - 1:m].broadcast_to([P, nb, m])
                pool.tensor_tensor(e4[:, :, 0, :], ref, a4[:, :, 0, :], ALU.subtract)
                pool.tensor_tensor(e4[:, :, 1, :], a4[:, :, 1, :], ref, ALU.subtract).then_inc(diff_ready, 1)
        pool.wait_ge(bias_ready, 4)
        pool.wait_ge(masks01, 2)
        pool.wait_ge(topk_done, len(SCORED))
        pool.wait_ge(on_ready, 2)
        for i, (b, h) in enumerate(ITEMS):
            if i >= 2:
                pool.wait_ge(s_read, i - 1)
            n = min(256, P * (b + 1))
            pool.tensor_tensor(near[i % 2][:, 0:n], bias8[:, h, 256 - n:256], W[b][:, P * (b + 1) - n:P * (b + 1)],
                               ALU.add).then_inc(near_ready, 1)

    @block.scalar
    def _(act):
        steps = [0]

        def link(ins):
            steps[0] += 1
            ins.then_inc(act_step, 1)
            act.wait_ge(act_step, steps[0])

        def evac(g, out, in_, f=ACT.Copy, **kw):
            act.wait_ge(pj_full, g + 1)
            act.activation(out, in_, f, **kw).then_inc(pj_free, 1)

        act.wait_ge(vcol_ready, 1)
        act.activation(c_act[:, :], vcol[:, V_C:V_C + KD], ACT.Silu).then_inc(cact_ready, 1)
        for t in range(NT):
            act.wait_ge(x_loaded[t], 16)
            if t:
                act.wait_ge(xsq_done, t)
            act.activation(sq_junk, x_tok[:, t, :], ACT.Square, accum_out=ss[:, t:t + 1]).then_inc(xsq_done, 1)
        act.wait_ge(ssum1, 1)
        act.activation(rstd[:, 0:8], ss[:, 8:16], ACT.Sqrt).then_inc(std1_done, 1)
        act.wait_ge(lb_ready, 1)
        act.activation(lb_e[:, :], lb_e[:, :], ACT.Exp).then_inc(lbe_ready, 1)
        act.wait_ge(brow_full, 1)
        act.activation(brow[:, :], bank[6][0:NH, 0:384], ACT.Copy).then_inc(brow_ready, 1)
        act.wait_ge(ada_done, 16)
        act.activation(mod[:, 0:16], bank[0][:, 0:16], ACT.Copy).then_inc(mod_copied, 1)
        for t in range(NT):
            g = G_A + t
            act.wait_ge(pj_full, g + 1)
            ps = bank[g % 2]
            act.activation(sq_junk[:, 256 * (t % 4):256 * (t % 4) + LORA], ps[:, 0:LORA], ACT.Square, accum_out=ss[:, 16 + t:17 + t]).then_inc(cqsq_done, 1)
            if t >= 3:
                act.wait_ge(cqsq_done, t - 2)
            act.activation(cq_tok[:, t, :], ps[:, 0:LORA], ACT.Copy)
            act.activation(v_tok[:, t, :], ps[:, 256:384], ACT.Copy)
            act.activation(wi[:, t, :], ps[:, 384:392], ACT.Copy, scale=(NIH ** -0.5) * (HD ** -0.5)).then_inc(pj_free, 1)
        act.wait_ge(ssum2, 1)
        act.activation(rstd[:, 16:24], ss[:, 24:32], ACT.Sqrt).then_inc(std2_done, 1)
        for m, dst in enumerate((kT[0], kT[1], kiT)):
            for hf in range(2):
                g = G_B + 2 * m + hf
                evac(g, dst[:, hf * HALF:(hf + 1) * HALF], bank[g % 2])
        for m in range(4):
            for hf in range(2):
                g = G_UQI + 2 * m + hf
                evac(g, qiT[:, m, hf * HALF:(hf + 1) * HALF], bank[g % 2])
        i = 0
        for b in SCORED:
            n = P * (b + 1)
            for h in range(NIH):
                act.wait_ge(sc_full, i + 1)
                if i >= 2:
                    act.wait_ge(sc_added, i - 1)
                act.activation(relu_buf[i % 2][:, 0:n], pp[1 + i % 2][:, 0:n], ACT.Relu).then_inc(sc_relu, 1)
                i += 1
        for m in range(4):
            for hf in range(2):
                g = G_UQ + 2 * m + hf
                evac(g, qT[:, m, hf * HALF:(hf + 1) * HALF], bank[g % 2])
        for j in range(4):
            act.wait_ge(bias_full, j + 1)
            act.activation(bias8[:, 2 * j:2 * j + 2, :], bank[6 + j % 2].rearrange("p (h j) -> p h j", h=2), ACT.Copy).then_inc(bias_ready, 1)

        def rfq(h):
            for k, (dst, f) in enumerate(((sgT[h % 2], ACT.Sigmoid), (rqT[h % 2], ACT.Silu))):
                for hf in range(2):
                    g = G_RFQ[h] + 2 * k + hf
                    evac(g, dst[:, hf * HALF:(hf + 1) * HALF], bank[g % 2], f)

        def tokmajor(g0, dst, f):
            for j in range(2):
                for t in range(NT):
                    g = g0 + j * NT + t
                    evac(g, dst[:, t, j * 256:(j + 1) * 256], bank[g % 2][:, 0:256], f)

        def logf(h):
            act.wait_ge(f_ready, h + 1)
            act.wait_ge(kk_ready, h + 1)
            act.activation(sgT[h % 2], sgT[h % 2], ACT.Ln).then_inc(g_ready, 1)

        def rec(h):
            act.wait_ge(cum_ready, h + 1)
            a3 = cumT.rearrange("p (c t) -> p c t", t=P)
            act.activation(decay[:, :].unsqueeze(2), a3[:, :, P - 1:P], ACT.Exp).then_inc(act_step, 1)
            steps[0] += 1
            for u in range(UNITS):
                n = h * UNITS + u
                if u == 0:
                    if n >= 2:
                        act.wait_ge(z_ready, n - 1)
                    act.activation(expT[n % 2], cumT, ACT.Exp).then_inc(exp_ready, 1)
                else:
                    act.wait_ge(diff_ready, h * (UNITS - 1) + u)
                    act.activation(expT[n % 2], expT[n % 2], ACT.Exp).then_inc(exp_ready, 1)
                if u == 2:
                    for k in range(2):
                        act.wait_ge(kl_full, 2 * h + k + 1)
                        act.activation(kl_tok[:, 4 * k:4 * k + 4, :], bank[2 + k].rearrange("p (c t) -> p c t", t=P),
                                       ACT.Copy).then_inc(kl_free, 1)
            for k in range(2):
                act.wait_ge(ro_full, 2 * h + k + 1)
                act.activation(ri_tok[:, 4 * k:4 * k + 4, h * P:(h + 1) * P], bank[2 + k].rearrange("p (c t) -> p c t", t=P),
                               ACT.Copy).then_inc(ro_free, 1)

        gT = gates_d.rearrange("(m p) t -> m p t", p=P)

        def gates(q):
            for j in range(8):
                g = G_GATE[q] + j
                if q or j >= 2:
                    act.wait_ge(gate_stored[j % 2], 16 * ((8 * q + j) // 2))
                evac(g, gate_out[j % 2], bank[g % 2], ACT.Sigmoid)
                act.wait_ge(pj_free, g + 1)
                act.dma_start(gT[4 * q + j // 2, :, (j % 2) * HALF:(j % 2 + 1) * HALF], gate_out[j % 2]).then_inc(gate_stored[j % 2], 16)

        rfq(0)
        logf(0)
        tokmajor(G_RI, ri_tok, ACT.Copy)
        rfq(1)
        tokmajor(G_RG, rg_tok, ACT.Silu)
        rec(0)
        logf(1)
        rfq(2)
        gates(0)
        rec(1)
        logf(2)
        rfq(3)
        gates(1)
        rec(2)
        logf(3)
        gates(2)
        gates(3)
        rec(3)
        act.wait_ge(ro_free, 2 * RH)
        act.activation(o_sq, ri_tok.rearrange("p t c -> p (t c)"), ACT.Square).then_inc(osq_ready, 1)
        act.wait_ge(ada_done, 32)
        act.activation(mod[:, 16:32], bank[6][:, 0:16], ACT.Copy).then_inc(mod_copied, 1)
        act.wait_ge(ssum3, 1)
        act.activation(rstd[:, 32:64], ss[:, 32:64], ACT.Sqrt).then_inc(std3_done, 1)
        for n in range(8):
            h, k = divmod(n, 2)
            act.wait_ge(rt_full, n + 1)
            act.activation(recT[:, h, k * HALF:(k + 1) * HALF], bank[2 + n % 2], ACT.Copy,
                           scale=vcol[:, V_RN:V_RN + 1]).then_inc(rt_free, 1)

        def softmax(i):
            b, h = ITEMS[i]
            n = P * (b + 1)
            act.wait_ge(s_read, i + 1)
            if i >= 2:
                act.wait_ge(pt_full, PT_GROUPS[i - 1])
            if i >= 16:
                act.wait_ge(o_read, (i - 16) // NH + 1)
            act.activation(p_buf[i % 2][:, 0:n], s_buf[i % 2][:, 0:n], ACT.Exp, bias=nmax[:, i % 16:i % 16 + 1], scale=-1.0,
                           accum_out=rsum[:, i % 16:i % 16 + 1]).then_inc(p_ready, 1)

        def unload(i):
            b, h = ITEMS[i]
            if i >= 2:
                act.wait_ge(pv_full, i - 1)
            for k in range((b + 4) // 4):
                n = min(4, b + 1 - 4 * k)
                g = PT_GROUPS[i] + k
                act.wait_ge(pt_full, g + 1)
                act.activation(pT[i % 2][:, 4 * k:4 * k + n, :], bank[6 + g % 2][:, 0:n * P].rearrange("p (c t) -> p c t", t=P),
                               ACT.Copy).then_inc(pt_free, 1)

        def attn_out(b):
            act.wait_ge(at_full, b + 1)
            act.activation(attnT[:, :, b * P:(b + 1) * P], bank[b % 2].rearrange("p (c t) -> p c t", t=P), ACT.Copy).then_inc(attnT_ready, 1)

        for i in range(len(ITEMS)):
            softmax(i)
            if i >= 1:
                unload(i - 1)
            if i >= NH and i % NH == 6:
                attn_out(i // NH - 1)
        unload(len(ITEMS) - 1)
        attn_out(NT - 1)
        for hf in range(2):
            for t in range(4 * hf, 4 * hf + 4):
                act.wait_ge(x1_ready, 2 * t + 2)
                if t:
                    act.wait_ge(sq4_done, t)
                act.activation(junk2, x1[:, t, :], ACT.Square, accum_out=ss[:, t:t + 1]).then_inc(sq4_done, 1)
            act.wait_ge(ssum4, hf + 1)
            act.activation(rstd[:, 4 * hf:4 * hf + 4], ss[:, 8 + 4 * hf:12 + 4 * hf], ACT.Sqrt).then_inc(std4_done, 1)
        for hf in range(2):
            def two_hidden(i):
                for j in range(2):
                    act.wait_ge(g_full, i * 2 + (hf * KF + j + 1))
                    if hf or not isinstance(i, int):
                        act.wait_ge(hid_ready, i * 2 + (hf * KF + j - 1))
                    act.activation(silu_buf[j], bank[2 * j], ACT.Silu).then_inc(silu_ready, 1)

            two_hidden(0)
            with act.Fori(1, KF // 2) as i:
                two_hidden(i)
            for t in range(4 * hf, 4 * hf + 4):
                act.wait_ge(x2_ready, 8 * hf + 4 + (t % 4) + 1)
                if t:
                    act.wait_ge(sq5_done, t)
                act.activation(junk2, x1[:, t, :], ACT.Square, accum_out=ss[:, 16 + t:17 + t]).then_inc(sq5_done, 1)
            act.wait_ge(ssum5, hf + 1)
            act.activation(rstd[:, 16 + 4 * hf:20 + 4 * hf], ss[:, 24 + 4 * hf:28 + 4 * hf], ACT.Sqrt).then_inc(std5_done, 1)

    @block.tensor
    def _(pe):
        def use(name):
            pe.wait_ge(ring_full[ring.slot[name]], ring.full[name])

        def product(out, pairs):
            for k, (a, b) in enumerate(pairs):
                last = pe.matmul(out, a, b, start=(k == 0), stop=(k == len(pairs) - 1))
            return last

        def turn4(dst, tiles):
            for c, a in enumerate(tiles):
                last = pe.transpose(dst[:, c * P:(c + 1) * P], a, ident[:, :])
            return last

        pe.wait_ge(ident_ready, 1)
        pe.wait_ge(vec_loaded, 16 * 7)
        pe.transpose(bank[7][:, 0:V_END], vrows[0:V_END, :], ident[0:V_END, 0:V_END]).then_inc(vt_full, 1)
        pe.wait_ge(rb_loaded, 32)
        pe.matmul(bank[6][0:NH, 0:384], rb_sb[:, :], bk_sb, start=True, stop=True).then_inc(brow_full, 1)
        pe.wait_ge(cact_ready, 1)

        def ada_col(j, out):
            use(("ada", j))
            w = ring_buf[:, ring.slot[("ada", j)]]
            product(out, [(w[:, k, :], c_act[:, k:k + 1]) for k in range(KD)]).then_inc(ada_done, 1)

        for j in range(16):
            ada_col(j, bank[0][:, j:j + 1])

        for g in range(16):
            hf, k = divmod(g, KD)
            pe.wait_ge(xn_ready, 4 * hf + 4)
            if g >= 4:
                pe.wait_ge(tr_free, g - 3)
            turn4(bank[2 + g % 4], [x_tok[:, 4 * hf + t, k * P:(k + 1) * P] for t in range(4)]).then_inc(tr_full, 1)

        for n in ("cq0", "cq1", "v", "wi"):
            use(n)
        pe.wait_ge(mod_copied, 1)
        for t in range(NT):
            g = G_A + t
            if t in (0, 4):
                pe.wait_ge(tr_free, 8 + 2 * t)
            if g >= 2:
                pe.wait_ge(pj_free, g - 1)
            product(bank[g % 2][:, 0:392], [(hT[:, k, t * P:(t + 1) * P], ring_flat[:, k, 0:392]) for k in range(KD)]).then_inc(pj_full, 1)

        def featmajor(g0, w, rhs, kn):
            for hf in range(2):
                g = g0 + hf
                pe.wait_ge(pj_free, g - 1)
                product(bank[g % 2], [(w(k), rhs[:, k, hf * HALF:(hf + 1) * HALF]) for k in range(kn)]).then_inc(pj_full, 1)

        def one_tile(name, g0):
            use(name)
            featmajor(g0, lambda k: ring_buf[:, ring.slot[name], k, :], hT, KD)

        for m, name in enumerate(("k0", "k1", "ki")):
            one_tile(name, G_B + 2 * m)
        pe.wait_ge(cqn_ready, 1)
        for n in range(4):
            g = TR_CQ + n
            kk, hf = divmod(n, 2)
            pe.wait_ge(tr_free, g - 3)
            turn4(bank[2 + g % 4], [cq_tok[:, 4 * hf + t, kk * P:(kk + 1) * P] for t in range(4)]).then_inc(tr_full, 1)
        use("uqi")
        pe.wait_ge(tr_free, 20)
        for m in range(4):
            featmajor(G_UQI + 2 * m, lambda k: ring_uq[3][:, k, m * P:(m + 1) * P], cqT, 2)
        pe.wait_ge(pj_free, G_UQI + 8)
        for i, (b, h) in enumerate([(b, h) for b in SCORED for h in range(NIH)]):
            n, lo = P * (b + 1), HD * (h % 2)
            if i >= 2:
                pe.wait_ge(sc_relu, i - 1)
            for c0 in range(0, n, HALF):
                c1 = min(n, c0 + HALF)
                last = pe.matmul(pp[1 + i % 2][:, c0:c1], qiT[lo:lo + HD, h // 2, b * P:(b + 1) * P], kiT[lo:lo + HD, c0:c1], start=True, stop=True)
            last.then_inc(sc_full, 1)
        use("uq")
        for m in range(4):
            featmajor(G_UQ + 2 * m, lambda k: ring_uq[0][:, k, m * P:(m + 1) * P], cqT, 2)
        pe.wait_ge(flip_ready, 1)
        pe.wait_ge(bias_loaded, 16)
        for j in range(4):
            if j >= 2:
                pe.wait_ge(bias_ready, j - 1)
            pe.matmul(bank[6 + j % 2], flip, bias_rev[:, 2 * j:2 * j + 2, :], start=True, stop=True).then_inc(bias_full, 1)

        def rfq(h):
            one_tile(("rf", h), G_RFQ[h])
            one_tile(("rq", h), G_RFQ[h] + 2)

        def tokmajor(name, g0):
            for j in range(2):
                w = ring_pair[ring.slot[((name, j), 0)] // 2]
                use(((name, j), 0))
                use(((name, j), 1))
                for t in range(NT):
                    g = g0 + j * NT + t
                    pe.wait_ge(pj_free, g - 1)
                    product(bank[g % 2][:, 0:256], [(hT[:, k, t * P:(t + 1) * P], w[:, k, :]) for k in range(KD)]).then_inc(pj_full, 1)

        def rec(h):
            q, nz = rqT[h % 2], 8 * h
            if h:
                pe.wait_ge(ro_free, 2 * h)
            else:
                pe.wait_ge(sc_relu, len(SCORED) * NIH)
                pe.wait_ge(bias_ready, 4)
            pe.wait_ge(z_ready, h * UNITS + 2)
            for k in range(2):
                turn4(bank[2 + k], [zT[nz % 2][:, c * P:(c + 1) * P] for c in range(4 * k, 4 * k + 4)]).then_inc(kl_full, 1)

            def level(u):
                a, r = (kkT, q) if u == 0 else (zT[(nz + u) % 2],) * 2
                for k in range(2):
                    g = 16 * h + 2 * u + k
                    if g >= 2:
                        pe.wait_ge(lv_free, g - 1)
                    for c in range(4 * k, 4 * k + 4):
                        last = pe.matmul(bank[6 + k][:, (c % 4) * P:(c % 4 + 1) * P], a[:, c * P:(c + 1) * P], r[:, c * P:(c + 1) * P], start=True, stop=True)
                    last.then_inc(lv_full, 1)

            level(0)
            pe.wait_ge(kl_free, 2 * h + 2)
            for k in range(2):
                for c in range(4 * k, min(4 * k + 4, NT - 1)):
                    last = pe.matmul(bank[4 + k][:, (c % 4) * P:(c % 4 + 1) * P], kl_tok[:, c, :], ri_tok[:, c, h * P:(h + 1) * P], start=True, stop=True)
                last.then_inc(u_full, 1)
            for u in range(1, 8):
                pe.wait_ge(z_ready, h * UNITS + u + 2)
                level(u)
            pe.wait_ge(lv_free, 16 * h + 16)
            pe.wait_ge(state_ready, h + 1)
            for k in range(2):
                for c in range(4 * k, 4 * k + 4):
                    pairs = [(pT_rec[:, c, :], ri_tok[:, c, h * P:(h + 1) * P])]
                    if c:
                        pairs.append((qaT[:, c * P:(c + 1) * P], states[:, c, :]))
                    last = product(bank[2 + k][:, (c % 4) * P:(c % 4 + 1) * P], pairs)
                last.then_inc(ro_full, 1)

        def gates(q):
            for j in range(4):
                one_tile(("gate", q, j), G_GATE[q] + 2 * j)

        rfq(0)
        tokmajor("ri", G_RI)
        rfq(1)
        tokmajor("rg", G_RG)
        rec(0)
        rfq(2)
        gates(0)
        rec(1)
        rfq(3)
        gates(1)
        rec(2)
        gates(2)
        gates(3)
        rec(3)
        pe.wait_ge(cwide_ready, 1)
        for j in range(8):
            w = ring_pair[ring.slot[(("g", j), 0)] // 2]
            use((("g", j), 0))
            use((("g", j), 1))
            if j >= 2:
                pe.wait_ge(grow_ready, j - 1)
            product(bank[4 + j % 2][:, 0:256], [(c_wide[:, k, :], w[:, k, :]) for k in range(KD)]).then_inc(gr_full, 1)
        pe.wait_ge(lv_free, 16 * RH)
        for j in range(16):
            ada_col(16 + j, bank[6][:, j:j + 1])
        pe.wait_ge(ro_free, 2 * RH)
        pe.wait_ge(on_ready, 2)
        for n in range(2 * RH):
            h, k = divmod(n, 2)
            if n >= 2:
                pe.wait_ge(rt_free, n - 1)
            turn4(bank[2 + n % 2], [ri_tok[:, 4 * k + c, h * P:(h + 1) * P] for c in range(4)]).then_inc(rt_full, 1)
        pe.wait_ge(rt_free, 2 * RH)
        pe.wait_ge(grow_ready, 8)
        pe.wait_ge(pj_free, G_END)
        pe.wait_ge(mod_copied, 2)

        def scores(i):
            b, h = ITEMS[i]
            n, lo, kt = P * (b + 1), HD * (h % 2), kT[h // 4]
            if i >= 2:
                pe.wait_ge(s_read, i - 1)
            for c0 in range(0, n, HALF):
                c1 = min(n, c0 + HALF)
                last = pe.matmul(pp[1 + i % 2][:, c0:c1], qT[lo:lo + HD, h // 2, b * P:(b + 1) * P], kt[lo:lo + HD, c0:c1], start=True, stop=True)
            last.then_inc(s_full, 1)

        def turn(i):
            b, h = ITEMS[i]
            pe.wait_ge(p_ready, i + 1)
            for k in range((b + 4) // 4):
                g = PT_GROUPS[i] + k
                if g >= 2:
                    pe.wait_ge(pt_free, g - 1)
                turn4(bank[6 + g % 2], [p_buf[i % 2][:, c * P:(c + 1) * P] for c in range(4 * k, min(4 * k + 4, b + 1))]).then_inc(pt_full, 1)

        def weigh(i):
            b, h = ITEMS[i]
            pe.wait_ge(pt_free, PT_GROUPS[i + 1])
            if h == 0 and b >= 2:
                pe.wait_ge(attnT_ready, b - 1)
            product(bank[b % 2][:, h * HD:(h + 1) * HD],
                    [(pT[i % 2][:, c, :], v_tok[:, c, (h // 4) * HD:(h // 4 + 1) * HD]) for c in range(b + 1)]).then_inc(pv_full, 1)

        def attn_out(b):
            pe.wait_ge(o_read, b + 1)
            turn4(bank[b % 2], [attn_tok[:, m * P:(m + 1) * P] for m in range(4)]).then_inc(at_full, 1)

        for i in range(len(ITEMS) + 2):
            if i < len(ITEMS):
                scores(i)
            if 1 <= i <= len(ITEMS):
                turn(i - 1)
            if i >= 2:
                weigh(i - 2)
                if ITEMS[i - 2][1] == 3 and i - 2 >= NH:
                    attn_out(ITEMS[i - 2][0] - 1)
        attn_out(NT - 1)
        pe.wait_ge(attnT_ready, NT)
        pe.wait_ge(wbr_loaded, 32)
        for n in range(16):
            m, hf = divmod(n, 2)
            if n >= 2:
                pe.wait_ge(mix_ready, n - 1)
            for r, src in enumerate((attnT, recT)):
                product(bank[2 + 2 * (n % 2) + r],
                        [(w_br[r][:, k, m * P:(m + 1) * P], src[:, k, hf * HALF:(hf + 1) * HALF]) for k in range(4)]).then_inc(y_full, 1)
        pe.wait_ge(mix_ready, 16)
        for n in range(16):
            t, dh = divmod(n, 2)
            pe.wait_ge(wo_loaded[dh], 16)
            if n >= 4:
                pe.wait_ge(x1_ready, n - 3)
            product(bank[(6 + n % 4) % 8], [(mixT[:, k, t * P:(t + 1) * P], w_o[:, k, dh * HALF:(dh + 1) * HALF]) for k in range(KD)]).then_inc(wo_full, 1)
        for g in range(16):
            hf, k = divmod(g, KD)
            pe.wait_ge(xn2_ready, 4 * hf + 4)
            if g >= 4:
                pe.wait_ge(t2_free, g - 3)
            turn4(bank[2 + g % 4], [xn2[:, t, k * P:(k + 1) * P] for t in range(4)]).then_inc(t2_full, 1)
        pe.wait_ge(t2_free, 16)
        pe.wait_ge(x1_ready, 16)
        for hf in range(2):
            def two_hidden(i):
                for j in range(2):
                    if hf or not isinstance(i, int):
                        pe.wait_ge(hid_ready, i * 2 + (hf * KF + j - 1))
                    for m, full in enumerate((g_full, up_full)):
                        s = (2 + 2 * j + m) % 4
                        pe.wait_ge(ring_full[s], i * 16 + 16 * (ff_fills[s] + hf * (KF // 2) + 1))
                        product(bank[2 * j + m], [(ring_buf[:, s, k, :], h2T[hf][:, k, :]) for k in range(KD)]).then_inc(full, 1)

            two_hidden(0)
            with pe.Fori(1, KF // 2) as i:
                two_hidden(i)
            pe.wait_ge(hid_ready, (hf + 1) * KF)
            for dh in range(2):
                for f in range(KF):
                    n = (hf * 2 + dh) * KF + f
                    pe.wait_ge(wd_full[n % 8], 16 * (n // 8 + 1))
                    for t in range(4):
                        if f == 0 and (hf or dh):
                            pe.wait_ge(x2_ready, 8 * hf + 4 * dh - 4 + t + 1)
                        last = pe.matmul(bank[4 + t], hidT[:, f, t * P:(t + 1) * P], wd_ring[:, n % 8, :], start=(f == 0), stop=(f == KF - 1))
                        if f == KF - 1:
                            last.then_inc(dn_full, 1)
                    if f < KF - 1:
                        last.then_inc(wd_used, 1)

    @block.vector
    def _(dve):
        steps = [0]

        def link(ins):
            steps[0] += 1
            ins.then_inc(dve_step, 1)
            dve.wait_ge(dve_step, steps[0])

        link(dve.memset(scan_gate[:, :], 1.0))
        link(dve.memset(scan_gate[:, 0:SEQ:P], 0.0))
        link(dve.memset(pT_rec, 0.0))
        dve.wait_ge(vt_full, 1)
        dve.tensor_copy(vcol[:, :], bank[7][:, 0:V_END]).then_inc(vcol_ready, 1)
        dve.wait_ge(cact_ready, 1)
        dve.tensor_copy(c_wide[:, :, :], c_act[:, :].unsqueeze(2).broadcast_to([P, KD, P])).then_inc(cwide_ready, 1)
        dve.wait_ge(mask_loaded, 16)
        link(dve.tensor_copy(lvl_mask[:, :, :], mask_wide.bitcast(I32)))
        dve.wait_ge(xsq_done, NT)
        dve.tensor_scalar(ss[:, 8:16], ss[:, 0:8], 1.0 / D, EPS, ALU.mult, ALU.add).then_inc(ssum1, 1)
        dve.wait_ge(vcol_ready, 1)
        lb0, lb1 = vcol[:, V_LB:V_LB + RH], vcol[:, V_LB + RH:V_LB + 2 * RH]
        link(dve.tensor_tensor(lb[:, :], lb0, lb1, ALU.max))
        dve.tensor_tensor(lb_e[:, 0:RH], lb0, lb[:, :], ALU.subtract)
        dve.tensor_tensor(lb_e[:, RH:2 * RH], lb1, lb[:, :], ALU.subtract).then_inc(lb_ready, 1)
        dve.wait_ge(std1_done, 1)
        link(dve.reciprocal(rstd[:, 8:16], rstd[:, 0:8]))
        for t in range(NT):
            dve.tensor_scalar(x_tok[:, t, :], x_tok[:, t, :], rstd[:, 8 + t:9 + t], None, ALU.mult).then_inc(xn_ready, 1)
        dve.wait_ge(lbe_ready, 1)
        link(dve.tensor_tensor(one_lb[:, :], lb_e[:, 0:RH], lb_e[:, RH:2 * RH], ALU.add))
        link(dve.reciprocal(one_lb[:, :], one_lb[:, :]))
        link(dve.tensor_tensor(lb[:, :], lb_e[:, 0:RH], one_lb[:, :], ALU.mult))
        dve.tensor_scalar(one_lb[:, :], lb[:, :], -1.0, 1.0, ALU.mult, ALU.add).then_inc(lb_ready, 1)
        dve.wait_ge(mod_copied, 1)
        link(dve.tensor_tensor(mod[:, 0:16], mod[:, 0:16], vcol[:, V_BADA:V_BADA + 16], ALU.add))
        link(dve.tensor_scalar(gain1[:, :], mod[:, 8:16], 1.0, None, ALU.add))
        link(dve.tensor_tensor(gain1[:, :], gain1[:, :], vcol[:, V_N1:V_N1 + KD], ALU.mult))
        for g in range(16):
            hf, k = divmod(g, KD)
            dve.wait_ge(tr_full, g + 1)
            dve.tensor_scalar(hT[:, k, hf * HALF:(hf + 1) * HALF], bank[2 + g % 4], gain1[:, k:k + 1], mod[:, k:k + 1],
                              ALU.mult, ALU.add).then_inc(tr_free, 1)
        dve.wait_ge(pj_free, G_A + NT)
        dve.tensor_scalar(ss[:, 24:32], ss[:, 16:24], 1.0 / LORA, EPS, ALU.mult, ALU.add).then_inc(ssum2, 1)
        dve.wait_ge(std2_done, 1)
        link(dve.reciprocal(rstd[:, 24:32], rstd[:, 16:24]))
        dve.tensor_tensor(cq_tok, cq_tok, rstd[:, 24:32].unsqueeze(2).broadcast_to([P, NT, LORA]), ALU.mult).then_inc(cqn_ready, 1)
        for n in range(4):
            g = TR_CQ + n
            kk, hf = divmod(n, 2)
            dve.wait_ge(tr_full, g + 1)
            dve.tensor_scalar(cqT[:, kk, hf * HALF:(hf + 1) * HALF], bank[2 + g % 4], vcol[:, V_QN + kk:V_QN + kk + 1], None,
                              ALU.mult).then_inc(tr_free, 1)
        i = 0
        for b in SCORED:
            n = P * (b + 1)
            for h in range(NIH):
                dve.wait_ge(sc_relu, i + 1)
                if h == 0:
                    ins = dve.tensor_scalar(W[b], relu_buf[i % 2][:, 0:n], wi[:, b, h:h + 1], None, ALU.mult)
                else:
                    dve.wait_ge(sc_added, i)
                    ins = dve.scalar_tensor_tensor(W[b], relu_buf[i % 2][:, 0:n], wi[:, b, h:h + 1], W[b], ALU.mult, ALU.add)
                ins.then_inc(sc_added, 1)
                i += 1

        def topk(b):
            dve.wait_ge(sc_masked, b - SCORED[0] + 1)
            for r in range(TOPK // 8):
                link(dve.max(top8[:, :], W[b]))
                link(dve.match_replace(out=W[b], in_to_replace=top8[:, :], in_values=W[b], imm_value=PICKED))
            dve.tensor_scalar(W[b], W[b], (PICKED + NONCAUSAL) / 2, MASKED, ALU.is_gt, ALU.mult).then_inc(topk_done, 1)

        def cumulate(h):
            dve.wait_ge(g_ready, h + 1)
            if h:
                dve.wait_ge(ro_full, 2 * h)
            dve.tensor_tensor_scan(cumT, scan_gate[:, :], sgT[h % 2], 0.0, ALU.mult, ALU.add).then_inc(cum_ready, 1)

        def rec(h):
            q, nz = rqT[h % 2], 8 * h

            def weigh(u):
                n = h * UNITS + u
                dve.wait_ge(exp_ready, n + 1)
                e = expT[n % 2]
                if u == 0:
                    if h:
                        dve.wait_ge(ro_full, 2 * h)
                    else:
                        dve.wait_ge(pj_free, G_RFQ[h] + 4)
                    dve.tensor_tensor(qaT, q, e, ALU.mult).then_inc(z_ready, 1)
                    return
                z = zT[(nz + u - 1) % 2]
                if u == 1:
                    dve.wait_ge(kk_ready, h + 1)
                    if h:
                        dve.wait_ge(lv_full, 16 * h)
                    dve.tensor_tensor(z, kkT, e, ALU.mult).then_inc(z_ready, 1)
                    return
                if u == 3:
                    dve.wait_ge(kl_full, 2 * h + 2)
                elif u > 3:
                    dve.wait_ge(lv_full, 16 * h + 2 * (u - 2))
                m = P >> (u - 1)
                z4, e4, k4, q4 = (a.rearrange("p (b two m) -> p b two m", two=2, m=m) for a in (z, e, kkT, q))
                dve.tensor_tensor(z4[:, :, 0, :], k4[:, :, 0, :], e4[:, :, 0, :], ALU.mult)
                dve.tensor_tensor(z4[:, :, 1, :], q4[:, :, 1, :], e4[:, :, 1, :], ALU.mult).then_inc(z_ready, 1)

            def place(u):
                for k in range(2):
                    g = 16 * h + 2 * u + k
                    dve.wait_ge(lv_full, g + 1)
                    dve.copy_predicated(pT_rec[:, 4 * k:4 * k + 4, :], lvl_mask[:, u, :].unsqueeze(1).broadcast_to([P, 4, P]),
                                        bank[6 + k].rearrange("p (c t) -> p c t", t=P)).then_inc(lv_free, 1)

            for u in range(3):
                weigh(u)
            weigh(3)
            place(0)
            for c in range(NT - 1):
                if c % 4 == 0:
                    dve.wait_ge(u_full, 2 * h + c // 4 + 1)
                add = bank[4 + c // 4][:, (c % 4) * P:(c % 4 + 1) * P]
                if c == 0:
                    link(dve.tensor_copy(states[:, 1, :], add))
                else:
                    ins = dve.scalar_tensor_tensor(states[:, c + 1, :], states[:, c, :], decay[:, c:c + 1], add, ALU.mult, ALU.add)
                    if c < NT - 2:
                        link(ins)
                    else:
                        ins.then_inc(state_ready, 1)
            for u in range(4, UNITS):
                place(u - 3)
                weigh(u)
            place(6)
            place(7)

        topk(2)
        cumulate(0)
        topk(3)
        topk(4)
        rec(0)
        cumulate(1)
        topk(5)
        rec(1)
        cumulate(2)
        topk(6)
        rec(2)
        cumulate(3)
        topk(7)
        rec(3)
        dve.wait_ge(gb_loaded, 32)
        for j in range(8):
            row = (g1_row if j < 4 else g2_row)[:, 256 * (j % 4):256 * (j % 4) + 256]
            dve.wait_ge(gr_full, j + 1)
            dve.tensor_tensor(row, bank[4 + j % 2][:, 0:256], row, ALU.add).then_inc(grow_ready, 1)
        dve.wait_ge(osq_ready, 1)
        link(dve.tensor_reduce(ss[:, 32:64], o_sq.rearrange("p (n c) -> p n c", c=P), AX.X, ALU.add))
        dve.tensor_scalar(ss[:, 32:64], ss[:, 32:64], 1.0 / P, EPS, ALU.mult, ALU.add).then_inc(ssum3, 1)
        dve.wait_ge(std3_done, 1)
        link(dve.reciprocal(rstd[:, 32:64], rstd[:, 32:64]))
        o3 = at(F0, NT * RH, P)
        dve.tensor_tensor(o3, o3, rstd[:, 32:64].unsqueeze(2).broadcast_to([P, NT * RH, P]), ALU.mult).then_inc(on_ready, 1)
        dve.wait_ge(on_ready, 1)
        dve.tensor_tensor(ri_tok, ri_tok, rg_tok, ALU.mult).then_inc(on_ready, 1)
        dve.wait_ge(mod_copied, 2)
        link(dve.tensor_tensor(mod[:, 16:32], mod[:, 16:32], vcol[:, V_BADA + 24:V_BADA + 40], ALU.add))
        link(dve.tensor_scalar(gain2[:, :], mod[:, 24:32], 1.0, None, ALU.add))
        link(dve.tensor_tensor(gain2[:, :], gain2[:, :], vcol[:, V_N2:V_N2 + KD], ALU.mult))

        def read_scores(i):
            b, h = ITEMS[i]
            n = P * (b + 1)
            far = max(0, n - 256)
            dve.wait_ge(s_full, i + 1)
            dve.wait_ge(near_ready, i + 1)
            if i >= 2:
                dve.wait_ge(p_ready, i - 1)
            top = nmax[:, i % 16:i % 16 + 1]
            start = 3.0e38
            if far:
                start = far_max[:, i % 2:i % 2 + 1]
                dve.tensor_tensor_reduce(out=s_buf[i % 2][:, 0:far], in0=pp[1 + i % 2][:, 0:far], in1=W[b][:, 0:far], scale=-(HD ** -0.5),
                                         scalar=3.0e38, op0=ALU.add, op1=ALU.min, accum_out=start).then_inc(far_done, 1)
                dve.wait_ge(far_done, i - 2 * NH + 1)
            dve.tensor_tensor_reduce(out=s_buf[i % 2][:, far:n], in0=pp[1 + i % 2][:, far:n], in1=near[i % 2][:, 0:n - far], scale=-(HD ** -0.5),
                                     scalar=start, op0=ALU.add, op1=ALU.min, accum_out=top).then_inc(s_read, 1)

        def attn_norm(b):
            dve.wait_ge(pv_full, NH * (b + 1))
            if b:
                dve.wait_ge(at_full, b)
            link(dve.reciprocal(rinv[:, :], rsum[:, NH * (b % 2):NH * (b % 2) + NH]))
            dve.tensor_tensor(attn_tok.rearrange("p (h c) -> p h c", c=HD), bank[b % 2].rearrange("p (h c) -> p h c", c=HD),
                              rinv[:, :].unsqueeze(2).broadcast_to([P, NH, HD]), ALU.mult).then_inc(o_read, 1)

        for i in range(len(ITEMS)):
            read_scores(i)
            if i >= NH and i % NH == 3:
                attn_norm(i // NH - 1)
        attn_norm(NT - 1)
        for n in range(16):
            m, hf = divmod(n, 2)
            dve.wait_ge(gin_loaded[n % 2], 16 * (n // 2 + 1))
            if n >= 2:
                dve.wait_ge(mix_ready, n - 1)
            for r in range(2):
                dve.wait_ge(y_full, 2 * n + r + 1)
                ins = dve.tensor_tensor(y_tmp[n % 2][:, r, :], bank[2 + 2 * (n % 2) + r], gate_in[n % 2][:, r, :], ALU.mult)
                if r:
                    link(ins)
            dve.tensor_tensor(mixT[:, m, hf * HALF:(hf + 1) * HALF], y_tmp[n % 2][:, 0, :], y_tmp[n % 2][:, 1, :], ALU.add).then_inc(mix_ready, 1)

        def xn2_tiles(hf):
            dve.wait_ge(sq4_done, 4 * hf + 4)
            dve.tensor_scalar(ss[:, 8 + 4 * hf:12 + 4 * hf], ss[:, 4 * hf:4 * hf + 4], 1.0 / D, EPS, ALU.mult, ALU.add).then_inc(ssum4, 1)
            dve.wait_ge(std4_done, hf + 1)
            link(dve.reciprocal(rstd[:, 8 + 4 * hf:12 + 4 * hf], rstd[:, 4 * hf:4 * hf + 4]))
            for t in range(4):
                if hf and t == 0:
                    dve.wait_ge(t2_full, 8)
                dve.tensor_scalar(xn2[:, t, :], x1[:, 4 * hf + t, :], rstd[:, 8 + 4 * hf + t:9 + 4 * hf + t], None, ALU.mult).then_inc(xn2_ready, 1)

        for n in range(16):
            t, dh = divmod(n, 2)
            if n == 10:
                xn2_tiles(0)
            cols = slice(dh * HALF, (dh + 1) * HALF)
            dve.wait_ge(xr_loaded[t], 16)
            dve.wait_ge(wo_full, n + 1)
            if n:
                dve.wait_ge(x1_ready, n)
            link(dve.tensor_tensor(ff_tmp, bank[(6 + n % 4) % 8], g1_row[:, cols], ALU.mult))
            dve.tensor_tensor(x1[:, t, cols], x1[:, t, cols], ff_tmp, ALU.add).then_inc(x1_ready, 1)
        for hf in range(2):
            if hf:
                xn2_tiles(1)
            for k in range(KD):
                g = hf * KD + k
                dve.wait_ge(t2_full, g + 1)
                dve.tensor_scalar(h2T[hf][:, k, :], bank[2 + g % 4], gain2[:, k:k + 1], mod[:, 16 + k:17 + k], ALU.mult, ALU.add).then_inc(t2_free, 1)
        dve.wait_ge(fin_loaded, 16)
        for hf in range(2):
            def two_hidden(i):
                for j in range(2):
                    dve.wait_ge(silu_ready, i * 2 + (hf * KF + j + 1))
                    dve.wait_ge(up_full, i * 2 + (hf * KF + j + 1))
                    dst = at(C0, KF * HALF)[:, bass.ds(i * (2 * HALF) + j * HALF, HALF)]
                    dve.tensor_tensor(dst, bank[2 * j + 1], silu_buf[j], ALU.mult).then_inc(hid_ready, 1)

            two_hidden(0)
            with dve.Fori(1, KF // 2) as i:
                two_hidden(i)
            for dh in range(2):
                cols = slice(dh * HALF, (dh + 1) * HALF)
                for t in range(4):
                    dve.wait_ge(dn_full, 8 * hf + 4 * dh + t + 1)
                    if hf or dh or t:
                        dve.wait_ge(x2_ready, 8 * hf + 4 * dh + t)
                    link(dve.tensor_tensor(ff_tmp, bank[4 + t], g2_row[:, cols], ALU.mult))
                    dve.tensor_tensor(x1[:, 4 * hf + t, cols], x1[:, 4 * hf + t, cols], ff_tmp, ALU.add).then_inc(x2_ready, 1)
            dve.wait_ge(sq5_done, 4 * hf + 4)
            dve.tensor_scalar(ss[:, 24 + 4 * hf:28 + 4 * hf], ss[:, 16 + 4 * hf:20 + 4 * hf], 1.0 / D, EPS, ALU.mult, ALU.add).then_inc(ssum5, 1)
            dve.wait_ge(std5_done, hf + 1)
            link(dve.reciprocal(rstd[:, 24 + 4 * hf:28 + 4 * hf], rstd[:, 16 + 4 * hf:20 + 4 * hf]))
            for t in range(4 * hf, 4 * hf + 4):
                dve.scalar_tensor_tensor(x1[:, t, :], x1[:, t, :], rstd[:, 24 + t:25 + t], fin_row, ALU.mult, ALU.mult).then_inc(y_ready, 1)


def bucket_steps():
    out = np.zeros((NB, 384), np.float32)
    dist = 255 - np.arange(256)
    exact = NB // 2
    nf = np.maximum(dist, 1).astype(np.float32)
    large = exact + (np.log(nf / np.float32(exact)) / np.float32(math.log(MAXD / exact)) * np.float32(NB - exact)).astype(np.int32)
    bucket = np.where(dist < exact, dist, np.minimum(large, NB - 1))
    out[bucket, np.arange(256)] += 8.0
    out[NB - 1, 0:256] -= 8.0
    return out


def level_masks():
    s, t = np.meshgrid(np.arange(P), np.arange(P), indexing="ij")
    out = [s == t]
    m = P // 2
    while m:
        out.append((s // (2 * m) == t // (2 * m)) & (s % (2 * m) < m) & (t % (2 * m) >= m))
        m //= 2
    return np.ascontiguousarray(np.stack(out, 1).astype(np.int32).reshape(P, 8 * P))


_INS = ["x", "c", "w_ada", "b_ada", "norm1_w", "w_in", "q_norm_w", "w_uq", "w_uq_idx", "rel_bias", "lb_logits", "rec_norm_w",
        "w_branch_attn", "w_branch_rec", "w_out", "norm2_w", "w_ffn_gate", "w_ffn_up", "w_ffn_down", "final_norm_w"]


def kernel(**inputs):
    import concourse.bacc as bacc
    from concourse.bass_utils import run_bass_kernel_spmd

    nc = bacc.Bacc("TRN2", target_bir_lowering=False, num_devices=1)
    arrays = {n: np.ascontiguousarray(inputs[n]) for n in _INS}
    arrays["bucket_steps"] = bucket_steps()
    arrays["level_masks"] = level_masks()
    aps = {n: nc.dram_tensor(f"in_{n}", a.shape, mybir.dt.from_np(a.dtype), kind="ExternalInput").ap() for n, a in arrays.items()}
    aps["out"] = nc.dram_tensor("out_0", [1, SEQ, D], F32, kind="ExternalOutput").ap()
    block_kernel(nc, aps)
    r = run_bass_kernel_spmd(nc, [{f"in_{n}": a for n, a in arrays.items()}], core_ids=[0])
    return r.results[0]["out_0"]
```

```python
import math
from contextlib import ExitStack

import numpy as np

import concourse.bass as bass
from concourse import mybir

F32 = mybir.dt.float32
F32R = mybir.dt.float32r
I32 = mybir.dt.int32
U8 = mybir.dt.uint8
ALU = mybir.AluOpType
ACT = mybir.ActivationFunctionType
AX = mybir.AxisListType

P = 128
SEQ = 1024
D = 1024
KD = D // P
NT = SEQ // P
HALF = 512
NH = 8
HD = 64
LORA = 256
NIH = 8
TOPK = 256
NB = 32
MAXD = 128
RH = 4
RW = RH * P
FF = 2816
KF = FF // P
EPS = 1e-6
C_CQ, C_K, C_V, C_KI, C_WI = 0, 256, 384, 512, 576
C_RQ, C_RF, C_RI, C_RG, C_GATE = 584, 1096, 1608, 2120, 2632

NONCAUSAL = -3.0e38
PICKED = -3.4e38
MASKED = -1.0e30

V_C, V_N1, V_N2, V_QN, V_RN, V_LB, V_BADA, V_END = 0, 8, 16, 24, 26, 27, 35, 83


class Ring:

    def __init__(self, slots):
        self.order, self.src, self.dst, self.slot, self.full, self.free = [], {}, {}, {}, {}, {}
        self.fills, self.last = [0] * slots, [(None, None)] * slots

    def add(self, name, slot, src, dst, done, over=None):
        self.order.append(name)
        self.src[name], self.dst[name], self.slot[name] = src, dst, slot
        self.fills[slot] += len(dst) if isinstance(dst, list) else 1
        self.full[name] = 16 * self.fills[slot]
        free = {}
        for s in over or [slot]:
            now, before = self.last[s]
            if now != done:
                now, before = done, now
            self.last[s] = (now, before)
            if before:
                free[before[0].name] = max(before, free.get(before[0].name, before), key=lambda x: x[1])
        self.free[name] = list(free.values())


def block_kernel(nc, T):
    ctx = ExitStack()
    with ctx:
        build(nc, ctx, T)


def build(nc, ctx, T):
    def sb(name, shape, dt=F32):
        return ctx.enter_context(nc.sbuf_tensor(name, shape, dt))

    def sem(name):
        return ctx.enter_context(nc.semaphore(name))

    arena = sb("arena", [P, 47616])
    arena_base = nc.sbuf_base - 4 * 47616

    def rounded(name, off, *dims):
        return nc.alloc_sbuf_tensor_at(name, [P, *dims], F32R, offset=arena_base + 4 * off)

    def own(name, off, *dims):
        return nc.alloc_sbuf_tensor_at(name, [P, *dims], F32, offset=arena_base + 4 * off)[:]

    def at(off, *dims):
        n = 1
        for d in dims:
            n *= d
        ap = arena[:, off:off + n]
        if len(dims) == 2:
            ap = ap.rearrange("p (a b) -> p a b", a=dims[0])
        if len(dims) == 3:
            ap = ap.rearrange("p (a b c) -> p a b c", a=dims[0], b=dims[1])
        return ap

    A0, B0, C0, D0, E0, F0, G0, H0 = 0, 8192, 12288, 16384, 20480, 25088, 29184, 43520
    hT = at(A0, KD, SEQ)
    x_tok = at(B0, NT, D)
    qT = at(B0, 4, SEQ)
    qiT = at(C0, 4, SEQ)
    kT = [at(D0, SEQ), at(D0 + 1024, SEQ)]
    kiT = at(D0 + 2048, SEQ)
    v_tok = at(D0 + 3072, NT, P)
    W_OFF = [sum(P * (j + 1) for j in range(b)) for b in range(NT)]
    W = [at(E0 + W_OFF[b], P * (b + 1)) for b in range(NT)]
    cq_tok = at(G0, NT, LORA)
    cqT = at(G0 + 2048, 2, SEQ)
    relu_buf = [at(G0 + 4096 + 1024 * i, SEQ) for i in range(2)]
    sq_junk = at(G0 + 6144, D)
    ri_tok = at(F0, NT, RW)
    rg_tok = at(C0, NT, RW)
    sgT = [at(G0 + 1024 * i, SEQ) for i in range(2)]
    rqT = [at(G0 + 2048 + 1024 * i, SEQ) for i in range(2)]
    kkT = at(G0 + 4096, SEQ)
    cumT = at(G0 + 5120, SEQ)
    expT = [at(G0 + 6144 + 1024 * i, SEQ) for i in range(2)]
    zT = [at(G0 + 8192 + 1024 * i, SEQ) for i in range(2)]
    bias_rev = at(G0 + 8192, NH, 256)
    flip = at(G0 + 10240, P)
    qaT = at(G0 + 10240, SEQ)
    gb_rows = at(G0 + 11264, 2, D)
    mask_wide = at(G0 + 11264, 8, P)
    kl_tok = at(G0 + 11264, NT, P)
    pT_rec = at(G0 + 12288, NT, P)
    states = at(G0 + 13312, NT, P)
    recT = at(G0, RH, SEQ)
    o_sq = at(G0 + 4096, NT * RW)
    s_buf = [at(G0 + 4096 + 1024 * i, SEQ) for i in range(2)]
    p_buf = [at(G0 + 6144 + 1024 * i, SEQ) for i in range(2)]
    pT = [at(G0 + 8192 + 1024 * i, NT, P) for i in range(2)]
    near = [at(G0 + 10240 + 256 * i, 256) for i in range(2)]
    attn_tok = at(G0 + 10752, 512)
    attn_hi, attn_lo = rounded("attn_hi", A0, 4, SEQ), rounded("attn_lo", A0 + 4096, 4, SEQ)
    rec_hi, rec_lo = rounded("rec_hi", G0, 4, SEQ), rounded("rec_lo", F0, 4, SEQ)
    raw = own("raw", H0, 4, SEQ)
    w_hi = [rounded(f"w_hi{i}", o, SEQ) for i, o in enumerate((22528, 40960))]
    w_lo = [rounded(f"w_lo{i}", o + SEQ, SEQ) for i, o in enumerate((22528, 40960))]
    gate_out = [at(D0 + 2048 + HALF * i, HALF) for i in range(2)]
    gate_in = [own(f"gate_in{i}", G0 + 4096 + 2048 * i, 2, SEQ) for i in range(2)]
    y_tmp = own("y_tmp", G0 + 8192, 2, SEQ)
    mixT = own("mixT", B0, KD * SEQ)
    x1 = own("x1", A0, NT, D)
    mix_hi = [rounded(f"mix_hi{i}", D0 + 1024 * i, HALF) for i in range(2)]
    mix_lo = [rounded(f"mix_lo{i}", D0 + 1024 * i + HALF, HALF) for i in range(2)]
    res_tmp = [own(f"res_tmp{i}", D0 + 2048 + 1024 * i, D) for i in range(2)]
    sq_tmp = own("sq_tmp", D0 + 4096, D)
    h2_hi, h2_lo = rounded("h2_hi", 24576, KD, SEQ), rounded("h2_lo", 32768, KD, SEQ)
    xn2 = [x1[:, t, :] for t in range(4)] + [own(f"xn2_{t}", B0 + D * t, D) for t in range(4)]
    h2_tmp = [own(f"h2_tmp{i}", D0 + HALF * i, HALF) for i in range(2)]
    hidT = own("hidT", A0, KF * SEQ)
    x1b = own("x1b", 24576, NT, D)
    hid_hi = [rounded(f"hid_hi{i}", 32768 + 1024 * i, HALF) for i in range(2)]
    hid_lo = [rounded(f"hid_lo{i}", 32768 + 1024 * i + HALF, HALF) for i in range(2)]
    res2_tmp = [own(f"res2_tmp{i}", 34816 + 1024 * i, D) for i in range(2)]
    fin_row = own("fin_row", 36864, D)
    sq2_tmp = own("sq2_tmp", 37888, D)

    ring_buf = at(H0, 4, 8, P)
    ring_flat = at(H0, 8, 512)
    ring_pair = [at(H0, 8, 256), at(H0 + 2048, 8, 256)]
    ring_uq = [at(H0 + 1024 * i, 2, 512) for i in range(4)]

    ident = sb("ident", [P, P])
    vrows = sb("vrows", [P, P])
    vcol = sb("vcol", [P, V_END])
    c_act = sb("c_act", [P, KD])
    c_wide = sb("c_wide", [P, KD, P])
    mod = sb("mod", [P, 32])
    gain1 = sb("gain1", [P, KD])
    gain2 = sb("gain2", [P, KD])
    lb = sb("lb", [P, RH])
    one_lb = sb("one_lb", [P, RH])
    lb_e = sb("lb_e", [P, 2 * RH])
    ss = sb("ss", [P, 64])
    rstd = sb("rstd", [P, 64])
    wi = sb("wi", [P, NT, NIH])
    top8 = sb("top8", [P, 16])
    scan_gate = sb("scan_gate", [P, SEQ])
    decay = sb("decay", [P, NT])
    lvl_mask = sb("lvl_mask", [P, 8, P], U8)
    bias8 = sb("bias8", [P, NH, 256])
    brow = sb("brow", [NH, 384])
    rb_sb = sb("rb_sb", [NB, NH])
    bk_sb = at(G0 + 7168, 384)[0:NB, :]
    silu_buf = [bias8.rearrange("p h j -> p (h j)")[:, HALF * i:HALF * (i + 1)] for i in range(4)]
    g1_row = c_wide.rearrange("p k c -> p (k c)")
    g2_row = scan_gate[:, :]
    nmax = sb("nmax", [P, 16])
    rsum = sb("rsum", [P, 16])
    rinv = sb("rinv", [P, 8])
    far_max = sb("far_max", [P, 2])

    pp = [ctx.enter_context(nc.psum_tensor(f"pp{i}", [P, 1024], F32)) for i in range(4)]
    bank = [pp[i // 2][:, (i % 2) * 512:(i % 2) * 512 + 512] for i in range(8)]

    bias_d = nc.dram_tensor("bias_rows", [NH, 384], F32, kind="Internal").ap()
    x1_d = nc.dram_tensor("x1_rows", [SEQ, D], F32, kind="Internal").ap().rearrange("(t p) d -> t p d", p=P)
    gates_d = nc.dram_tensor("gates_t", [2 * D, SEQ], F32, kind="Internal").ap()

    x_d = T["x"][0].rearrange("(t p) d -> t p d", p=P)
    out_d = T["out"][0].rearrange("(t p) d -> t p d", p=P)

    def wtile(w, c0, n=P):
        return w[:, c0:c0 + n].rearrange("(k p) c -> p k c", p=P)

    w_in = T["w_in"][0]
    w_ada = T["w_ada"][0]

    ring_full = [sem(f"ring_full{i}") for i in range(4)]
    vec_loaded = sem("vec_loaded")
    rb_loaded = sem("rb_loaded")
    x_loaded = [sem(f"x_loaded{t}") for t in range(NT)]
    mask_loaded = sem("mask_loaded")
    brow_stored = sem("brow_stored")
    bias_loaded = sem("bias_loaded")
    flip_ready = sem("flip_ready")
    bias_full = sem("bias_full")
    bias_ready = sem("bias_ready")
    ident_ready = sem("ident_ready")
    masks01 = sem("masks01")
    vt_full = sem("vt_full")
    vcol_ready = sem("vcol_ready")
    cact_ready = sem("cact_ready")
    cwide_ready = sem("cwide_ready")
    brow_full = sem("brow_full")
    brow_ready = sem("brow_ready")
    pj_full = sem("pj_full")
    pj_free = sem("pj_free")
    tr_full = sem("tr_full")
    tr_free = sem("tr_free")
    xsq_done = sem("xsq_done")
    std1_done = sem("std1_done")
    ssum1 = sem("ssum1")
    xn_ready = sem("xn_ready")
    lbe_ready = sem("lbe_ready")
    lb_ready = sem("lb_ready")
    cqsq_done = sem("cqsq_done")
    ssum2 = sem("ssum2")
    std2_done = sem("std2_done")
    cqn_ready = sem("cqn_ready")
    sc_full = sem("sc_full")
    sc_relu = sem("sc_relu")
    sc_added = sem("sc_added")
    sc_masked = sem("sc_masked")
    topk_step = sem("topk_step")
    topk_done = sem("topk_done")
    dve_step = sem("dve_step")
    act_step = sem("act_step")
    pool_step = sem("pool_step")
    ada_done = sem("ada_done")
    mod_read = sem("mod_read")
    gb_loaded = sem("gb_loaded")
    gate_stored = [sem(f"gate_stored{i}") for i in range(2)]
    f_ready = sem("f_ready")
    kk_ready = sem("kk_ready")
    g_ready = sem("g_ready")
    cum_ready = sem("cum_ready")
    diff_ready = sem("diff_ready")
    exp_ready = sem("exp_ready")
    z_ready = sem("z_ready")
    kl_full = sem("kl_full")
    kl_free = sem("kl_free")
    u_full = sem("u_full")
    state_ready = sem("state_ready")
    lv_full = sem("lv_full")
    lv_free = sem("lv_free")
    ro_full = sem("ro_full")
    ro_free = sem("ro_free")
    osq_ready = sem("osq_ready")
    ssum3 = sem("ssum3")
    std3_done = sem("std3_done")
    on_ready = sem("on_ready")
    rt_full = sem("rt_full")
    rt_free = sem("rt_free")
    grow_ready = sem("grow_ready")
    near_ready = sem("near_ready")
    s_full = sem("s_full")
    s_read = sem("s_read")
    p_ready = sem("p_ready")
    pt_full = sem("pt_full")
    pt_free = sem("pt_free")
    pv_full = sem("pv_full")
    o_read = sem("o_read")
    at_full = sem("at_full")
    attn_hi_ready = sem("attn_hi_ready")
    attn_lo_ready = sem("attn_lo_ready")
    rt_lo = sem("rt_lo")
    raw_full = [sem(f"raw_full{i}") for i in range(4)]
    hi_ready = sem("hi_ready")
    lo_ready = sem("lo_ready")
    w_used = sem("w_used")
    st_hi = sem("st_hi")
    st_lo = sem("st_lo")
    gin_loaded = [sem(f"gin_loaded{i}") for i in range(2)]
    y_full = sem("y_full")
    y_gated = sem("y_gated")
    mix_ready = sem("mix_ready")
    xr_loaded = [sem(f"xr_loaded{t}") for t in range(NT)]
    res_full = sem("res_full")
    res_gated = sem("res_gated")
    x1_ready = sem("x1_ready")
    x1_stored = [sem(f"x1_stored{i}") for i in range(2)]
    sq4_done = sem("sq4_done")
    ssum4 = sem("ssum4")
    std4_done = sem("std4_done")
    xn2_ready = sem("xn2_ready")
    t2_full = sem("t2_full")
    t2_read = sem("t2_read")
    h2_hi_ready = sem("h2_hi_ready")
    h2_ready = sem("h2_ready")
    g_full = sem("g_full")
    up_full = sem("up_full")
    silu_ready = sem("silu_ready")
    hid_ready = sem("hid_ready")
    x1_back = [sem(f"x1_back{t}") for t in range(NT)]
    dn_full = sem("dn_full")
    dn_gated = sem("dn_gated")
    x2_ready = sem("x2_ready")
    far_done = sem("far_done")
    sq5_done = sem("sq5_done")
    ssum5 = sem("ssum5")
    std5_done = sem("std5_done")
    y_ready = sem("y_ready")
    out_stored0 = sem("out_stored0")
    out_stored = sem("out_stored")
    fin_loaded = sem("fin_loaded")

    block = ctx.enter_context(nc.Block())

    G_A = 0
    G_B = G_A + NT
    G_UQI = G_B + 6
    G_UQ = G_UQI + 8
    G_RFQ = [G_UQ + 8, 0, 0, 0]
    G_RI = G_RFQ[0] + 4
    G_RFQ[1] = G_RI + 16
    G_RG = G_RFQ[1] + 4
    G_RFQ[2] = G_RG + 16
    G_GATE = [G_RFQ[2] + 4]
    G_RFQ[3] = G_GATE[0] + 8
    G_GATE += [G_RFQ[3] + 4 + 8 * q for q in range(3)]
    G_END = G_GATE[3] + 8

    ring = Ring(4)
    ADA_COLS = [D * part + HALF * j for part in (0, 1, 3, 4, 2, 5) for j in range(2)]

    def plan_ada(a, b):
        for j in range(a, b):
            for q in range(4):
                src = w_ada[2 * q * P:2 * (q + 1) * P, ADA_COLS[j]:ADA_COLS[j] + HALF].rearrange("(k p) c -> p k c", p=P)
                ring.add(("ada", j, q), q, src, ring_uq[q], (ada_done, 4 * j + q + 1))

    plan_ada(0, 4)
    for s, (name, c0, n) in enumerate((("cq0", C_CQ, P), ("cq1", C_CQ + P, P), ("v", C_V, P), ("wi", C_WI, NIH))):
        ring.add(name, s, wtile(w_in, c0, n), ring_flat[:, :, s * P:s * P + n], (pj_full, G_A + NT), range(4))
    for s, (name, c0) in enumerate((("k0", C_K), ("k1", C_K + HD), ("ki", C_KI))):
        ring.add(name, s, wtile(w_in, c0, HD), [ring_buf[:, s, :, 0:HD], ring_buf[:, s, :, HD:P]], (pj_full, G_B + 2 * s + 2))
    ring.add("uqi", 3, T["w_uq_idx"][0].rearrange("(k p) c -> p k c", p=P), ring_uq[3], (pj_full, G_UQI + 8))
    ring.add("uq", 0, T["w_uq"][0].rearrange("(k p) c -> p k c", p=P), ring_uq[0], (pj_full, G_UQ + 8))

    def plan_rf_rq(h, s):
        ring.add(("rf", h), s, wtile(w_in, C_RF + h * P), ring_buf[:, s], (pj_full, G_RFQ[h] + 2))
        ring.add(("rq", h), s + 1, wtile(w_in, C_RQ + h * P), ring_buf[:, s + 1], (pj_full, G_RFQ[h] + 4))

    def plan_pair(name, w, c0, which, done):
        for m in range(2):
            ring.add((name, m), 2 * which + m, wtile(w, c0 + m * P), ring_pair[which][:, :, m * P:(m + 1) * P], done, (2 * which, 2 * which + 1))

    def plan_gates(q, s0):
        for j in range(4):
            s = (s0 + j) % 4
            ring.add(("gate", q, j), s, wtile(w_in, C_GATE + (4 * q + j) * P), ring_buf[:, s], (pj_full, G_GATE[q] + 2 * j + 2))

    plan_rf_rq(0, 2)
    for j in range(2):
        plan_pair(("ri", j), w_in, C_RI + 256 * j, j, (pj_full, G_RI + NT * (j + 1)))
    plan_rf_rq(1, 0)
    for j in range(2):
        plan_pair(("rg", j), w_in, C_RG + 256 * j, 1 - j, (pj_full, G_RG + NT * (j + 1)))
    plan_rf_rq(2, 2)
    plan_gates(0, 0)
    plan_rf_rq(3, 0)
    plan_gates(1, 2)
    plan_ada(4, 6)
    plan_gates(2, 0)
    plan_gates(3, 0)
    plan_ada(6, 12)
    SCORED = list(range(TOPK // P, NT))
    TR_X, TR_CQ = 0, 16
    S_WO = KD
    S_FF = S_WO + 2 * KD
    S_DN = S_FF + 2 * KF
    ST_DN = 2 * KD
    DN_LOOP = (KF - 2) // 4

    def raw_count(n):
        return 32 * (n // 4 + 1) if n < KD else 16 * (KD // 4) + 16 * (n // 4 + 1)

    def split_hi(act, n, i=0, per=0):
        act.wait_ge(raw_full[n % 4], i * (4 * per) + raw_count(n))
        if n >= 2:
            act.wait_ge(w_used, i * per + (n - 1))
        act.activation(w_hi[n % 2][:, :], raw[:, n % 4, :], ACT.Copy).then_inc(hi_ready, 1)

    def split_lo(dve, n, i=0, per=0):
        dve.wait_ge(hi_ready, i * per + (n + 1))
        dve.tensor_tensor(w_lo[n % 2][:, :], raw[:, n % 4, :], w_hi[n % 2][:, :].bitcast(F32), ALU.subtract).then_inc(lo_ready, 1)

    def split_product(out, pairs, start=True, stop=True):
        for k, (ah, al, bh, bl) in enumerate(pairs):
            nc.tensor.matmul(out, ah, bh, start=start and k == 0, stop=False)
            nc.tensor.matmul(out, ah, bl, start=False, stop=False)
            last = nc.tensor.matmul(out, al, bh, start=False, stop=stop and k == len(pairs) - 1)
        return last

    UNITS = 9
    ITEMS = [(b, h) for b in range(NT) for h in range(NH)]
    PT_GROUPS = [0]
    for b, h in ITEMS:
        PT_GROUPS.append(PT_GROUPS[-1] + (b + 4) // 4)

    @block.sync
    def _(sp):
        rows = [
            (V_C, T["c"].rearrange("o (r p) -> (o r) p", p=P), 8),
            (V_N1, T["norm1_w"].rearrange("o (r p) -> (o r) p", p=P), 8),
            (V_N2, T["norm2_w"].rearrange("o (r p) -> (o r) p", p=P), 8),
            (V_QN, T["q_norm_w"].rearrange("o (r p) -> (o r) p", p=P), 2),
            (V_RN, T["rec_norm_w"], 1),
            (V_LB, T["lb_logits"].rearrange("l (r p) -> (l r) p", p=P), 8),
            (V_BADA, T["b_ada"].rearrange("o (r p) -> (o r) p", p=P), 48),
        ]
        for r0, s, n in rows:
            sp.dma_start(vrows[r0:r0 + n, :], s).then_inc(vec_loaded, 16)
        for t in range(NT):
            sp.dma_start(x_tok[:, t, :], x_d[t]).then_inc(x_loaded[t], 16)
        sp.dma_start(mask_wide.bitcast(I32), T["level_masks"].rearrange("p (u t) -> p u t", u=8)).then_inc(mask_loaded, 16)

        def load(name):
            for signal, value in ring.free[name]:
                sp.wait_ge(signal, value)
            dst = ring.dst[name]
            for part in dst if isinstance(dst, list) else [dst]:
                sp.dma_start(part, ring.src[name]).then_inc(ring_full[ring.slot[name]], 16)

        def load_from(a, b):
            for name in ring.order[ring.order.index(a):ring.order.index(b)]:
                load(name)

        load_from(("ada", 0, 0), ("ada", 1, 0))
        sp.dma_start(rb_sb[:, :], T["rel_bias"]).then_inc(rb_loaded, 16)
        sp.dma_start(bk_sb, T["bucket_steps"]).then_inc(rb_loaded, 16)
        load_from(("ada", 1, 0), "uq")
        sp.wait_ge(brow_ready, 1)
        sp.dma_start(bias_d, brow[:, :]).then_inc(brow_stored, 16)
        sp.wait_ge(brow_stored, 16)
        sp.dma_start(bias_rev, bass.AP(bias_d.tensor, 0, [[1, P], [384, NH], [1, 256]])).then_inc(bias_loaded, 16)
        load_from("uq", ("ada", 9, 0))
        sp.wait_ge(ro_full, 2 * RH)
        for r, c0 in enumerate((2 * D, 5 * D)):
            sp.dma_start(gb_rows[:, r, :], T["b_ada"][:, c0:c0 + D].broadcast_to([P, D])).then_inc(gb_loaded, 16)
        load_from(("ada", 9, 0), ("ada", 11, 3))
        load(("ada", 11, 3))
        def raw_free(n):
            sp.wait_ge(lo_ready, n - 3)

        sp.wait_ge(ada_done, 48)
        gv = gates_d.rearrange("(g m p) t -> p m g t", g=2, p=P)
        wbr = [T[n][0].rearrange("(k p) c -> p k c", p=P) for n in ("w_branch_attn", "w_branch_rec")]
        for m in range(KD):
            if m >= 4:
                raw_free(m)
            for r in range(2):
                sp.dma_start(raw[:, m % 4, 4 * P * r:4 * P * (r + 1)].rearrange("p (k c) -> p k c", c=P),
                             wbr[r][:, :, m * P:(m + 1) * P]).then_inc(raw_full[m % 4], 16)
            if m == 3:
                sp.wait_ge(at_full, NT)
                for st in range(2):
                    sp.wait_ge(gate_stored[st], 16 * 16)
                for j in range(2):
                    sp.dma_start(gate_in[j], gv[:, j]).then_inc(gin_loaded[j], 16)
            if m >= 4:
                sp.wait_ge(y_gated, m - 3)
                sp.dma_start(gate_in[m % 2], gv[:, m - 2]).then_inc(gin_loaded[m % 2], 16)
        wo = T["w_out"][0].rearrange("(f p) c -> p f c", p=P)

        def out_tile(i):
            n = S_WO + i
            raw_free(n)
            sp.dma_start(raw[:, n % 4, :], wo[:, i % KD, :]).then_inc(raw_full[n % 4], 16)

        for i in range(4):
            out_tile(i)
            if i in (0, 1):
                sp.wait_ge(y_gated, 5 + i)
                sp.dma_start(gate_in[i], gv[:, 6 + i]).then_inc(gin_loaded[i], 16)
        sp.wait_ge(w_used, KD)
        for t in range(NT):
            sp.dma_start(x1[:, t, :], x_d[t]).then_inc(xr_loaded[t], 16)
        for i in range(4, 2 * KD):
            out_tile(i)
        wg = T["w_ffn_gate"][0].rearrange("(k p) c -> p k c", p=P)
        wu = T["w_ffn_up"][0].rearrange("(k p) c -> p k c", p=P)
        wd = T["w_ffn_down"][0].rearrange("(f p) c -> p f c", p=P)

        def ffn_tiles(i):
            for j in range(2):
                for m, w in enumerate((wg, wu)):
                    n = S_FF + 2 * j + m
                    sp.wait_ge(lo_ready, i * 4 + (n - 3))
                    sp.dma_start(raw[:, n % 4, :].rearrange("p (k c) -> p k c", c=P), w[:, :, bass.ds(i * 256 + j * P, P)]).then_inc(raw_full[n % 4], 16)

        ffn_tiles(0)
        with sp.Fori(1, KF // 2) as i:
            ffn_tiles(i)

        def down_steps(th, steps, i=0):
            for f in steps:
                n = S_DN + th * KF + f
                sp.wait_ge(lo_ready, i * 4 + (n - 3))
                sp.dma_start(raw[:, n % 4, :].unsqueeze(1), wd[:, bass.ds(i * 4 + f, 1), :]).then_inc(raw_full[n % 4], 16)

        down_steps(0, range(2))
        for hf in range(2):
            sp.wait_ge(x1_stored[hf], 16 * 4)
        sp.wait_ge(w_used, S_DN)
        for t in range(NT):
            sp.dma_start(x1b[:, t, :], x1_d[t]).then_inc(x1_back[t], 16)
        sp.dma_start(fin_row, T["final_norm_w"].rearrange("(o d) -> o d", o=1).broadcast_to([P, D])).then_inc(fin_loaded, 16)
        with sp.Fori(0, DN_LOOP) as i:
            down_steps(0, range(2, 6), i)
        down_steps(1, range(2))
        with sp.Fori(0, DN_LOOP) as i:
            down_steps(1, range(2, 6), i)
        for t in range(4, NT):
            sp.wait_ge(y_ready, t + 1)
            sp.dma_start(out_d[t], x1b[:, t, :]).then_inc(out_stored, 16)
        sp.wait_ge(out_stored, 16 * 4)

    @block.gpsimd
    def _(pool):
        pool.memset(ident[:, :], 0.0).then_inc(pool_step, 1)
        pool.wait_ge(pool_step, 1)
        pool.affine_select(out=ident[:, :], in_=ident[:, :], compare_op=ALU.not_equal, fill=1.0, base=0,
                           pattern=[[-1, P]], channel_multiplier=1).then_inc(ident_ready, 1)
        pool.memset(flip, 0.0).then_inc(pool_step, 1)
        pool.wait_ge(pool_step, 2)
        pool.affine_select(out=flip, in_=flip, compare_op=ALU.not_equal, fill=1.0, base=1 - P,
                           pattern=[[1, P]], channel_multiplier=1).then_inc(flip_ready, 1)
        pool.memset(arena[:, E0:E0 + 3 * P], 0.0).then_inc(pool_step, 1)
        pool.wait_ge(pool_step, 3)
        pool.affine_select(out=W[0], in_=W[0], compare_op=ALU.is_ge, fill=MASKED, base=0,
                           pattern=[[-1, P]], channel_multiplier=1).then_inc(masks01, 1)
        pool.affine_select(out=W[1], in_=W[1], compare_op=ALU.is_ge, fill=MASKED, base=P,
                           pattern=[[-1, 2 * P]], channel_multiplier=1).then_inc(masks01, 1)
        for n, b in enumerate(SCORED):
            pool.wait_ge(sc_added, NIH * (n + 1))
            diag = W[b][:, b * P:(b + 1) * P]
            pool.affine_select(out=diag, in_=diag, compare_op=ALU.is_ge, fill=NONCAUSAL, base=0,
                               pattern=[[-1, P]], channel_multiplier=1).then_inc(sc_masked, 1)
        for h in range(RH):
            pool.wait_ge(lb_ready, 1)
            pool.wait_ge(pj_free, G_RFQ[h] + 2)
            pool.tensor_scalar(sgT[h % 2], sgT[h % 2], one_lb[:, h:h + 1], lb[:, h:h + 1], ALU.mult, ALU.add).then_inc(f_ready, 1)
            pool.wait_ge(f_ready, h + 1)
            if h:
                pool.wait_ge(ro_full, 2 * h)
            pool.tensor_scalar(kkT, sgT[h % 2], -1.0, 1.0, ALU.mult, ALU.add).then_inc(kk_ready, 1)
            pool.wait_ge(cum_ready, h + 1)
            a3 = cumT.rearrange("p (c t) -> p c t", t=P)
            for u in range(1, UNITS):
                n = h * UNITS + u
                if n >= 2:
                    pool.wait_ge(z_ready, n - 1)
                e = expT[n % 2]
                if u == 1:
                    pool.tensor_tensor(e.rearrange("p (c t) -> p c t", t=P), a3[:, :, P - 1:P].broadcast_to([P, NT, P]), a3,
                                       ALU.subtract).then_inc(diff_ready, 1)
                    continue
                m = P >> (u - 1)
                a4 = cumT.rearrange("p (b two m) -> p b two m", two=2, m=m)
                e4 = e.rearrange("p (b two m) -> p b two m", two=2, m=m)
                nb = SEQ // (2 * m)
                ref = a4[:, :, 0, m - 1:m].broadcast_to([P, nb, m])
                pool.tensor_tensor(e4[:, :, 0, :], ref, a4[:, :, 0, :], ALU.subtract)
                pool.tensor_tensor(e4[:, :, 1, :], a4[:, :, 1, :], ref, ALU.subtract).then_inc(diff_ready, 1)
        pool.wait_ge(bias_ready, 4)
        pool.wait_ge(masks01, 2)
        pool.wait_ge(topk_done, len(SCORED))
        pool.wait_ge(on_ready, 2)
        for i, (b, h) in enumerate(ITEMS):
            if i >= 2:
                pool.wait_ge(s_read, i - 1)
            n = min(256, P * (b + 1))
            pool.tensor_tensor(near[i % 2][:, 0:n], bias8[:, h, 256 - n:256], W[b][:, P * (b + 1) - n:P * (b + 1)],
                               ALU.add).then_inc(near_ready, 1)
        for t in range(NT):
            pool.wait_ge(res_gated, t + 1)
            pool.wait_ge(xr_loaded[t], 16)
            pool.tensor_tensor(x1[:, t, :], x1[:, t, :], res_tmp[t % 2], ALU.add).then_inc(x1_ready, 1)
        for t in range(NT):
            pool.wait_ge(dn_gated, t + 1)
            pool.wait_ge(x1_back[t], 16)
            pool.tensor_tensor(x1b[:, t, :], x1b[:, t, :], res2_tmp[t % 2], ALU.add).then_inc(x2_ready, 1)
            if t == 3:
                for u in range(4):
                    pool.wait_ge(y_ready, u + 1)
                    pool.dma_start(out_d[u], x1b[:, u, :]).then_inc(out_stored0, 16)
        pool.wait_ge(out_stored0, 16 * 4)

    @block.scalar
    def _(act):
        steps = [0]

        def link(ins):
            steps[0] += 1
            ins.then_inc(act_step, 1)
            act.wait_ge(act_step, steps[0])

        def evac(g, out, in_, f=ACT.Copy, **kw):
            act.wait_ge(pj_full, g + 1)
            act.activation(out, in_, f, **kw).then_inc(pj_free, 1)

        act.wait_ge(vcol_ready, 1)
        act.activation(c_act[:, :], vcol[:, V_C:V_C + KD], ACT.Silu).then_inc(cact_ready, 1)
        for t in range(NT):
            act.wait_ge(x_loaded[t], 16)
            if t:
                act.wait_ge(xsq_done, t)
            act.activation(sq_junk, x_tok[:, t, :], ACT.Square, accum_out=ss[:, t:t + 1]).then_inc(xsq_done, 1)
        act.wait_ge(ssum1, 1)
        act.activation(rstd[:, 0:8], ss[:, 8:16], ACT.Sqrt).then_inc(std1_done, 1)
        act.wait_ge(lb_ready, 1)
        act.activation(lb_e[:, :], lb_e[:, :], ACT.Exp).then_inc(lbe_ready, 1)
        act.wait_ge(brow_full, 1)
        act.activation(brow[:, :], bank[6][0:NH, 0:384], ACT.Copy).then_inc(brow_ready, 1)
        for t in range(NT):
            g = G_A + t
            act.wait_ge(pj_full, g + 1)
            ps = bank[g % 2]
            act.activation(sq_junk[:, 256 * (t % 4):256 * (t % 4) + LORA], ps[:, 0:LORA], ACT.Square, accum_out=ss[:, 16 + t:17 + t]).then_inc(cqsq_done, 1)
            if t >= 3:
                act.wait_ge(cqsq_done, t - 2)
            act.activation(cq_tok[:, t, :], ps[:, 0:LORA], ACT.Copy)
            act.activation(v_tok[:, t, :], ps[:, 256:384], ACT.Copy)
            act.activation(wi[:, t, :], ps[:, 384:392], ACT.Copy, scale=(NIH ** -0.5) * (HD ** -0.5)).then_inc(pj_free, 1)
        act.wait_ge(ssum2, 1)
        act.activation(rstd[:, 16:24], ss[:, 24:32], ACT.Sqrt).then_inc(std2_done, 1)
        for m, dst in enumerate((kT[0], kT[1], kiT)):
            for hf in range(2):
                g = G_B + 2 * m + hf
                evac(g, dst[:, hf * HALF:(hf + 1) * HALF], bank[g % 2])
        for m in range(4):
            for hf in range(2):
                g = G_UQI + 2 * m + hf
                evac(g, qiT[:, m, hf * HALF:(hf + 1) * HALF], bank[g % 2])
        i = 0
        for b in SCORED:
            n = P * (b + 1)
            for h in range(NIH):
                act.wait_ge(sc_full, i + 1)
                if i >= 2:
                    act.wait_ge(sc_added, i - 1)
                act.activation(relu_buf[i % 2][:, 0:n], pp[1 + i % 2][:, 0:n], ACT.Relu).then_inc(sc_relu, 1)
                i += 1
        for m in range(4):
            for hf in range(2):
                g = G_UQ + 2 * m + hf
                evac(g, qT[:, m, hf * HALF:(hf + 1) * HALF], bank[g % 2])
        for j in range(4):
            act.wait_ge(bias_full, j + 1)
            act.activation(bias8[:, 2 * j:2 * j + 2, :], bank[6 + j % 2].rearrange("p (h j) -> p h j", h=2), ACT.Copy).then_inc(bias_ready, 1)

        def rfq(h):
            for k, (dst, f) in enumerate(((sgT[h % 2], ACT.Sigmoid), (rqT[h % 2], ACT.Silu))):
                for hf in range(2):
                    g = G_RFQ[h] + 2 * k + hf
                    evac(g, dst[:, hf * HALF:(hf + 1) * HALF], bank[g % 2], f)

        def tokmajor(g0, dst, f):
            for j in range(2):
                for t in range(NT):
                    g = g0 + j * NT + t
                    evac(g, dst[:, t, j * 256:(j + 1) * 256], bank[g % 2][:, 0:256], f)

        def logf(h):
            act.wait_ge(f_ready, h + 1)
            act.wait_ge(kk_ready, h + 1)
            act.activation(sgT[h % 2], sgT[h % 2], ACT.Ln).then_inc(g_ready, 1)

        def rec(h):
            act.wait_ge(cum_ready, h + 1)
            a3 = cumT.rearrange("p (c t) -> p c t", t=P)
            act.activation(decay[:, :].unsqueeze(2), a3[:, :, P - 1:P], ACT.Exp).then_inc(act_step, 1)
            steps[0] += 1
            for u in range(UNITS):
                n = h * UNITS + u
                if u == 0:
                    if n >= 2:
                        act.wait_ge(z_ready, n - 1)
                    act.activation(expT[n % 2], cumT, ACT.Exp).then_inc(exp_ready, 1)
                else:
                    act.wait_ge(diff_ready, h * (UNITS - 1) + u)
                    act.activation(expT[n % 2], expT[n % 2], ACT.Exp).then_inc(exp_ready, 1)
                if u == 2:
                    for k in range(2):
                        act.wait_ge(kl_full, 2 * h + k + 1)
                        act.activation(kl_tok[:, 4 * k:4 * k + 4, :], bank[2 + k].rearrange("p (c t) -> p c t", t=P),
                                       ACT.Copy).then_inc(kl_free, 1)
            for k in range(2):
                act.wait_ge(ro_full, 2 * h + k + 1)
                act.activation(ri_tok[:, 4 * k:4 * k + 4, h * P:(h + 1) * P], bank[2 + k].rearrange("p (c t) -> p c t", t=P),
                               ACT.Copy).then_inc(ro_free, 1)

        gT = gates_d.rearrange("(m p) t -> m p t", p=P)

        def gates(q):
            for j in range(8):
                g = G_GATE[q] + j
                if q or j >= 2:
                    act.wait_ge(gate_stored[j % 2], 16 * ((8 * q + j) // 2))
                evac(g, gate_out[j % 2], bank[g % 2], ACT.Sigmoid)
                act.wait_ge(pj_free, g + 1)
                act.dma_start(gT[4 * q + j // 2, :, (j % 2) * HALF:(j % 2 + 1) * HALF], gate_out[j % 2]).then_inc(gate_stored[j % 2], 16)

        rfq(0)
        logf(0)
        tokmajor(G_RI, ri_tok, ACT.Copy)
        rfq(1)
        tokmajor(G_RG, rg_tok, ACT.Silu)
        rec(0)
        logf(1)
        rfq(2)
        gates(0)
        rec(1)
        logf(2)
        rfq(3)
        gates(1)
        rec(2)
        logf(3)
        gates(2)
        gates(3)
        rec(3)
        act.wait_ge(ro_free, 2 * RH)
        act.activation(o_sq, ri_tok.rearrange("p t c -> p (t c)"), ACT.Square).then_inc(osq_ready, 1)
        act.wait_ge(ssum3, 1)
        act.activation(rstd[:, 32:64], ss[:, 32:64], ACT.Sqrt).then_inc(std3_done, 1)
        for n in range(8):
            h, k = divmod(n, 2)
            act.wait_ge(rt_full, n + 1)
            act.activation(rec_hi[:, h, k * HALF:(k + 1) * HALF], bank[2 + n % 2], ACT.Copy,
                           scale=vcol[:, V_RN:V_RN + 1]).then_inc(rt_free, 1)

        def softmax(i):
            b, h = ITEMS[i]
            n = P * (b + 1)
            act.wait_ge(s_read, i + 1)
            if i >= 2:
                act.wait_ge(pt_full, PT_GROUPS[i - 1])
            if i >= 16:
                act.wait_ge(o_read, (i - 16) // NH + 1)
            act.activation(p_buf[i % 2][:, 0:n], s_buf[i % 2][:, 0:n], ACT.Exp, bias=nmax[:, i % 16:i % 16 + 1], scale=-1.0,
                           accum_out=rsum[:, i % 16:i % 16 + 1]).then_inc(p_ready, 1)

        def unload(i):
            b, h = ITEMS[i]
            if i >= 2:
                act.wait_ge(pv_full, i - 1)
            for k in range((b + 4) // 4):
                n = min(4, b + 1 - 4 * k)
                g = PT_GROUPS[i] + k
                act.wait_ge(pt_full, g + 1)
                act.activation(pT[i % 2][:, 4 * k:4 * k + n, :], bank[6 + g % 2][:, 0:n * P].rearrange("p (c t) -> p c t", t=P),
                               ACT.Copy).then_inc(pt_free, 1)

        def attn_out(b):
            act.wait_ge(at_full, b + 1)
            act.activation(attn_hi[:, :, b * P:(b + 1) * P], bank[b % 2].rearrange("p (c t) -> p c t", t=P), ACT.Copy).then_inc(attn_hi_ready, 1)

        for i in range(len(ITEMS)):
            softmax(i)
            if i >= 1:
                unload(i - 1)
            if i >= NH and i % NH == 6:
                attn_out(i // NH - 1)
        unload(len(ITEMS) - 1)
        attn_out(NT - 1)
        for m in range(KD):
            split_hi(act, m)

        def stationary_hi(st, src):
            hi = mix_hi if st < ST_DN else hid_hi
            act.activation(hi[st % 2][:, :], src, ACT.Copy).then_inc(st_hi, 1)

        def square(t):
            act.wait_ge(x1_ready, t + 1)
            if t:
                act.wait_ge(sq4_done, t)
            act.activation(sq_tmp, x1[:, t, :], ACT.Square, accum_out=ss[:, t:t + 1]).then_inc(sq4_done, 1)
            act.dma_start(x1_d[t], x1[:, t, :]).then_inc(x1_stored[t // 4], 16)

        def root(hf):
            act.wait_ge(ssum4, hf + 1)
            act.activation(rstd[:, 4 * hf:4 * hf + 4], ss[:, 8 + 4 * hf:12 + 4 * hf], ACT.Sqrt).then_inc(std4_done, 1)

        for i in range(2 * KD):
            th, k = divmod(i, KD)
            if i == 13:
                for t in range(4):
                    square(t)
            if i == 14:
                root(0)
            split_hi(act, S_WO + i)
            act.wait_ge(mix_ready, k + 1)
            stationary_hi(i, mixT[:, k * SEQ + th * HALF:k * SEQ + (th + 1) * HALF])
        split_hi(act, S_FF)
        split_hi(act, S_FF + 1)
        for g in range(2 * KD):
            hf, k = divmod(g, KD)
            if g == KD:
                for t in range(4, NT):
                    square(t)
                root(1)
            act.wait_ge(t2_read, g + 1)
            act.activation(h2_hi[:, k, hf * HALF:(hf + 1) * HALF], h2_tmp[g % 2], ACT.Copy).then_inc(h2_hi_ready, 1)

        def two_hidden(i):
            for j in range(2):
                for hf in range(2):
                    if hf:
                        act.wait_ge(w_used, i * 4 + (S_FF + 2 * j + 1))
                    else:
                        act.wait_ge(g_full, i * 2 + (j + 1))
                    if not isinstance(i, int):
                        act.wait_ge(hid_ready, i * 4 + (2 * j + hf - 3))
                    act.activation(silu_buf[2 * j + hf], bank[4 * j + hf], ACT.Silu).then_inc(silu_ready, 1)
                for m in range(2):
                    split_hi(act, S_FF + 2 * j + m + 2, i, 4)

        two_hidden(0)
        with act.Fori(1, KF // 2) as i:
            two_hidden(i)

        def down_steps(th, steps, i=0):
            for f in steps:
                st = ST_DN + th * KF + f
                if th or f >= 2:
                    split_hi(act, S_DN + th * KF + f, i, 4)
                else:
                    act.wait_ge(hid_ready, 2 * KF)
                stationary_hi(st, hidT[:, bass.ds(i * (4 * SEQ) + (f * SEQ + th * HALF), HALF)])

        def final_sums(hf):
            for t in range(4 * hf, 4 * hf + 4):
                act.wait_ge(x2_ready, t + 1)
                if t:
                    act.wait_ge(sq5_done, t)
                act.activation(sq2_tmp, x1b[:, t, :], ACT.Square, accum_out=ss[:, 16 + t:17 + t]).then_inc(sq5_done, 1)
            act.wait_ge(ssum5, hf + 1)
            act.activation(rstd[:, 16 + 4 * hf:20 + 4 * hf], ss[:, 24 + 4 * hf:28 + 4 * hf], ACT.Sqrt).then_inc(std5_done, 1)

        down_steps(0, range(2))
        with act.Fori(0, DN_LOOP) as i:
            down_steps(0, range(2, 6), i)
        down_steps(1, range(2))
        with act.Fori(0, 3) as i:
            down_steps(1, range(2, 6), i)
        final_sums(0)
        with act.Fori(3, DN_LOOP) as i:
            down_steps(1, range(2, 6), i)
        final_sums(1)

    @block.tensor
    def _(pe):
        def use(name):
            pe.wait_ge(ring_full[ring.slot[name]], ring.full[name])

        def product(out, pairs):
            for k, (a, b) in enumerate(pairs):
                last = pe.matmul(out, a, b, start=(k == 0), stop=(k == len(pairs) - 1))
            return last

        def turn4(dst, tiles):
            for c, a in enumerate(tiles):
                last = pe.transpose(dst[:, c * P:(c + 1) * P], a, ident[:, :])
            return last

        pe.wait_ge(ident_ready, 1)
        pe.wait_ge(vec_loaded, 16 * 7)
        pe.transpose(bank[7][:, 0:V_END], vrows[0:V_END, :], ident[0:V_END, 0:V_END]).then_inc(vt_full, 1)
        pe.wait_ge(rb_loaded, 32)
        pe.matmul(bank[6][0:NH, 0:384], rb_sb[:, :], bk_sb, start=True, stop=True).then_inc(brow_full, 1)
        pe.wait_ge(cact_ready, 1)

        def ada_chunk(j, out):
            for q in range(4):
                use(("ada", j, q))
                for k in range(2):
                    last = pe.matmul(out, c_wide[:, 2 * q + k, :], ring_uq[q][:, k, :], start=(q + k == 0), stop=(q == 3 and k == 1))
                last.then_inc(ada_done, 1)

        pe.wait_ge(cwide_ready, 1)
        for j in range(4):
            ada_chunk(j, bank[j])

        for g in range(16):
            hf, k = divmod(g, KD)
            pe.wait_ge(xn_ready, 4 * hf + 4)
            if g == 0:
                pe.wait_ge(mod_read, 4)
            if g >= 4:
                pe.wait_ge(tr_free, g - 3)
            turn4(bank[2 + g % 4], [x_tok[:, 4 * hf + t, k * P:(k + 1) * P] for t in range(4)]).then_inc(tr_full, 1)

        for n in ("cq0", "cq1", "v", "wi"):
            use(n)
        for t in range(NT):
            g = G_A + t
            if t in (0, 4):
                pe.wait_ge(tr_free, 8 + 2 * t)
            if g >= 2:
                pe.wait_ge(pj_free, g - 1)
            product(bank[g % 2][:, 0:392], [(hT[:, k, t * P:(t + 1) * P], ring_flat[:, k, 0:392]) for k in range(KD)]).then_inc(pj_full, 1)

        def featmajor(g0, w, rhs, kn):
            for hf in range(2):
                g = g0 + hf
                pe.wait_ge(pj_free, g - 1)
                product(bank[g % 2], [(w(k), rhs[:, k, hf * HALF:(hf + 1) * HALF]) for k in range(kn)]).then_inc(pj_full, 1)

        def one_tile(name, g0):
            use(name)
            featmajor(g0, lambda k: ring_buf[:, ring.slot[name], k, :], hT, KD)

        for m, name in enumerate(("k0", "k1", "ki")):
            one_tile(name, G_B + 2 * m)
        pe.wait_ge(cqn_ready, 1)
        for n in range(4):
            g = TR_CQ + n
            kk, hf = divmod(n, 2)
            pe.wait_ge(tr_free, g - 3)
            turn4(bank[2 + g % 4], [cq_tok[:, 4 * hf + t, kk * P:(kk + 1) * P] for t in range(4)]).then_inc(tr_full, 1)
        use("uqi")
        pe.wait_ge(tr_free, 20)
        for m in range(4):
            featmajor(G_UQI + 2 * m, lambda k: ring_uq[3][:, k, m * P:(m + 1) * P], cqT, 2)
        pe.wait_ge(pj_free, G_UQI + 8)
        for i, (b, h) in enumerate([(b, h) for b in SCORED for h in range(NIH)]):
            n, lo = P * (b + 1), HD * (h % 2)
            if i >= 2:
                pe.wait_ge(sc_relu, i - 1)
            for c0 in range(0, n, HALF):
                c1 = min(n, c0 + HALF)
                last = pe.matmul(pp[1 + i % 2][:, c0:c1], qiT[lo:lo + HD, h // 2, b * P:(b + 1) * P], kiT[lo:lo + HD, c0:c1], start=True, stop=True)
            last.then_inc(sc_full, 1)
        use("uq")
        for m in range(4):
            featmajor(G_UQ + 2 * m, lambda k: ring_uq[0][:, k, m * P:(m + 1) * P], cqT, 2)
        pe.wait_ge(flip_ready, 1)
        pe.wait_ge(bias_loaded, 16)
        for j in range(4):
            if j >= 2:
                pe.wait_ge(bias_ready, j - 1)
            pe.matmul(bank[6 + j % 2], flip, bias_rev[:, 2 * j:2 * j + 2, :], start=True, stop=True).then_inc(bias_full, 1)

        def rfq(h):
            one_tile(("rf", h), G_RFQ[h])
            one_tile(("rq", h), G_RFQ[h] + 2)

        def tokmajor(name, g0):
            for j in range(2):
                w = ring_pair[ring.slot[((name, j), 0)] // 2]
                use(((name, j), 0))
                use(((name, j), 1))
                for t in range(NT):
                    g = g0 + j * NT + t
                    pe.wait_ge(pj_free, g - 1)
                    product(bank[g % 2][:, 0:256], [(hT[:, k, t * P:(t + 1) * P], w[:, k, :]) for k in range(KD)]).then_inc(pj_full, 1)

        def rec(h):
            q, nz = rqT[h % 2], 8 * h
            if h:
                pe.wait_ge(ro_free, 2 * h)
            else:
                pe.wait_ge(sc_relu, len(SCORED) * NIH)
                pe.wait_ge(bias_ready, 4)
            pe.wait_ge(z_ready, h * UNITS + 2)
            for k in range(2):
                turn4(bank[2 + k], [zT[nz % 2][:, c * P:(c + 1) * P] for c in range(4 * k, 4 * k + 4)]).then_inc(kl_full, 1)

            def level(u):
                a, r = (kkT, q) if u == 0 else (zT[(nz + u) % 2],) * 2
                for k in range(2):
                    g = 16 * h + 2 * u + k
                    if g >= 2:
                        pe.wait_ge(lv_free, g - 1)
                    for c in range(4 * k, 4 * k + 4):
                        last = pe.matmul(bank[6 + k][:, (c % 4) * P:(c % 4 + 1) * P], a[:, c * P:(c + 1) * P], r[:, c * P:(c + 1) * P], start=True, stop=True)
                    last.then_inc(lv_full, 1)

            level(0)
            pe.wait_ge(kl_free, 2 * h + 2)
            for k in range(2):
                for c in range(4 * k, min(4 * k + 4, NT - 1)):
                    last = pe.matmul(bank[4 + k][:, (c % 4) * P:(c % 4 + 1) * P], kl_tok[:, c, :], ri_tok[:, c, h * P:(h + 1) * P], start=True, stop=True)
                last.then_inc(u_full, 1)
            for u in range(1, 8):
                pe.wait_ge(z_ready, h * UNITS + u + 2)
                level(u)
            pe.wait_ge(lv_free, 16 * h + 16)
            pe.wait_ge(state_ready, h + 1)
            for k in range(2):
                for c in range(4 * k, 4 * k + 4):
                    pairs = [(pT_rec[:, c, :], ri_tok[:, c, h * P:(h + 1) * P])]
                    if c:
                        pairs.append((qaT[:, c * P:(c + 1) * P], states[:, c, :]))
                    last = product(bank[2 + k][:, (c % 4) * P:(c % 4 + 1) * P], pairs)
                last.then_inc(ro_full, 1)

        def gates(q):
            for j in range(4):
                one_tile(("gate", q, j), G_GATE[q] + 2 * j)

        rfq(0)
        tokmajor("ri", G_RI)
        rfq(1)
        tokmajor("rg", G_RG)
        rec(0)
        rfq(2)
        gates(0)
        rec(1)
        rfq(3)
        gates(1)
        pe.wait_ge(pj_free, G_GATE[1] + 8)
        ada_chunk(4, bank[0])
        ada_chunk(5, bank[1])
        rec(2)
        pe.wait_ge(mod_read, 6)
        gates(2)
        gates(3)
        pe.wait_ge(pj_free, G_END)
        ada_chunk(6, bank[0])
        ada_chunk(7, bank[1])
        rec(3)
        pe.wait_ge(lv_free, 16 * RH)
        for j in range(8, 12):
            ada_chunk(j, bank[j - 4])
        pe.wait_ge(ro_free, 2 * RH)
        pe.wait_ge(on_ready, 2)
        for n in range(2 * RH):
            h, k = divmod(n, 2)
            if n >= 2:
                pe.wait_ge(rt_lo, n - 1)
            turn4(bank[2 + n % 2], [rg_tok[:, 4 * k + c, h * P:(h + 1) * P] for c in range(4)]).then_inc(rt_full, 1)
        pe.wait_ge(rt_lo, 2 * RH)
        pe.wait_ge(grow_ready, 2)
        pe.wait_ge(mod_read, 8)

        def scores(i):
            b, h = ITEMS[i]
            n, lo, kt = P * (b + 1), HD * (h % 2), kT[h // 4]
            if i >= 2:
                pe.wait_ge(s_read, i - 1)
            for c0 in range(0, n, HALF):
                c1 = min(n, c0 + HALF)
                last = pe.matmul(pp[1 + i % 2][:, c0:c1], qT[lo:lo + HD, h // 2, b * P:(b + 1) * P], kt[lo:lo + HD, c0:c1], start=True, stop=True)
            last.then_inc(s_full, 1)

        def turn(i):
            b, h = ITEMS[i]
            pe.wait_ge(p_ready, i + 1)
            for k in range((b + 4) // 4):
                g = PT_GROUPS[i] + k
                if g >= 2:
                    pe.wait_ge(pt_free, g - 1)
                turn4(bank[6 + g % 2], [p_buf[i % 2][:, c * P:(c + 1) * P] for c in range(4 * k, min(4 * k + 4, b + 1))]).then_inc(pt_full, 1)

        def weigh(i):
            b, h = ITEMS[i]
            pe.wait_ge(pt_free, PT_GROUPS[i + 1])
            if h == 0 and b >= 2:
                pe.wait_ge(attn_lo_ready, b - 1)
            product(bank[b % 2][:, h * HD:(h + 1) * HD],
                    [(pT[i % 2][:, c, :], v_tok[:, c, (h // 4) * HD:(h // 4 + 1) * HD]) for c in range(b + 1)]).then_inc(pv_full, 1)

        def attn_out(b):
            pe.wait_ge(o_read, b + 1)
            turn4(bank[b % 2], [attn_tok[:, m * P:(m + 1) * P] for m in range(4)]).then_inc(at_full, 1)

        for i in range(len(ITEMS) + 2):
            if i < len(ITEMS):
                scores(i)
            if 1 <= i <= len(ITEMS):
                turn(i - 1)
            if i >= 2:
                weigh(i - 2)
                if ITEMS[i - 2][1] == 3 and i - 2 >= NH:
                    attn_out(ITEMS[i - 2][0] - 1)
        attn_out(NT - 1)
        pe.wait_ge(attn_lo_ready, NT)
        for m in range(KD):
            pe.wait_ge(lo_ready, m + 1)
            if m >= 2:
                pe.wait_ge(y_gated, m - 1)
            for r, (hi, lo) in enumerate(((attn_hi, attn_lo), (rec_hi, rec_lo))):
                for hf in range(2):
                    cols = slice(hf * HALF, (hf + 1) * HALF)
                    w = [slice((4 * r + k) * P, (4 * r + k + 1) * P) for k in range(4)]
                    last = split_product(bank[4 * (m % 2) + 2 * r + hf],
                                         [(w_hi[m % 2][:, w[k]], w_lo[m % 2][:, w[k]], hi[:, k, cols], lo[:, k, cols]) for k in range(4)])
                last.then_inc(w_used if r else y_full, 1)

        def rows(n, ah, al, full, start=False, stop=False, gated=None):
            for t in range(4):
                a = slice(t * P, (t + 1) * P)
                if gated:
                    pe.wait_ge(gated[0], gated[1] + t)
                for dh in range(2):
                    cols = slice(dh * HALF, (dh + 1) * HALF)
                    last = split_product(bank[2 * t + dh], [(ah[:, a], al[:, a], w_hi[n % 2][:, cols], w_lo[n % 2][:, cols])], start, stop)
                if t == 3:
                    last.then_inc(w_used, 1)
                elif stop:
                    last.then_inc(full, 1)

        pe.wait_ge(y_gated, KD)
        for i in range(2 * KD):
            th, k = divmod(i, KD)
            pe.wait_ge(lo_ready, S_WO + i + 1)
            pe.wait_ge(st_lo, i + 1)
            rows(S_WO + i, mix_hi[i % 2], mix_lo[i % 2], res_full, k == 0, k == KD - 1, (res_gated, 1) if i == KD else None)

        def turn_xn2(hf):
            pe.wait_ge(xn2_ready, 4 * hf + 4)
            for k in range(KD):
                g = hf * KD + k
                if g >= 4:
                    pe.wait_ge(t2_read, g - 3)
                turn4(bank[4 + g % 4], [xn2[4 * hf + t][:, k * P:(k + 1) * P] for t in range(4)]).then_inc(t2_full, 1)

        def hidden(j, m, hf, i=0):
            n = S_FF + 2 * j + m
            if hf == 0:
                pe.wait_ge(lo_ready, i * 4 + (n + 1))
            if not isinstance(i, int):
                pe.wait_ge(hid_ready, i * 4 + (2 * j + hf - 3))
            last = split_product(bank[4 * j + 2 * m + hf],
                                 [(w_hi[n % 2][:, k * P:(k + 1) * P], w_lo[n % 2][:, k * P:(k + 1) * P],
                                   h2_hi[:, k, hf * HALF:(hf + 1) * HALF], h2_lo[:, k, hf * HALF:(hf + 1) * HALF]) for k in range(KD)])
            last.then_inc(w_used if hf else (up_full if m else g_full), 1)

        pe.wait_ge(res_gated, NT)
        turn_xn2(0)
        pe.wait_ge(h2_ready, KD)
        for m in range(2):
            hidden(0, m, 0)
        turn_xn2(1)
        pe.wait_ge(h2_ready, 2 * KD)
        for m in range(2):
            hidden(0, m, 1)
        for m in range(2):
            for hf in range(2):
                hidden(1, m, hf)
        with pe.Fori(1, KF // 2) as i:
            for j in range(2):
                for m in range(2):
                    for hf in range(2):
                        hidden(j, m, hf, i)

        def down_steps(th, steps, i=0):
            for f in steps:
                n, st = S_DN + th * KF + f, ST_DN + th * KF + f
                pe.wait_ge(lo_ready, i * 4 + (n + 1))
                pe.wait_ge(st_lo, i * 4 + (st + 1))
                rows(n, hid_hi[st % 2], hid_lo[st % 2], dn_full, f == 0, f == KF - 1, (dn_gated, 1) if th and f == 0 else None)

        for th in range(2):
            down_steps(th, range(2))
            with pe.Fori(0, DN_LOOP - 1) as i:
                down_steps(th, range(2, 6), i)
            down_steps(th, range(KF - 4, KF))

    @block.vector
    def _(dve):
        steps = [0]

        def link(ins):
            steps[0] += 1
            ins.then_inc(dve_step, 1)
            dve.wait_ge(dve_step, steps[0])

        link(dve.memset(scan_gate[:, :], 1.0))
        link(dve.memset(scan_gate[:, 0:SEQ:P], 0.0))
        link(dve.memset(pT_rec, 0.0))
        dve.wait_ge(vt_full, 1)
        dve.tensor_copy(vcol[:, :], bank[7][:, 0:V_END]).then_inc(vcol_ready, 1)
        dve.wait_ge(cact_ready, 1)
        dve.tensor_copy(c_wide[:, :, :], c_act[:, :].unsqueeze(2).broadcast_to([P, KD, P])).then_inc(cwide_ready, 1)
        dve.wait_ge(mask_loaded, 16)
        link(dve.tensor_copy(lvl_mask[:, :, :], mask_wide.bitcast(I32)))
        dve.wait_ge(xsq_done, NT)
        dve.tensor_scalar(ss[:, 8:16], ss[:, 0:8], 1.0 / D, EPS, ALU.mult, ALU.add).then_inc(ssum1, 1)
        dve.wait_ge(vcol_ready, 1)
        lb0, lb1 = vcol[:, V_LB:V_LB + RH], vcol[:, V_LB + RH:V_LB + 2 * RH]
        link(dve.tensor_tensor(lb[:, :], lb0, lb1, ALU.max))
        dve.tensor_tensor(lb_e[:, 0:RH], lb0, lb[:, :], ALU.subtract)
        dve.tensor_tensor(lb_e[:, RH:2 * RH], lb1, lb[:, :], ALU.subtract).then_inc(lb_ready, 1)
        dve.wait_ge(std1_done, 1)
        link(dve.reciprocal(rstd[:, 8:16], rstd[:, 0:8]))
        for t in range(NT):
            dve.tensor_scalar(x_tok[:, t, :], x_tok[:, t, :], rstd[:, 8 + t:9 + t], None, ALU.mult).then_inc(xn_ready, 1)
        dve.wait_ge(lbe_ready, 1)
        link(dve.tensor_tensor(one_lb[:, :], lb_e[:, 0:RH], lb_e[:, RH:2 * RH], ALU.add))
        link(dve.reciprocal(one_lb[:, :], one_lb[:, :]))
        link(dve.tensor_tensor(lb[:, :], lb_e[:, 0:RH], one_lb[:, :], ALU.mult))
        dve.tensor_scalar(one_lb[:, :], lb[:, :], -1.0, 1.0, ALU.mult, ALU.add).then_inc(lb_ready, 1)
        def mod_columns(j):
            dve.wait_ge(ada_done, 4 * j + 4)
            for c in range(4):
                link(dve.tensor_tensor(vrows[:, :], bank[j if j < 4 else j % 2][:, c * P:(c + 1) * P], ident[:, :], ALU.mult))
                ins = dve.tensor_reduce(mod[:, 4 * j + c:4 * j + c + 1], vrows[:, :], AX.X, ALU.add)
                if c < 3:
                    link(ins)
            ins.then_inc(mod_read, 1)
            dve.wait_ge(mod_read, j + 1)

        dve.wait_ge(ident_ready, 1)
        for j in range(4):
            mod_columns(j)
        link(dve.tensor_tensor(mod[:, 0:16], mod[:, 0:16], vcol[:, V_BADA:V_BADA + 16], ALU.add))
        link(dve.tensor_scalar(gain1[:, :], mod[:, 8:16], 1.0, None, ALU.add))
        link(dve.tensor_tensor(gain1[:, :], gain1[:, :], vcol[:, V_N1:V_N1 + KD], ALU.mult))
        for g in range(16):
            hf, k = divmod(g, KD)
            dve.wait_ge(tr_full, g + 1)
            dve.tensor_scalar(hT[:, k, hf * HALF:(hf + 1) * HALF], bank[2 + g % 4], gain1[:, k:k + 1], mod[:, k:k + 1],
                              ALU.mult, ALU.add).then_inc(tr_free, 1)
        dve.wait_ge(pj_free, G_A + NT)
        dve.tensor_scalar(ss[:, 24:32], ss[:, 16:24], 1.0 / LORA, EPS, ALU.mult, ALU.add).then_inc(ssum2, 1)
        dve.wait_ge(std2_done, 1)
        link(dve.reciprocal(rstd[:, 24:32], rstd[:, 16:24]))
        dve.tensor_tensor(cq_tok, cq_tok, rstd[:, 24:32].unsqueeze(2).broadcast_to([P, NT, LORA]), ALU.mult).then_inc(cqn_ready, 1)
        for n in range(4):
            g = TR_CQ + n
            kk, hf = divmod(n, 2)
            dve.wait_ge(tr_full, g + 1)
            dve.tensor_scalar(cqT[:, kk, hf * HALF:(hf + 1) * HALF], bank[2 + g % 4], vcol[:, V_QN + kk:V_QN + kk + 1], None,
                              ALU.mult).then_inc(tr_free, 1)
        topk_steps = [0, 0, 0]
        i = 0
        for b in SCORED:
            n = P * (b + 1)
            for h in range(NIH):
                dve.wait_ge(sc_relu, i + 1)
                if h == 0:
                    ins = dve.tensor_scalar(W[b], relu_buf[i % 2][:, 0:n], wi[:, b, h:h + 1], None, ALU.mult)
                else:
                    dve.wait_ge(sc_added, i)
                    ins = dve.scalar_tensor_tensor(W[b], relu_buf[i % 2][:, 0:n], wi[:, b, h:h + 1], W[b], ALU.mult, ALU.add)
                ins.then_inc(sc_added, 1)
                i += 1

        def topk(*blocks):
            for b in blocks:
                dve.wait_ge(sc_masked, b - SCORED[0] + 1)
            for r in range(TOPK // 8):
                for j, b in enumerate(blocks):
                    if topk_steps[j]:
                        dve.wait_ge(topk_step, topk_steps[j])
                    dve.max(top8[:, 8 * j:8 * j + 8], W[b]).then_inc(topk_step, 1)
                    topk_steps[2] += 1
                    topk_steps[j] = topk_steps[2]
                for j, b in enumerate(blocks):
                    dve.wait_ge(topk_step, topk_steps[j])
                    dve.match_replace(out=W[b], in_to_replace=top8[:, 8 * j:8 * j + 8], in_values=W[b], imm_value=PICKED).then_inc(topk_step, 1)
                    topk_steps[2] += 1
                    topk_steps[j] = topk_steps[2]
            for j, b in enumerate(blocks):
                dve.wait_ge(topk_step, topk_steps[j])
                dve.tensor_scalar(W[b], W[b], (PICKED + NONCAUSAL) / 2, MASKED, ALU.is_gt, ALU.mult).then_inc(topk_done, 1)

        def cumulate(h):
            dve.wait_ge(g_ready, h + 1)
            if h:
                dve.wait_ge(ro_full, 2 * h)
            dve.tensor_tensor_scan(cumT, scan_gate[:, :], sgT[h % 2], 0.0, ALU.mult, ALU.add).then_inc(cum_ready, 1)

        def rec(h):
            q, nz = rqT[h % 2], 8 * h

            def weigh(u):
                n = h * UNITS + u
                dve.wait_ge(exp_ready, n + 1)
                e = expT[n % 2]
                if u == 0:
                    if h:
                        dve.wait_ge(ro_full, 2 * h)
                    else:
                        dve.wait_ge(pj_free, G_RFQ[h] + 4)
                    dve.tensor_tensor(qaT, q, e, ALU.mult).then_inc(z_ready, 1)
                    return
                z = zT[(nz + u - 1) % 2]
                if u == 1:
                    dve.wait_ge(kk_ready, h + 1)
                    if h:
                        dve.wait_ge(lv_full, 16 * h)
                    dve.tensor_tensor(z, kkT, e, ALU.mult).then_inc(z_ready, 1)
                    return
                if u == 3:
                    dve.wait_ge(kl_full, 2 * h + 2)
                elif u > 3:
                    dve.wait_ge(lv_full, 16 * h + 2 * (u - 2))
                m = P >> (u - 1)
                z4, e4, k4, q4 = (a.rearrange("p (b two m) -> p b two m", two=2, m=m) for a in (z, e, kkT, q))
                dve.tensor_tensor(z4[:, :, 0, :], k4[:, :, 0, :], e4[:, :, 0, :], ALU.mult)
                dve.tensor_tensor(z4[:, :, 1, :], q4[:, :, 1, :], e4[:, :, 1, :], ALU.mult).then_inc(z_ready, 1)

            def place(u):
                for k in range(2):
                    g = 16 * h + 2 * u + k
                    dve.wait_ge(lv_full, g + 1)
                    dve.copy_predicated(pT_rec[:, 4 * k:4 * k + 4, :], lvl_mask[:, u, :].unsqueeze(1).broadcast_to([P, 4, P]),
                                        bank[6 + k].rearrange("p (c t) -> p c t", t=P)).then_inc(lv_free, 1)

            for u in range(3):
                weigh(u)
            weigh(3)
            place(0)
            for c in range(NT - 1):
                if c % 4 == 0:
                    dve.wait_ge(u_full, 2 * h + c // 4 + 1)
                add = bank[4 + c // 4][:, (c % 4) * P:(c % 4 + 1) * P]
                if c == 0:
                    link(dve.tensor_copy(states[:, 1, :], add))
                else:
                    ins = dve.scalar_tensor_tensor(states[:, c + 1, :], states[:, c, :], decay[:, c:c + 1], add, ALU.mult, ALU.add)
                    if c < NT - 2:
                        link(ins)
                    else:
                        ins.then_inc(state_ready, 1)
            for u in range(4, UNITS):
                place(u - 3)
                weigh(u)
            place(6)
            place(7)

        topk(2, 3)
        cumulate(0)
        rec(0)
        cumulate(1)
        topk(4, 5)
        rec(1)
        cumulate(2)
        topk(6)
        mod_columns(4)
        mod_columns(5)
        rec(2)
        cumulate(3)
        topk(7)
        rec(3)
        mod_columns(6)
        mod_columns(7)
        dve.wait_ge(osq_ready, 1)
        link(dve.tensor_reduce(ss[:, 32:64], o_sq.rearrange("p (n c) -> p n c", c=P), AX.X, ALU.add))
        dve.tensor_scalar(ss[:, 32:64], ss[:, 32:64], 1.0 / P, EPS, ALU.mult, ALU.add).then_inc(ssum3, 1)
        dve.wait_ge(std3_done, 1)
        link(dve.reciprocal(rstd[:, 32:64], rstd[:, 32:64]))
        o3 = at(F0, NT * RH, P)
        dve.tensor_tensor(o3, o3, rstd[:, 32:64].unsqueeze(2).broadcast_to([P, NT * RH, P]), ALU.mult).then_inc(on_ready, 1)
        dve.wait_ge(on_ready, 1)
        dve.tensor_tensor(rg_tok, ri_tok, rg_tok, ALU.mult).then_inc(on_ready, 1)
        dve.wait_ge(gb_loaded, 32)
        dve.wait_ge(ada_done, 48)
        dve.tensor_tensor(g1_row, pp[2][:, :], gb_rows[:, 0, :], ALU.add).then_inc(grow_ready, 1)
        dve.tensor_tensor(g2_row, pp[3][:, :], gb_rows[:, 1, :], ALU.add).then_inc(grow_ready, 1)
        dve.wait_ge(on_ready, 2)
        for n in range(2 * RH):
            h, k = divmod(n, 2)
            cols = slice(k * HALF, (k + 1) * HALF)
            dve.wait_ge(rt_free, n + 1)
            dve.scalar_tensor_tensor(rec_lo[:, h, cols], bank[2 + n % 2], vcol[:, V_RN:V_RN + 1], rec_hi[:, h, cols].bitcast(F32),
                                     ALU.mult, ALU.subtract).then_inc(rt_lo, 1)
        link(dve.tensor_tensor(mod[:, 16:32], mod[:, 16:32], vcol[:, V_BADA + 24:V_BADA + 40], ALU.add))
        link(dve.tensor_scalar(gain2[:, :], mod[:, 24:32], 1.0, None, ALU.add))
        link(dve.tensor_tensor(gain2[:, :], gain2[:, :], vcol[:, V_N2:V_N2 + KD], ALU.mult))

        def read_scores(i):
            b, h = ITEMS[i]
            n = P * (b + 1)
            far = max(0, n - 256)
            dve.wait_ge(s_full, i + 1)
            dve.wait_ge(near_ready, i + 1)
            if i >= 2:
                dve.wait_ge(p_ready, i - 1)
            top = nmax[:, i % 16:i % 16 + 1]
            start = 3.0e38
            if far:
                start = far_max[:, i % 2:i % 2 + 1]
                dve.tensor_tensor_reduce(out=s_buf[i % 2][:, 0:far], in0=pp[1 + i % 2][:, 0:far], in1=W[b][:, 0:far], scale=-(HD ** -0.5),
                                         scalar=3.0e38, op0=ALU.add, op1=ALU.min, accum_out=start).then_inc(far_done, 1)
                dve.wait_ge(far_done, i - 2 * NH + 1)
            dve.tensor_tensor_reduce(out=s_buf[i % 2][:, far:n], in0=pp[1 + i % 2][:, far:n], in1=near[i % 2][:, 0:n - far], scale=-(HD ** -0.5),
                                     scalar=start, op0=ALU.add, op1=ALU.min, accum_out=top).then_inc(s_read, 1)

        def attn_norm(b):
            dve.wait_ge(pv_full, NH * (b + 1))
            if b:
                dve.wait_ge(at_full, b)
            link(dve.reciprocal(rinv[:, :], rsum[:, NH * (b % 2):NH * (b % 2) + NH]))
            dve.tensor_tensor(attn_tok.rearrange("p (h c) -> p h c", c=HD), bank[b % 2].rearrange("p (h c) -> p h c", c=HD),
                              rinv[:, :].unsqueeze(2).broadcast_to([P, NH, HD]), ALU.mult).then_inc(o_read, 1)

        def attn_rest(b):
            dve.wait_ge(attn_hi_ready, b + 1)
            cols = slice(b * P, (b + 1) * P)
            dve.tensor_tensor(attn_lo[:, :, cols], bank[b % 2].rearrange("p (c t) -> p c t", t=P), attn_hi[:, :, cols].bitcast(F32),
                              ALU.subtract).then_inc(attn_lo_ready, 1)

        for i in range(len(ITEMS)):
            read_scores(i)
            if i >= NH and i % NH == 7:
                attn_rest(i // NH - 1)
            if i >= NH and i % NH == 3:
                attn_norm(i // NH - 1)
        attn_norm(NT - 1)
        attn_rest(NT - 1)
        split_lo(dve, 0)
        split_lo(dve, 1)
        for m in range(KD):
            dve.wait_ge(gin_loaded[m % 2], 16 * (m // 2 + 1))
            if m:
                dve.wait_ge(mix_ready, m)
            for r in range(2):
                dve.wait_ge(w_used if r else y_full, m + 1)
                ins = dve.tensor_tensor(y_tmp[:, r, :], pp[2 * (m % 2) + r][:, :], gate_in[m % 2][:, r, :], ALU.mult)
            ins.then_inc(y_gated, 1)
            dve.wait_ge(y_gated, m + 1)
            dve.tensor_tensor(mixT[:, m * SEQ:(m + 1) * SEQ], y_tmp[:, 0, :], y_tmp[:, 1, :], ALU.add).then_inc(mix_ready, 1)
            split_lo(dve, m + 2)

        def stationary_lo(st, src, i=0):
            hi, lo = (mix_hi, mix_lo) if st < ST_DN else (hid_hi, hid_lo)
            dve.wait_ge(st_hi, i * 4 + (st + 1))
            dve.tensor_tensor(lo[st % 2][:, :], src, hi[st % 2][:, :].bitcast(F32), ALU.subtract).then_inc(st_lo, 1)

        def gate_rows(t, full, last_step, tmp, gate, gated, added):
            if t % 4 == 3:
                dve.wait_ge(w_used, last_step)
            else:
                dve.wait_ge(full, 3 * (t // 4) + t % 4 + 1)
            if t >= 2:
                dve.wait_ge(added, t - 1)
            dve.tensor_tensor(tmp[t % 2], pp[t % 4][:, :], gate, ALU.mult).then_inc(gated, 1)

        def gate_res(t):
            gate_rows(t, res_full, S_WO + KD * (t // 4 + 1), res_tmp, g1_row, res_gated, x1_ready)

        def norm2(hf):
            dve.wait_ge(sq4_done, 4 * hf + 4)
            dve.tensor_scalar(ss[:, 8 + 4 * hf:12 + 4 * hf], ss[:, 4 * hf:4 * hf + 4], 1.0 / D, EPS, ALU.mult, ALU.add).then_inc(ssum4, 1)
            dve.wait_ge(std4_done, hf + 1)
            link(dve.reciprocal(rstd[:, 8 + 4 * hf:12 + 4 * hf], rstd[:, 4 * hf:4 * hf + 4]))
            if hf == 0:
                dve.wait_ge(x1_stored[0], 16 * 4)
            for t in range(4 * hf, 4 * hf + 4):
                dve.tensor_scalar(xn2[t], x1[:, t, :], rstd[:, 8 + t:9 + t], None, ALU.mult).then_inc(xn2_ready, 1)

        for i in range(2 * KD):
            th, k = divmod(i, KD)
            if i >= 2:
                split_lo(dve, S_WO + i)
            stationary_lo(i, mixT[:, k * SEQ + th * HALF:k * SEQ + (th + 1) * HALF])
            if i == KD:
                gate_res(0)
                gate_res(1)
            if i == KD + 1:
                gate_res(2)
                gate_res(3)
            if i == 13:
                norm2(0)
        split_lo(dve, S_FF)
        for t in range(4, NT):
            gate_res(t)
        split_lo(dve, S_FF + 1)

        def h2_read(g):
            k = g % KD
            dve.wait_ge(t2_full, g + 1)
            if g >= 2:
                dve.wait_ge(h2_ready, g - 1)
            dve.tensor_scalar(h2_tmp[g % 2], bank[4 + g % 4], gain2[:, k:k + 1], mod[:, 16 + k:17 + k], ALU.mult, ALU.add).then_inc(t2_read, 1)

        def h2_rest(g):
            hf, k = divmod(g, KD)
            cols = slice(hf * HALF, (hf + 1) * HALF)
            dve.wait_ge(h2_hi_ready, g + 1)
            dve.tensor_tensor(h2_lo[:, k, cols], h2_tmp[g % 2], h2_hi[:, k, cols].bitcast(F32), ALU.subtract).then_inc(h2_ready, 1)

        for hf in range(2):
            if hf:
                norm2(1)
            for k in range(KD):
                h2_read(hf * KD + k)
                if k:
                    h2_rest(hf * KD + k - 1)
            h2_rest(hf * KD + KD - 1)
        dve.wait_ge(x1_stored[1], 16 * 4)

        def two_hidden(i):
            for j in range(2):
                split_lo(dve, S_FF + 2 * j + 2, i, 4)
                for hf in range(2):
                    dve.wait_ge(silu_ready, i * 4 + (2 * j + hf + 1))
                    if hf:
                        dve.wait_ge(w_used, i * 4 + (S_FF + 2 * j + 2))
                    else:
                        dve.wait_ge(up_full, i * 2 + (j + 1))
                    dve.tensor_tensor(hidT[:, bass.ds(i * (2 * SEQ) + (j * SEQ + hf * HALF), HALF)], bank[4 * j + 2 + hf], silu_buf[2 * j + hf],
                                      ALU.mult).then_inc(hid_ready, 1)
                split_lo(dve, S_FF + 2 * j + 3, i, 4)

        two_hidden(0)
        with dve.Fori(1, KF // 2) as i:
            two_hidden(i)

        def down_steps(th, steps, i=0):
            for f in steps:
                if th or f >= 2:
                    split_lo(dve, S_DN + th * KF + f, i, 4)
                stationary_lo(ST_DN + th * KF + f, hidT[:, bass.ds(i * (4 * SEQ) + (f * SEQ + th * HALF), HALF)], i)

        def gate_down(t):
            gate_rows(t, dn_full, S_DN + KF * (t // 4 + 1), res2_tmp, g2_row, dn_gated, x2_ready)

        def final_norm(hf):
            dve.wait_ge(sq5_done, 4 * hf + 4)
            dve.tensor_scalar(ss[:, 24 + 4 * hf:28 + 4 * hf], ss[:, 16 + 4 * hf:20 + 4 * hf], 1.0 / D, EPS, ALU.mult, ALU.add).then_inc(ssum5, 1)
            dve.wait_ge(std5_done, hf + 1)
            link(dve.reciprocal(rstd[:, 24 + 4 * hf:28 + 4 * hf], rstd[:, 16 + 4 * hf:20 + 4 * hf]))
            for t in range(4 * hf, 4 * hf + 4):
                dve.scalar_tensor_tensor(x1b[:, t, :], x1b[:, t, :], rstd[:, 24 + t:25 + t], fin_row, ALU.mult, ALU.mult).then_inc(y_ready, 1)

        down_steps(0, range(2))
        with dve.Fori(0, DN_LOOP) as i:
            down_steps(0, range(2, 6), i)
        down_steps(1, range(1))
        gate_down(0)
        gate_down(1)
        down_steps(1, range(1, 2))
        gate_down(2)
        gate_down(3)
        with dve.Fori(0, 3) as i:
            down_steps(1, range(2, 6), i)
        dve.wait_ge(fin_loaded, 16)
        final_norm(0)
        with dve.Fori(3, DN_LOOP) as i:
            down_steps(1, range(2, 6), i)
        for t in range(4, NT):
            gate_down(t)
        final_norm(1)


def bucket_steps():
    out = np.zeros((NB, 384), np.float32)
    dist = 255 - np.arange(256)
    exact = NB // 2
    nf = np.maximum(dist, 1).astype(np.float32)
    large = exact + (np.log(nf / np.float32(exact)) / np.float32(math.log(MAXD / exact)) * np.float32(NB - exact)).astype(np.int32)
    bucket = np.where(dist < exact, dist, np.minimum(large, NB - 1))
    out[bucket, np.arange(256)] += 8.0
    out[NB - 1, 0:256] -= 8.0
    return out


def level_masks():
    s, t = np.meshgrid(np.arange(P), np.arange(P), indexing="ij")
    out = [s == t]
    m = P // 2
    while m:
        out.append((s // (2 * m) == t // (2 * m)) & (s % (2 * m) < m) & (t % (2 * m) >= m))
        m //= 2
    return np.ascontiguousarray(np.stack(out, 1).astype(np.int32).reshape(P, 8 * P))


_INS = ["x", "c", "w_ada", "b_ada", "norm1_w", "w_in", "q_norm_w", "w_uq", "w_uq_idx", "rel_bias", "lb_logits", "rec_norm_w",
        "w_branch_attn", "w_branch_rec", "w_out", "norm2_w", "w_ffn_gate", "w_ffn_up", "w_ffn_down", "final_norm_w"]


def kernel(**inputs):
    import concourse.bacc as bacc
    from concourse.bass_utils import run_bass_kernel_spmd

    nc = bacc.Bacc("TRN2", target_bir_lowering=False, num_devices=1)
    arrays = {n: np.ascontiguousarray(inputs[n]) for n in _INS}
    arrays["bucket_steps"] = bucket_steps()
    arrays["level_masks"] = level_masks()
    aps = {n: nc.dram_tensor(f"in_{n}", a.shape, mybir.dt.from_np(a.dtype), kind="ExternalInput").ap() for n, a in arrays.items()}
    aps["out"] = nc.dram_tensor("out_0", [1, SEQ, D], F32, kind="ExternalOutput").ap()
    block_kernel(nc, aps)
    r = run_bass_kernel_spmd(nc, [{f"in_{n}": a for n, a in arrays.items()}], core_ids=[0])
    return r.results[0]["out_0"]
```

```python
import math
from contextlib import ExitStack

import numpy as np

import concourse.bass as bass
from concourse import mybir

F32 = mybir.dt.float32
F32R = mybir.dt.float32r
I32 = mybir.dt.int32
U8 = mybir.dt.uint8
ALU = mybir.AluOpType
ACT = mybir.ActivationFunctionType
AX = mybir.AxisListType

P = 128
SEQ = 1024
D = 1024
KD = D // P
NT = SEQ // P
HALF = 512
NH = 8
HD = 64
LORA = 256
NIH = 8
TOPK = 256
NB = 32
MAXD = 128
RH = 4
RW = RH * P
FF = 2816
KF = FF // P
EPS = 1e-6
C_CQ, C_K, C_V, C_KI, C_WI = 0, 256, 384, 512, 576
C_RQ, C_RF, C_RI, C_RG, C_GATE = 584, 1096, 1608, 2120, 2632

NONCAUSAL = -3.0e38
PICKED = -3.4e38
MASKED = -1.0e30

V_C, V_N1, V_N2, V_QN, V_RN, V_LB, V_BADA, V_END = 0, 8, 16, 24, 26, 27, 35, 83


class Ring:

    def __init__(self, slots):
        self.order, self.src, self.dst, self.slot, self.full, self.free = [], {}, {}, {}, {}, {}
        self.fills, self.last = [0] * slots, [(None, None)] * slots

    def add(self, name, slot, src, dst, done, over=None):
        self.order.append(name)
        self.src[name], self.dst[name], self.slot[name] = src, dst, slot
        self.fills[slot] += len(dst) if isinstance(dst, list) else 1
        self.full[name] = 16 * self.fills[slot]
        free = {}
        for s in over or [slot]:
            now, before = self.last[s]
            if now != done:
                now, before = done, now
            self.last[s] = (now, before)
            if before:
                free[before[0].name] = max(before, free.get(before[0].name, before), key=lambda x: x[1])
        self.free[name] = list(free.values())


def block_kernel(nc, T):
    ctx = ExitStack()
    with ctx:
        build(nc, ctx, T)


def build(nc, ctx, T):
    def sb(name, shape, dt=F32):
        return ctx.enter_context(nc.sbuf_tensor(name, shape, dt))

    def sem(name):
        return ctx.enter_context(nc.semaphore(name))

    arena = sb("arena", [P, 47616])
    arena_base = nc.sbuf_base - 4 * 47616

    def rounded(name, off, *dims):
        return nc.alloc_sbuf_tensor_at(name, [P, *dims], F32R, offset=arena_base + 4 * off)

    def own(name, off, *dims):
        return nc.alloc_sbuf_tensor_at(name, [P, *dims], F32, offset=arena_base + 4 * off)[:]

    def at(off, *dims):
        n = 1
        for d in dims:
            n *= d
        ap = arena[:, off:off + n]
        if len(dims) == 2:
            ap = ap.rearrange("p (a b) -> p a b", a=dims[0])
        if len(dims) == 3:
            ap = ap.rearrange("p (a b c) -> p a b c", a=dims[0], b=dims[1])
        return ap

    A0, B0, C0, D0, E0, F0, G0, H0 = 0, 8192, 12288, 16384, 20480, 25088, 29184, 43520
    hT_hi, hT_lo = rounded("hT_hi", A0, KD, SEQ), rounded("hT_lo", B0, KD, SEQ)
    x_tok = at(G0, NT, D)
    h_tmp = [own(f"h_tmp{i}", G0 + 8192 + HALF * i, HALF) for i in range(4)]
    qT = at(B0, 4, SEQ)
    qiT = at(F0, 4, SEQ)
    kT = [at(D0, SEQ), at(D0 + 1024, SEQ)]
    kiT = at(D0 + 2048, SEQ)
    v_tok = at(D0 + 3072, NT, P)
    W_OFF = [sum(P * (j + 1) for j in range(b)) for b in range(NT)]
    W = [at(E0 + W_OFF[b], P * (b + 1)) for b in range(NT)]
    cq_tok = at(G0, NT, LORA)
    cqT = at(G0 + 2048, 2, SEQ)
    relu_buf = [at(G0 + 4096 + 1024 * i, SEQ) for i in range(2)]
    sq_junk = at(F0, D)
    ri_tok = at(F0, NT, RW)
    rg_tok = at(C0, NT, RW)
    sgT = [at(G0 + 1024 * i, SEQ) for i in range(2)]
    rqT = [at(G0 + 2048 + 1024 * i, SEQ) for i in range(2)]
    kkT = at(G0 + 4096, SEQ)
    cumT = at(G0 + 5120, SEQ)
    expT = [at(G0 + 6144 + 1024 * i, SEQ) for i in range(2)]
    zT = [at(G0 + 8192 + 1024 * i, SEQ) for i in range(2)]
    bias_rev = at(G0 + 8192, NH, 256)
    flip = at(G0 + 10240, P)
    qaT = at(G0 + 10240, SEQ)
    gb_rows = at(G0 + 11264, 2, D)
    mask_wide = at(G0 + 11264, 8, P)
    kl_tok = at(G0 + 11264, NT, P)
    pT_rec = at(G0 + 12288, NT, P)
    states = at(G0 + 13312, NT, P)
    o_sq = at(G0 + 4096, NT * RW)
    s_buf = [at(G0 + 4096 + 1024 * i, SEQ) for i in range(2)]
    p_buf = [at(G0 + 6144 + 1024 * i, SEQ) for i in range(2)]
    pT = [at(G0 + 8192 + 1024 * i, NT, P) for i in range(2)]
    near = [at(G0 + 10240 + 256 * i, 256) for i in range(2)]
    attn_tok = at(G0 + 10752, 512)
    attn_hi, attn_lo = rounded("attn_hi", A0, 4, SEQ), rounded("attn_lo", A0 + 4096, 4, SEQ)
    rec_hi, rec_lo = rounded("rec_hi", G0, 4, SEQ), rounded("rec_lo", F0, 4, SEQ)
    raw = own("raw", H0, 4, SEQ)
    w_hi = [rounded(f"w_hi{i}", o, SEQ) for i, o in enumerate((22528, 40960))]
    w_lo = [rounded(f"w_lo{i}", o + SEQ, SEQ) for i, o in enumerate((22528, 40960))]
    spill = [at(D0 + 2048 + HALF * i, HALF) for i in range(2)]
    gate_in = [own(f"gate_in{i}", G0 + 4096 + 2048 * i, 2, SEQ) for i in range(2)]
    y_tmp = own("y_tmp", G0 + 8192, 2, SEQ)
    mixT = own("mixT", B0, KD * SEQ)
    x1 = own("x1", A0, NT, D)
    mix_hi = [rounded(f"mix_hi{i}", D0 + 1024 * i, HALF) for i in range(2)]
    mix_lo = [rounded(f"mix_lo{i}", D0 + 1024 * i + HALF, HALF) for i in range(2)]
    res_tmp = [own(f"res_tmp{i}", D0 + 2048 + 1024 * i, D) for i in range(2)]
    sq_tmp = own("sq_tmp", D0 + 4096, D)
    h2_hi, h2_lo = rounded("h2_hi", 24576, KD, SEQ), rounded("h2_lo", 32768, KD, SEQ)
    xn2 = [x1[:, t, :] for t in range(4)] + [own(f"xn2_{t}", B0 + D * t, D) for t in range(4)]
    h2_tmp = [own(f"h2_tmp{i}", D0 + HALF * i, HALF) for i in range(2)]
    hidT = own("hidT", A0, KF * SEQ)
    x1b = own("x1b", 24576, NT, D)
    hid_hi = [rounded(f"hid_hi{i}", 32768 + 1024 * i, HALF) for i in range(2)]
    hid_lo = [rounded(f"hid_lo{i}", 32768 + 1024 * i + HALF, HALF) for i in range(2)]
    res2_tmp = [own(f"res2_tmp{i}", 34816 + 1024 * i, D) for i in range(2)]
    fin_row = own("fin_row", 36864, D)
    sq2_tmp = own("sq2_tmp", 37888, D)

    ring_buf = at(H0, 4, 8, P)
    ring_uq = [at(H0 + 1024 * i, 2, 512) for i in range(4)]

    ident = sb("ident", [P, P])
    vrows = sb("vrows", [P, P])
    vcol = sb("vcol", [P, V_END])
    c_act = sb("c_act", [P, KD])
    c_wide = sb("c_wide", [P, KD, P])
    mod = sb("mod", [P, 32])
    gain1 = sb("gain1", [P, KD])
    gain2 = sb("gain2", [P, KD])
    lb = sb("lb", [P, RH])
    one_lb = sb("one_lb", [P, RH])
    lb_e = sb("lb_e", [P, 2 * RH])
    ss = sb("ss", [P, 64])
    rstd = sb("rstd", [P, 64])
    wi = sb("wi", [P, NT, NIH])
    top8 = sb("top8", [P, 16])
    scan_gate = sb("scan_gate", [P, SEQ])
    decay = sb("decay", [P, NT])
    lvl_mask = sb("lvl_mask", [P, 8, P], U8)
    bias8 = sb("bias8", [P, NH, 256])
    early_at = [arena_base + 4 * (H0 + 2 * SEQ), nc.sbuf_base - 4 * 2 * SEQ]
    e_hi = [nc.alloc_sbuf_tensor_at(f"e_hi{i}", [P, SEQ], F32R, offset=o) for i, o in enumerate(early_at)]
    e_lo = [nc.alloc_sbuf_tensor_at(f"e_lo{i}", [P, SEQ], F32R, offset=o + 4 * SEQ) for i, o in enumerate(early_at)]
    brow = sb("brow", [NH, 384])
    rb_sb = sb("rb_sb", [NB, NH])
    bk_sb = at(E0 + 1024, 384)[0:NB, :]
    silu_buf = [bias8.rearrange("p h j -> p (h j)")[:, HALF * i:HALF * (i + 1)] for i in range(4)]
    g1_row = c_wide.rearrange("p k c -> p (k c)")
    g2_row = scan_gate[:, :]
    nmax = sb("nmax", [P, 16])
    rsum = sb("rsum", [P, 16])
    rinv = sb("rinv", [P, 8])
    far_max = sb("far_max", [P, 2])

    pp = [ctx.enter_context(nc.psum_tensor(f"pp{i}", [P, 1024], F32)) for i in range(4)]
    bank = [pp[i // 2][:, (i % 2) * 512:(i % 2) * 512 + 512] for i in range(8)]

    bias_d = nc.dram_tensor("bias_rows", [NH, 384], F32, kind="Internal").ap()
    x1_d = nc.dram_tensor("x1_rows", [SEQ, D], F32, kind="Internal").ap().rearrange("(t p) d -> t p d", p=P)
    q_d = nc.dram_tensor("queries_t", [4 * P, SEQ], F32, kind="Internal").ap()
    rg_d = nc.dram_tensor("rec_gate", [SEQ, RW], F32, kind="Internal").ap()
    gates_d = nc.dram_tensor("gates_t", [2 * D, SEQ], F32, kind="Internal").ap()

    x_d = T["x"][0].rearrange("(t p) d -> t p d", p=P)
    out_d = T["out"][0].rearrange("(t p) d -> t p d", p=P)

    def wtile(w, c0, n=P):
        return w[:, c0:c0 + n].rearrange("(k p) c -> p k c", p=P)

    w_in = T["w_in"][0]
    w_ada = T["w_ada"][0]

    ring_full = [sem(f"ring_full{i}") for i in range(4)]
    vec_loaded = sem("vec_loaded")
    rb_loaded = sem("rb_loaded")
    x_loaded = [sem(f"x_loaded{t}") for t in range(NT)]
    mask_loaded = sem("mask_loaded")
    brow_stored = sem("brow_stored")
    bias_loaded = sem("bias_loaded")
    flip_ready = sem("flip_ready")
    bias_full = sem("bias_full")
    bias_ready = sem("bias_ready")
    ident_ready = sem("ident_ready")
    masks01 = sem("masks01")
    vt_full = sem("vt_full")
    vcol_ready = sem("vcol_ready")
    cact_ready = sem("cact_ready")
    cwide_ready = sem("cwide_ready")
    brow_full = sem("brow_full")
    brow_ready = sem("brow_ready")
    pj_full = sem("pj_full")
    pj_free = sem("pj_free")
    tr_full = sem("tr_full")
    tr_free = sem("tr_free")
    xsq_done = sem("xsq_done")
    std1_done = sem("std1_done")
    ssum1 = sem("ssum1")
    xn_ready = sem("xn_ready")
    lbe_ready = sem("lbe_ready")
    lb_ready = sem("lb_ready")
    cqsq_done = sem("cqsq_done")
    ssum2 = sem("ssum2")
    std2_done = sem("std2_done")
    cqn_ready = sem("cqn_ready")
    sc_full = sem("sc_full")
    sc_relu = sem("sc_relu")
    sc_added = sem("sc_added")
    sc_masked = sem("sc_masked")
    topk_step = sem("topk_step")
    topk_done = sem("topk_done")
    dve_step = sem("dve_step")
    act_step = sem("act_step")
    pool_step = sem("pool_step")
    ada_done = sem("ada_done")
    mod_read = sem("mod_read")
    gb_loaded = sem("gb_loaded")
    spilled = [sem(f"spilled{i}") for i in range(2)]
    q_loaded = sem("q_loaded")
    rg_loaded = sem("rg_loaded")
    e_hi_ready = sem("e_hi_ready")
    e_lo_ready = sem("e_lo_ready")
    rows_used = sem("rows_used")
    ks_full = sem("ks_full")
    ks_read = sem("ks_read")
    hT_hi_ready = sem("hT_hi_ready")
    hT_lo_even = sem("hT_lo_even")
    hT_lo_odd = sem("hT_lo_odd")
    f_ready = sem("f_ready")
    kk_ready = sem("kk_ready")
    g_ready = sem("g_ready")
    cum_ready = sem("cum_ready")
    diff_ready = sem("diff_ready")
    exp_ready = sem("exp_ready")
    z_ready = sem("z_ready")
    kl_full = sem("kl_full")
    kl_free = sem("kl_free")
    u_full = sem("u_full")
    state_ready = sem("state_ready")
    lv_full = sem("lv_full")
    lv_free = sem("lv_free")
    ro_full = sem("ro_full")
    ro_free = sem("ro_free")
    osq_ready = sem("osq_ready")
    ssum3 = sem("ssum3")
    std3_done = sem("std3_done")
    on_ready = sem("on_ready")
    rt_full = sem("rt_full")
    rt_free = sem("rt_free")
    grow_ready = sem("grow_ready")
    near_ready = sem("near_ready")
    s_full = sem("s_full")
    s_read = sem("s_read")
    p_ready = sem("p_ready")
    pt_full = sem("pt_full")
    pt_free = sem("pt_free")
    pv_full = sem("pv_full")
    o_read = sem("o_read")
    at_full = sem("at_full")
    attn_hi_ready = sem("attn_hi_ready")
    attn_lo_ready = sem("attn_lo_ready")
    rt_lo = sem("rt_lo")
    raw_full = [sem(f"raw_full{i}") for i in range(4)]
    hi_ready = sem("hi_ready")
    lo_ready = sem("lo_ready")
    w_used = sem("w_used")
    st_hi = sem("st_hi")
    st_lo = sem("st_lo")
    gin_loaded = [sem(f"gin_loaded{i}") for i in range(2)]
    y_full = sem("y_full")
    y_gated = sem("y_gated")
    mix_ready = sem("mix_ready")
    res_full = sem("res_full")
    res_gated = sem("res_gated")
    x1_ready = sem("x1_ready")
    x1_stored = [sem(f"x1_stored{i}") for i in range(2)]
    sq4_done = sem("sq4_done")
    ssum4 = sem("ssum4")
    std4_done = sem("std4_done")
    xn2_ready = sem("xn2_ready")
    t2_full = sem("t2_full")
    t2_read = sem("t2_read")
    h2_hi_ready = sem("h2_hi_ready")
    h2_ready = sem("h2_ready")
    g_full = sem("g_full")
    up_full = sem("up_full")
    silu_ready = sem("silu_ready")
    hid_ready = sem("hid_ready")
    dn_full = sem("dn_full")
    dn_gated = sem("dn_gated")
    x2_ready = sem("x2_ready")
    far_done = sem("far_done")
    sq5_done = sem("sq5_done")
    ssum5 = sem("ssum5")
    std5_done = sem("std5_done")
    y_ready = sem("y_ready")
    out_stored0 = sem("out_stored0")
    out_stored = sem("out_stored")
    fin_loaded = sem("fin_loaded")

    block = ctx.enter_context(nc.Block())

    G_B = 0
    G_UQI = G_B + 6
    G_UQ = G_UQI + 8
    G_RFQ = [G_UQ + 8, G_UQ + 12, G_UQ + 24, G_UQ + 36]
    G_GATE = [g + 4 for g in G_RFQ[1:]]
    G_GATE.append(G_GATE[2] + 8)
    G_END = G_GATE[3] + 8

    ring = Ring(4)
    ADA_COLS = [D * part + HALF * j for part in (0, 1, 3, 4, 2, 5) for j in range(2)]

    def plan_ada(a, b):
        for j in range(a, b):
            for q in range(4):
                src = w_ada[2 * q * P:2 * (q + 1) * P, ADA_COLS[j]:ADA_COLS[j] + HALF].rearrange("(k p) c -> p k c", p=P)
                ring.add(("ada", j, q), q, src, ring_uq[q], (ada_done, 4 * j + q + 1))

    plan_ada(0, 4)
    E = {}

    def plan_split(name, src, dst):
        s = len(ring.order) % 2
        E[name] = len(E)
        ring.add(name, s, src(s), dst(s), (e_lo_ready, len(E)))

    def plan_tile(name, c0):
        plan_split(name, lambda s: wtile(w_in, c0), lambda s: ring_buf[:, s])

    def plan_rows(name, cols):
        for q in range(4):
            rows = w_in[2 * q * P:2 * (q + 1) * P, :].rearrange("(k p) c -> p k c", p=P)
            at0 = [sum(n for _, n in cols[:i]) for i in range(len(cols))]
            plan_split((name, q), lambda s: [rows[:, :, c0:c0 + n] for c0, n in cols],
                       lambda s: [ring_uq[s][:, :, o:o + n] for o, (_, n) in zip(at0, cols)])

    def plan_rf_rq(h):
        plan_tile(("rf", h), C_RF + h * P)
        plan_tile(("rq", h), C_RQ + h * P)

    def plan_gates(q):
        for j in range(4):
            plan_tile(("gate", q, j), C_GATE + (4 * q + j) * P)

    plan_rows("a", [(C_CQ, 256), (C_V, P), (C_WI, NIH)])
    for name, c0 in (("k0", C_K), ("k1", C_K + HD), ("ki", C_KI)):
        plan_split(name, lambda s: [wtile(w_in, c0, HD)] * 2, lambda s: [ring_buf[:, s, :, 0:HD], ring_buf[:, s, :, HD:P]])
    for name, done in (("uqi", G_UQI + 8), ("uq", G_UQ + 8)):
        slot = len(ring.order) % 2
        ring.add(name, slot, T["w_uq_idx" if name == "uqi" else "w_uq"][0].rearrange("(k p) c -> p k c", p=P), ring_uq[slot], (pj_full, done))
    plan_rf_rq(0)
    plan_rows("ri", [(C_RI, RW)])
    plan_rf_rq(1)
    plan_rows("rg", [(C_RG, RW)])
    plan_gates(0)
    plan_rf_rq(2)
    plan_gates(1)
    plan_rf_rq(3)
    plan_gates(2)
    plan_gates(3)
    plan_ada(4, 12)
    E_NAMES = list(E)
    E_GROUP = {"k0": G_B, "k1": G_B + 2, "ki": G_B + 4}
    for h in range(RH):
        E_GROUP[("rf", h)], E_GROUP[("rq", h)] = G_RFQ[h], G_RFQ[h] + 2
    for q in range(4):
        E_GROUP.update({("gate", q, j): G_GATE[q] + 2 * j for j in range(4)})
    E_USED = [(pj_full, E_GROUP[n] + 2) if n in E_GROUP else (rows_used, 4 * ("a", "ri", "rg").index(n[0]) + n[1] + 1) for n in E_NAMES]

    def split_views(name):
        e, s = E[name], ring.slot[name]
        if name[0] == "a":
            cut = lambda ap: ap.rearrange("p (k c) -> p k c", c=512)[:, :, 0:LORA + P + NIH]
            return ring_uq[s][:, :, 0:LORA + P + NIH], cut(e_hi[e % 2]), cut(e_lo[e % 2])
        return ring_buf[:, s].rearrange("p k c -> p (k c)"), e_hi[e % 2][:, :], e_lo[e % 2][:, :]

    SCORED = list(range(TOPK // P, NT))
    TR_X, TR_CQ = 0, 16
    S_WO = KD
    S_FF = S_WO + 2 * KD
    S_DN = S_FF + 2 * KF
    ST_DN = 2 * KD
    DN_LOOP = (KF - 2) // 4

    def raw_count(n):
        return 32 * (n // 4 + 1) if n < KD else 16 * (KD // 4) + 16 * (n // 4 + 1)

    def split_hi(act, n, i=0, per=0):
        act.wait_ge(raw_full[n % 4], i * (4 * per) + raw_count(n))
        if n >= 2:
            act.wait_ge(w_used, i * per + (n - 1))
        act.activation(w_hi[n % 2][:, :], raw[:, n % 4, :], ACT.Copy).then_inc(hi_ready, 1)

    def split_lo(dve, n, i=0, per=0):
        dve.wait_ge(hi_ready, i * per + (n + 1))
        dve.tensor_tensor(w_lo[n % 2][:, :], raw[:, n % 4, :], w_hi[n % 2][:, :].bitcast(F32), ALU.subtract).then_inc(lo_ready, 1)

    def split_product(out, pairs, start=True, stop=True):
        for k, (ah, al, bh, bl) in enumerate(pairs):
            nc.tensor.matmul(out, ah, bh, start=start and k == 0, stop=False)
            nc.tensor.matmul(out, ah, bl, start=False, stop=False)
            last = nc.tensor.matmul(out, al, bh, start=False, stop=stop and k == len(pairs) - 1)
        return last

    UNITS = 9
    ORDER = list(reversed(range(NT)))
    ITEMS = [(b, h) for b in ORDER for h in range(NH)]
    PT_GROUPS = [0]
    for b, h in ITEMS:
        PT_GROUPS.append(PT_GROUPS[-1] + (b + 4) // 4)

    @block.sync
    def _(sp):
        rows = [
            (V_C, T["c"].rearrange("o (r p) -> (o r) p", p=P), 8),
            (V_N1, T["norm1_w"].rearrange("o (r p) -> (o r) p", p=P), 8),
            (V_N2, T["norm2_w"].rearrange("o (r p) -> (o r) p", p=P), 8),
            (V_QN, T["q_norm_w"].rearrange("o (r p) -> (o r) p", p=P), 2),
            (V_RN, T["rec_norm_w"], 1),
            (V_LB, T["lb_logits"].rearrange("l (r p) -> (l r) p", p=P), 8),
            (V_BADA, T["b_ada"].rearrange("o (r p) -> (o r) p", p=P), 48),
        ]
        for r0, s, n in rows:
            sp.dma_start(vrows[r0:r0 + n, :], s).then_inc(vec_loaded, 16)
        for t in range(NT):
            sp.dma_start(x_tok[:, t, :], x_d[t]).then_inc(x_loaded[t], 16)
        sp.dma_start(mask_wide.bitcast(I32), T["level_masks"].rearrange("p (u t) -> p u t", u=8)).then_inc(mask_loaded, 16)

        def load(name):
            for signal, value in ring.free[name]:
                sp.wait_ge(signal, value)
            dst, src = ring.dst[name], ring.src[name]
            for to, of in zip(dst, src) if isinstance(dst, list) else [(dst, src)]:
                sp.dma_start(to, of).then_inc(ring_full[ring.slot[name]], 16)

        def load_from(a, b):
            for name in ring.order[ring.order.index(a):ring.order.index(b)]:
                load(name)

        load_from(("ada", 0, 0), ("ada", 1, 0))
        sp.dma_start(rb_sb[:, :], T["rel_bias"]).then_inc(rb_loaded, 16)
        sp.dma_start(bk_sb, T["bucket_steps"]).then_inc(rb_loaded, 16)
        load_from(("ada", 1, 0), "uqi")
        sp.wait_ge(brow_ready, 1)
        sp.dma_start(bias_d, brow[:, :]).then_inc(brow_stored, 16)
        load_from("uqi", ("ada", 4, 0))
        sp.wait_ge(pj_full, G_END)
        load_from(("ada", 4, 0), ("ada", 5, 0))
        for i in range(2):
            sp.wait_ge(spilled[i], 16 * 8)
        sp.dma_start(rg_tok, rg_d.rearrange("(t p) c -> p t c", p=P)).then_inc(rg_loaded, 16)
        sp.dma_start(qT, q_d.rearrange("(m p) t -> p m t", p=P)).then_inc(q_loaded, 16)
        sp.wait_ge(ro_full, 2 * RH)
        sp.wait_ge(brow_stored, 16)
        sp.dma_start(bias_rev, bass.AP(bias_d.tensor, 0, [[1, P], [384, NH], [1, 256]])).then_inc(bias_loaded, 16)
        for r, c0 in enumerate((2 * D, 5 * D)):
            sp.dma_start(gb_rows[:, r, :], T["b_ada"][:, c0:c0 + D].broadcast_to([P, D])).then_inc(gb_loaded, 16)
        load_from(("ada", 5, 0), ("ada", 11, 3))
        load(("ada", 11, 3))
        def raw_free(n):
            sp.wait_ge(lo_ready, n - 3)

        sp.wait_ge(ada_done, 48)
        gv = gates_d.rearrange("(g m p) t -> p m g t", g=2, p=P)
        wbr = [T[n][0].rearrange("(k p) c -> p k c", p=P) for n in ("w_branch_attn", "w_branch_rec")]
        for m in range(KD):
            if m >= 4:
                raw_free(m)
            for r in range(2):
                sp.dma_start(raw[:, m % 4, 4 * P * r:4 * P * (r + 1)].rearrange("p (k c) -> p k c", c=P),
                             wbr[r][:, :, m * P:(m + 1) * P]).then_inc(raw_full[m % 4], 16)
            if m == 3:
                sp.wait_ge(at_full, NT)
                for st in range(2):
                    sp.wait_ge(spilled[st], 16 * 24)
                for j in range(2):
                    sp.dma_start(gate_in[j], gv[:, j]).then_inc(gin_loaded[j], 16)
            if m >= 4:
                sp.wait_ge(y_gated, m - 3)
                sp.dma_start(gate_in[m % 2], gv[:, m - 2]).then_inc(gin_loaded[m % 2], 16)
        wo = T["w_out"][0].rearrange("(f p) c -> p f c", p=P)

        def out_tile(i):
            n = S_WO + i
            raw_free(n)
            sp.dma_start(raw[:, n % 4, :], wo[:, i % KD, :]).then_inc(raw_full[n % 4], 16)

        for i in range(4):
            out_tile(i)
            if i in (0, 1):
                sp.wait_ge(y_gated, 5 + i)
                sp.dma_start(gate_in[i], gv[:, 6 + i]).then_inc(gin_loaded[i], 16)
        sp.wait_ge(w_used, KD)
        for t in range(NT):
            sp.dma_start(x1[:, t, :], x_d[t]).then_inc(x_loaded[t], 16)
        for i in range(4, 2 * KD):
            out_tile(i)
        wg = T["w_ffn_gate"][0].rearrange("(k p) c -> p k c", p=P)
        wu = T["w_ffn_up"][0].rearrange("(k p) c -> p k c", p=P)
        wd = T["w_ffn_down"][0].rearrange("(f p) c -> p f c", p=P)

        def ffn_tiles(i):
            for j in range(2):
                for m, w in enumerate((wg, wu)):
                    n = S_FF + 2 * j + m
                    sp.wait_ge(lo_ready, i * 4 + (n - 3))
                    sp.dma_start(raw[:, n % 4, :].rearrange("p (k c) -> p k c", c=P), w[:, :, bass.ds(i * 256 + j * P, P)]).then_inc(raw_full[n % 4], 16)

        ffn_tiles(0)
        with sp.Fori(1, KF // 2) as i:
            ffn_tiles(i)

        def down_steps(th, steps, i=0):
            for f in steps:
                n = S_DN + th * KF + f
                sp.wait_ge(lo_ready, i * 4 + (n - 3))
                sp.dma_start(raw[:, n % 4, :].unsqueeze(1), wd[:, bass.ds(i * 4 + f, 1), :]).then_inc(raw_full[n % 4], 16)

        down_steps(0, range(2))
        with sp.Fori(0, 2) as i:
            down_steps(0, range(2, 6), i)
        for hf in range(2):
            sp.wait_ge(x1_stored[hf], 16 * 4)
        sp.wait_ge(w_used, S_DN)
        for t in range(NT):
            sp.dma_start(x1b[:, t, :], x1_d[t]).then_inc(x_loaded[t], 16)
        sp.dma_start(fin_row, T["final_norm_w"].rearrange("(o d) -> o d", o=1).broadcast_to([P, D])).then_inc(fin_loaded, 16)
        with sp.Fori(2, DN_LOOP) as i:
            down_steps(0, range(2, 6), i)
        down_steps(1, range(2))
        with sp.Fori(0, DN_LOOP) as i:
            down_steps(1, range(2, 6), i)
        for t in range(4, NT):
            sp.wait_ge(y_ready, t + 1)
            sp.dma_start(out_d[t], x1b[:, t, :]).then_inc(out_stored, 16)
        sp.wait_ge(out_stored, 16 * 4)

    @block.gpsimd
    def _(pool):
        pool.memset(ident[:, :], 0.0).then_inc(pool_step, 1)
        pool.wait_ge(pool_step, 1)
        pool.affine_select(out=ident[:, :], in_=ident[:, :], compare_op=ALU.not_equal, fill=1.0, base=0,
                           pattern=[[-1, P]], channel_multiplier=1).then_inc(ident_ready, 1)
        pool.memset(arena[:, E0:E0 + 3 * P], 0.0).then_inc(pool_step, 1)
        pool.wait_ge(pool_step, 2)
        pool.affine_select(out=W[0], in_=W[0], compare_op=ALU.is_ge, fill=MASKED, base=0,
                           pattern=[[-1, P]], channel_multiplier=1).then_inc(masks01, 1)
        pool.affine_select(out=W[1], in_=W[1], compare_op=ALU.is_ge, fill=MASKED, base=P,
                           pattern=[[-1, 2 * P]], channel_multiplier=1).then_inc(masks01, 1)
        for g in range(0, 16, 2):
            k, hf = divmod(g, 2)
            cols = slice(hf * HALF, (hf + 1) * HALF)
            pool.wait_ge(hT_hi_ready, g + 1)
            pool.tensor_tensor(hT_lo[:, k, cols], h_tmp[g % 4], hT_hi[:, k, cols].bitcast(F32), ALU.subtract).then_inc(hT_lo_even, 1)

        def split_rests(a, b):
            for e in range(E[a], E[b] + 1):
                name = E_NAMES[e]
                raw_tile, hi, lo = split_views(name)
                pool.wait_ge(e_hi_ready, e + 1)
                pool.tensor_tensor(lo, raw_tile, hi.bitcast(F32), ALU.subtract).then_inc(e_lo_ready, 1)

        split_rests(("a", 0), "ki")
        for n, b in enumerate(SCORED):
            pool.wait_ge(sc_added, NIH * (n + 1))
            diag = W[b][:, b * P:(b + 1) * P]
            pool.affine_select(out=diag, in_=diag, compare_op=ALU.is_ge, fill=NONCAUSAL, base=0,
                               pattern=[[-1, P]], channel_multiplier=1).then_inc(sc_masked, 1)
        for h in range(RH):
            if h == 0:
                split_rests(("rf", 0), ("rq", 0))
            pool.wait_ge(lb_ready, 1)
            pool.wait_ge(pj_free, G_RFQ[h] + 2)
            pool.tensor_scalar(sgT[h % 2], sgT[h % 2], one_lb[:, h:h + 1], lb[:, h:h + 1], ALU.mult, ALU.add).then_inc(f_ready, 1)
            pool.wait_ge(f_ready, h + 1)
            if h:
                pool.wait_ge(ro_full, 2 * h)
            pool.tensor_scalar(kkT, sgT[h % 2], -1.0, 1.0, ALU.mult, ALU.add).then_inc(kk_ready, 1)
            if h == 0:
                split_rests(("ri", 0), ("gate", 0, 3))
            if h == 1:
                split_rests(("rf", 2), ("gate", 1, 3))
            if h == 2:
                split_rests(("rf", 3), ("gate", 2, 3))
            if h == 3:
                split_rests(("gate", 3, 0), ("gate", 3, 3))
            pool.wait_ge(cum_ready, h + 1)
            a3 = cumT.rearrange("p (c t) -> p c t", t=P)
            for u in range(1, UNITS):
                n = h * UNITS + u
                if n >= 2:
                    pool.wait_ge(z_ready, n - 1)
                e = expT[n % 2]
                if u == 1:
                    pool.tensor_tensor(e.rearrange("p (c t) -> p c t", t=P), a3[:, :, P - 1:P].broadcast_to([P, NT, P]), a3,
                                       ALU.subtract).then_inc(diff_ready, 1)
                    continue
                m = P >> (u - 1)
                a4 = cumT.rearrange("p (b two m) -> p b two m", two=2, m=m)
                e4 = e.rearrange("p (b two m) -> p b two m", two=2, m=m)
                nb = SEQ // (2 * m)
                ref = a4[:, :, 0, m - 1:m].broadcast_to([P, nb, m])
                pool.tensor_tensor(e4[:, :, 0, :], ref, a4[:, :, 0, :], ALU.subtract)
                pool.tensor_tensor(e4[:, :, 1, :], a4[:, :, 1, :], ref, ALU.subtract).then_inc(diff_ready, 1)
        pool.wait_ge(ro_full, 2 * RH)
        pool.memset(flip, 0.0).then_inc(pool_step, 1)
        pool.wait_ge(pool_step, 3)
        pool.affine_select(out=flip, in_=flip, compare_op=ALU.not_equal, fill=1.0, base=1 - P,
                           pattern=[[1, P]], channel_multiplier=1).then_inc(flip_ready, 1)
        pool.wait_ge(bias_ready, 4)
        pool.wait_ge(masks01, 2)
        pool.wait_ge(topk_done, len(SCORED))
        pool.wait_ge(on_ready, 2)
        for i, (b, h) in enumerate(ITEMS):
            if i >= 2:
                pool.wait_ge(s_read, i - 1)
            n = min(256, P * (b + 1))
            pool.tensor_tensor(near[i % 2][:, 0:n], bias8[:, h, 256 - n:256], W[b][:, P * (b + 1) - n:P * (b + 1)],
                               ALU.add).then_inc(near_ready, 1)
        for t in range(NT):
            pool.wait_ge(res_gated, t + 1)
            pool.wait_ge(x_loaded[t], 32)
            pool.tensor_tensor(x1[:, t, :], x1[:, t, :], res_tmp[t % 2], ALU.add).then_inc(x1_ready, 1)
        for t in range(NT):
            pool.wait_ge(dn_gated, t + 1)
            pool.wait_ge(x_loaded[t], 48)
            pool.tensor_tensor(x1b[:, t, :], x1b[:, t, :], res2_tmp[t % 2], ALU.add).then_inc(x2_ready, 1)
            if t == 3:
                for u in range(4):
                    pool.wait_ge(y_ready, u + 1)
                    pool.dma_start(out_d[u], x1b[:, u, :]).then_inc(out_stored0, 16)
        pool.wait_ge(out_stored0, 16 * 4)

    @block.scalar
    def _(act):
        steps = [0]

        def link(ins):
            steps[0] += 1
            ins.then_inc(act_step, 1)
            act.wait_ge(act_step, steps[0])

        def evac(g, out, in_, f=ACT.Copy, **kw):
            act.wait_ge(pj_full, g + 1)
            act.activation(out, in_, f, **kw).then_inc(pj_free, 1)

        hi_done = [0]

        def split_to(last):
            while hi_done[0] <= last:
                e = hi_done[0]
                name = E_NAMES[e]
                raw_tile, hi, _ = split_views(name)
                act.wait_ge(ring_full[ring.slot[name]], ring.full[name])
                if e >= 2:
                    act.wait_ge(*E_USED[e - 2])
                else:
                    act.wait_ge(ada_done, 16)
                act.activation(hi, raw_tile, ACT.Copy).then_inc(e_hi_ready, 1)
                hi_done[0] += 1

        def split_ahead(name):
            split_to(E[name])
            e = E[name] + 1
            if e < len(E) and ring.order.index(E_NAMES[e]) == ring.order.index(name) + 1:
                split_to(e)

        act.wait_ge(vcol_ready, 1)
        act.activation(c_act[:, :], vcol[:, V_C:V_C + KD], ACT.Silu).then_inc(cact_ready, 1)
        for t in range(NT):
            act.wait_ge(x_loaded[t], 16)
            if t:
                act.wait_ge(xsq_done, t)
            act.activation(sq_junk, x_tok[:, t, :], ACT.Square, accum_out=ss[:, t:t + 1]).then_inc(xsq_done, 1)
        act.wait_ge(ssum1, 1)
        act.activation(rstd[:, 0:8], ss[:, 8:16], ACT.Sqrt).then_inc(std1_done, 1)
        act.wait_ge(lb_ready, 1)
        act.activation(lb_e[:, :], lb_e[:, :], ACT.Exp).then_inc(lbe_ready, 1)
        act.wait_ge(brow_full, 1)
        act.activation(brow[:, :], bank[6][0:NH, 0:384], ACT.Copy).then_inc(brow_ready, 1)
        for g in range(16):
            k, hf = divmod(g, 2)
            act.wait_ge(tr_free, g + 1)
            act.activation(hT_hi[:, k, hf * HALF:(hf + 1) * HALF], h_tmp[g % 4], ACT.Copy).then_inc(hT_hi_ready, 1)
            if g in (1, 3):
                split_to(g // 2)

        def wait_rows(n, t):
            if t == 7:
                act.wait_ge(rows_used, 4 * (n + 1))
            else:
                act.wait_ge(ks_full, 7 * n + t + 1)

        split_to(E["k0"])
        for t in range(NT):
            wait_rows(0, t)
            ps = bank[t]
            act.activation(sq_junk[:, 256 * (t % 4):256 * (t % 4) + LORA], ps[:, 0:LORA], ACT.Square, accum_out=ss[:, 16 + t:17 + t]).then_inc(cqsq_done, 1)
            if t >= 3:
                act.wait_ge(cqsq_done, t - 2)
            act.activation(cq_tok[:, t, :], ps[:, 0:LORA], ACT.Copy)
            act.activation(v_tok[:, t, :], ps[:, 256:384], ACT.Copy)
            act.activation(wi[:, t, :], ps[:, 384:392], ACT.Copy, scale=(NIH ** -0.5) * (HD ** -0.5)).then_inc(ks_read, 1)
        act.wait_ge(ssum2, 1)
        act.activation(rstd[:, 16:24], ss[:, 24:32], ACT.Sqrt).then_inc(std2_done, 1)
        for m, dst in enumerate((kT[0], kT[1], kiT)):
            split_ahead(("k0", "k1", "ki")[m])
            for hf in range(2):
                g = G_B + 2 * m + hf
                evac(g, dst[:, hf * HALF:(hf + 1) * HALF], bank[g % 2])
        for m in range(4):
            for hf in range(2):
                g = G_UQI + 2 * m + hf
                evac(g, qiT[:, m, hf * HALF:(hf + 1) * HALF], bank[g % 2])
        i = 0
        for b in SCORED:
            n = P * (b + 1)
            for h in range(NIH):
                act.wait_ge(sc_full, i + 1)
                if i >= 2:
                    act.wait_ge(sc_added, i - 1)
                act.activation(relu_buf[i % 2][:, 0:n], pp[1 + i % 2][:, 0:n], ACT.Relu).then_inc(sc_relu, 1)
                i += 1
        spills = [0]

        def to_dram(g, f, dst, in_=None):
            n = spills[0]
            spills[0] += 1
            if n >= 2:
                act.wait_ge(spilled[n % 2], 16 * (n // 2))
            if in_ is None:
                evac(g, spill[n % 2], bank[g % 2], f)
                act.wait_ge(pj_free, g + 1)
            else:
                act.activation(spill[n % 2], in_, f).then_inc(ks_read, 1)
                act.wait_ge(ks_read, g)
            act.dma_start(dst, spill[n % 2]).then_inc(spilled[n % 2], 16)

        qD = q_d.rearrange("(m p) t -> m p t", p=P)
        for m in range(4):
            for hf in range(2):
                to_dram(G_UQ + 2 * m + hf, ACT.Copy, qD[m, :, hf * HALF:(hf + 1) * HALF])

        def rfq(h):
            for k, (dst, f) in enumerate(((sgT[h % 2], ACT.Sigmoid), (rqT[h % 2], ACT.Silu))):
                split_ahead((("rf", "rq")[k], h))
                for hf in range(2):
                    g = G_RFQ[h] + 2 * k + hf
                    evac(g, dst[:, hf * HALF:(hf + 1) * HALF], bank[g % 2], f)

        def logf(h):
            act.wait_ge(f_ready, h + 1)
            act.wait_ge(kk_ready, h + 1)
            act.activation(sgT[h % 2], sgT[h % 2], ACT.Ln).then_inc(g_ready, 1)

        def exponentials(h, u):
            n = h * UNITS + u
            if u == 0:
                if n >= 2:
                    act.wait_ge(z_ready, n - 1)
                act.activation(expT[n % 2], cumT, ACT.Exp).then_inc(exp_ready, 1)
            else:
                act.wait_ge(diff_ready, h * (UNITS - 1) + u)
                act.activation(expT[n % 2], expT[n % 2], ACT.Exp).then_inc(exp_ready, 1)

        def rec_start(h):
            act.wait_ge(cum_ready, h + 1)
            a3 = cumT.rearrange("p (c t) -> p c t", t=P)
            act.activation(decay[:, :].unsqueeze(2), a3[:, :, P - 1:P], ACT.Exp).then_inc(act_step, 1)
            steps[0] += 1
            exponentials(h, 0)
            exponentials(h, 1)

        def rec(h):
            for u in range(2, UNITS):
                exponentials(h, u)
                if u == 2:
                    for k in range(2):
                        act.wait_ge(kl_full, 2 * h + k + 1)
                        act.activation(kl_tok[:, 4 * k:4 * k + 4, :], bank[2 + k].rearrange("p (c t) -> p c t", t=P),
                                       ACT.Copy).then_inc(kl_free, 1)
            for k in range(2):
                act.wait_ge(ro_full, 2 * h + k + 1)
                act.activation(ri_tok[:, 4 * k:4 * k + 4, h * P:(h + 1) * P], bank[2 + k].rearrange("p (c t) -> p c t", t=P),
                               ACT.Copy).then_inc(ro_free, 1)

        gT = gates_d.rearrange("(m p) t -> m p t", p=P)

        def gates(q):
            for j in range(8):
                if j == 6:
                    rec_start(q)
                if j % 2 == 0:
                    split_ahead(("gate", q, j // 2))
                to_dram(G_GATE[q] + j, ACT.Sigmoid, gT[4 * q + j // 2, :, (j % 2) * HALF:(j % 2 + 1) * HALF])

        rfq(0)
        logf(0)
        split_to(E[("rf", 1)])
        for t in range(NT):
            wait_rows(1, t)
            act.activation(ri_tok[:, t, :], bank[t], ACT.Copy).then_inc(ks_read, 1)
        rfq(1)
        split_to(E[("gate", 0, 0)])
        rgD = rg_d.rearrange("(t p) c -> t p c", p=P)
        for t in range(NT):
            wait_rows(2, t)
            to_dram(2 * NT + t + 1, ACT.Silu, rgD[t], bank[t])
        gates(0)
        rec(0)
        logf(1)
        rfq(2)
        gates(1)
        rec(1)
        logf(2)
        rfq(3)
        gates(2)
        rec(2)
        logf(3)
        gates(3)
        rec(3)
        act.wait_ge(ro_free, 2 * RH)
        act.activation(o_sq, ri_tok.rearrange("p t c -> p (t c)"), ACT.Square).then_inc(osq_ready, 1)
        act.wait_ge(ssum3, 1)
        act.activation(rstd[:, 32:64], ss[:, 32:64], ACT.Sqrt).then_inc(std3_done, 1)
        for n in range(8):
            h, k = divmod(n, 2)
            act.wait_ge(rt_full, n + 1)
            act.activation(rec_hi[:, h, k * HALF:(k + 1) * HALF], bank[2 + n % 2], ACT.Copy,
                           scale=vcol[:, V_RN:V_RN + 1]).then_inc(rt_free, 1)

        for j in range(4):
            act.wait_ge(bias_full, j + 1)
            act.activation(bias8[:, 2 * j:2 * j + 2, :], bank[j % 2].rearrange("p (h j) -> p h j", h=2), ACT.Copy).then_inc(bias_ready, 1)

        def softmax(i):
            b, h = ITEMS[i]
            n = P * (b + 1)
            act.wait_ge(s_read, i + 1)
            if i >= 2:
                act.wait_ge(pt_full, PT_GROUPS[i - 1])
            if i >= 16:
                act.wait_ge(o_read, (i - 16) // NH + 1)
            act.activation(p_buf[i % 2][:, 0:n], s_buf[i % 2][:, 0:n], ACT.Exp, bias=nmax[:, i % 16:i % 16 + 1], scale=-1.0,
                           accum_out=rsum[:, i % 16:i % 16 + 1]).then_inc(p_ready, 1)

        def unload(i):
            b, h = ITEMS[i]
            if i >= 2:
                act.wait_ge(pv_full, i - 1)
            for k in range((b + 4) // 4):
                n = min(4, b + 1 - 4 * k)
                g = PT_GROUPS[i] + k
                act.wait_ge(pt_full, g + 1)
                act.activation(pT[i % 2][:, 4 * k:4 * k + n, :], bank[6 + g % 2][:, 0:n * P].rearrange("p (c t) -> p c t", t=P),
                               ACT.Copy).then_inc(pt_free, 1)

        def attn_out(b):
            act.wait_ge(at_full, b + 1)
            act.activation(attn_hi[:, :, ORDER[b] * P:(ORDER[b] + 1) * P], bank[b % 2].rearrange("p (c t) -> p c t", t=P), ACT.Copy).then_inc(attn_hi_ready, 1)

        for i in range(len(ITEMS)):
            softmax(i)
            if i >= 1:
                unload(i - 1)
            if i >= NH and i % NH == 6:
                attn_out(i // NH - 1)
        unload(len(ITEMS) - 1)
        attn_out(NT - 1)
        for m in range(KD):
            split_hi(act, m)

        def stationary_hi(st, src):
            hi = mix_hi if st < ST_DN else hid_hi
            act.activation(hi[st % 2][:, :], src, ACT.Copy).then_inc(st_hi, 1)

        def square(t):
            act.wait_ge(x1_ready, t + 1)
            if t:
                act.wait_ge(sq4_done, t)
            act.activation(sq_tmp, x1[:, t, :], ACT.Square, accum_out=ss[:, t:t + 1]).then_inc(sq4_done, 1)
            act.dma_start(x1_d[t], x1[:, t, :]).then_inc(x1_stored[t // 4], 16)

        def root(hf):
            act.wait_ge(ssum4, hf + 1)
            act.activation(rstd[:, 4 * hf:4 * hf + 4], ss[:, 8 + 4 * hf:12 + 4 * hf], ACT.Sqrt).then_inc(std4_done, 1)

        for i in range(2 * KD):
            th, k = divmod(i, KD)
            if i == 13:
                for t in range(4):
                    square(t)
            if i == 14:
                root(0)
            split_hi(act, S_WO + i)
            act.wait_ge(mix_ready, k + 1)
            stationary_hi(i, mixT[:, k * SEQ + th * HALF:k * SEQ + (th + 1) * HALF])
        split_hi(act, S_FF)
        split_hi(act, S_FF + 1)
        for g in range(2 * KD):
            hf, k = divmod(g, KD)
            if g == KD:
                for t in range(4, NT):
                    square(t)
                root(1)
            act.wait_ge(t2_read, g + 1)
            act.activation(h2_hi[:, k, hf * HALF:(hf + 1) * HALF], h2_tmp[g % 2], ACT.Copy).then_inc(h2_hi_ready, 1)

        def two_hidden(i):
            for j in range(2):
                for hf in range(2):
                    if hf:
                        act.wait_ge(w_used, i * 4 + (S_FF + 2 * j + 1))
                    else:
                        act.wait_ge(g_full, i * 2 + (j + 1))
                    if not isinstance(i, int):
                        act.wait_ge(hid_ready, i * 4 + (2 * j + hf - 3))
                    act.activation(silu_buf[2 * j + hf], bank[4 * j + hf], ACT.Silu).then_inc(silu_ready, 1)
                for m in range(2):
                    split_hi(act, S_FF + 2 * j + m + 2, i, 4)

        two_hidden(0)
        with act.Fori(1, KF // 2) as i:
            two_hidden(i)

        def down_steps(th, steps, i=0):
            for f in steps:
                st = ST_DN + th * KF + f
                if th or f >= 2:
                    split_hi(act, S_DN + th * KF + f, i, 4)
                else:
                    act.wait_ge(hid_ready, 2 * KF)
                stationary_hi(st, hidT[:, bass.ds(i * (4 * SEQ) + (f * SEQ + th * HALF), HALF)])

        def final_sums(hf):
            for t in range(4 * hf, 4 * hf + 4):
                act.wait_ge(x2_ready, t + 1)
                if t:
                    act.wait_ge(sq5_done, t)
                act.activation(sq2_tmp, x1b[:, t, :], ACT.Square, accum_out=ss[:, 16 + t:17 + t]).then_inc(sq5_done, 1)
            act.wait_ge(ssum5, hf + 1)
            act.activation(rstd[:, 16 + 4 * hf:20 + 4 * hf], ss[:, 24 + 4 * hf:28 + 4 * hf], ACT.Sqrt).then_inc(std5_done, 1)

        down_steps(0, range(2))
        with act.Fori(0, DN_LOOP) as i:
            down_steps(0, range(2, 6), i)
        down_steps(1, range(2))
        with act.Fori(0, 3) as i:
            down_steps(1, range(2, 6), i)
        final_sums(0)
        with act.Fori(3, DN_LOOP) as i:
            down_steps(1, range(2, 6), i)
        final_sums(1)

    @block.tensor
    def _(pe):
        def use(name):
            pe.wait_ge(ring_full[ring.slot[name]], ring.full[name])

        def product(out, pairs):
            for k, (a, b) in enumerate(pairs):
                last = pe.matmul(out, a, b, start=(k == 0), stop=(k == len(pairs) - 1))
            return last

        def turn4(dst, tiles):
            for c, a in enumerate(tiles):
                last = pe.transpose(dst[:, c * P:(c + 1) * P], a, ident[:, :])
            return last

        pe.wait_ge(ident_ready, 1)
        pe.wait_ge(vec_loaded, 16 * 7)
        pe.transpose(bank[7][:, 0:V_END], vrows[0:V_END, :], ident[0:V_END, 0:V_END]).then_inc(vt_full, 1)
        pe.wait_ge(rb_loaded, 32)
        pe.matmul(bank[6][0:NH, 0:384], rb_sb[:, :], bk_sb, start=True, stop=True).then_inc(brow_full, 1)
        pe.wait_ge(cact_ready, 1)

        def ada_chunk(j, out):
            for q in range(4):
                use(("ada", j, q))
                for k in range(2):
                    last = pe.matmul(out, c_wide[:, 2 * q + k, :], ring_uq[ring.slot[("ada", j, q)]][:, k, :], start=(q + k == 0), stop=(q == 3 and k == 1))
                last.then_inc(ada_done, 1)

        pe.wait_ge(cwide_ready, 1)
        for j in range(4):
            ada_chunk(j, bank[j])

        pe.wait_ge(xn_ready, NT)
        for g in range(16):
            k, hf = divmod(g, 2)
            if g == 0:
                pe.wait_ge(mod_read, 4)
            if g >= 4:
                pe.wait_ge(tr_free, g - 3)
            turn4(bank[2 + g % 4], [x_tok[:, 4 * hf + t, k * P:(k + 1) * P] for t in range(4)]).then_inc(tr_full, 1)

        def token_major(n, name, width):
            for q in range(4):
                e = E[(name, q)]
                pe.wait_ge(e_lo_ready, e + 1)
                hi, lo = (w[e % 2].rearrange("p (k c) -> p k c", c=512) for w in (e_hi, e_lo))
                for t in range(NT):
                    cols = slice(t * P, (t + 1) * P)
                    last = split_product(bank[t][:, 0:width], [(hT_hi[:, 2 * q + k, cols], hT_lo[:, 2 * q + k, cols], hi[:, k, 0:width], lo[:, k, 0:width])
                                                               for k in range(2)], q == 0, q == 3)
                    if t == NT - 1:
                        last.then_inc(rows_used, 1)
                    elif q == 3:
                        last.then_inc(ks_full, 1)

        pe.wait_ge(tr_free, 16)
        pe.wait_ge(brow_ready, 1)
        pe.wait_ge(hT_lo_even, 8)
        pe.wait_ge(hT_lo_odd, 8)
        token_major(0, "a", LORA + P + NIH)

        def featmajor(g0, w, rhs, kn):
            for hf in range(2):
                g = g0 + hf
                pe.wait_ge(pj_free, g - 1)
                product(bank[g % 2], [(w(k), rhs[:, k, hf * HALF:(hf + 1) * HALF]) for k in range(kn)]).then_inc(pj_full, 1)

        def one_tile(name, g0):
            e = E[name]
            pe.wait_ge(e_lo_ready, e + 1)
            for hf in range(2):
                g = g0 + hf
                if g >= 2:
                    pe.wait_ge(pj_free, g - 1)
                if g < 2:
                    pe.wait_ge(ks_read, g + 1)
                if g - G_RFQ[1] in (0, 1):
                    pe.wait_ge(ks_read, NT + 1 + g % 2)
                if g - G_GATE[0] in (0, 1):
                    pe.wait_ge(ks_read, 2 * NT + 1 + g % 2)
                cols = slice(hf * HALF, (hf + 1) * HALF)
                split_product(bank[g % 2], [(e_hi[e % 2][:, k * P:(k + 1) * P], e_lo[e % 2][:, k * P:(k + 1) * P],
                                             hT_hi[:, k, cols], hT_lo[:, k, cols]) for k in range(KD)]).then_inc(pj_full, 1)

        for m, name in enumerate(("k0", "k1", "ki")):
            one_tile(name, G_B + 2 * m)
        pe.wait_ge(cqn_ready, 1)
        for n in range(4):
            g = TR_CQ + n
            kk, hf = divmod(n, 2)
            pe.wait_ge(tr_free, g - 3)
            turn4(bank[2 + g % 4], [cq_tok[:, 4 * hf + t, kk * P:(kk + 1) * P] for t in range(4)]).then_inc(tr_full, 1)
        use("uqi")
        w_qi = ring_uq[ring.slot["uqi"]]
        pe.wait_ge(tr_free, 20)
        for m in range(4):
            featmajor(G_UQI + 2 * m, lambda k: w_qi[:, k, m * P:(m + 1) * P], cqT, 2)
        pe.wait_ge(pj_free, G_UQI + 8)
        for i, (b, h) in enumerate([(b, h) for b in SCORED for h in range(NIH)]):
            n, lo = P * (b + 1), HD * (h % 2)
            if i >= 2:
                pe.wait_ge(sc_relu, i - 1)
            for c0 in range(0, n, HALF):
                c1 = min(n, c0 + HALF)
                last = pe.matmul(pp[1 + i % 2][:, c0:c1], qiT[lo:lo + HD, h // 2, b * P:(b + 1) * P], kiT[lo:lo + HD, c0:c1], start=True, stop=True)
            last.then_inc(sc_full, 1)
        use("uq")
        w_q = ring_uq[ring.slot["uq"]]
        for m in range(4):
            featmajor(G_UQ + 2 * m, lambda k: w_q[:, k, m * P:(m + 1) * P], cqT, 2)
        def rfq(h):
            one_tile(("rf", h), G_RFQ[h])
            one_tile(("rq", h), G_RFQ[h] + 2)

        def rec(h):
            q, nz = rqT[h % 2], 8 * h
            if h:
                pe.wait_ge(ro_free, 2 * h)
            else:
                pe.wait_ge(sc_relu, len(SCORED) * NIH)
                pe.wait_ge(ks_read, 3 * NT)
            pe.wait_ge(z_ready, h * UNITS + 2)
            for k in range(2):
                turn4(bank[2 + k], [zT[nz % 2][:, c * P:(c + 1) * P] for c in range(4 * k, 4 * k + 4)]).then_inc(kl_full, 1)

            def level(u):
                a, r = (kkT, q) if u == 0 else (zT[(nz + u) % 2],) * 2
                for k in range(2):
                    g = 16 * h + 2 * u + k
                    if g >= 2:
                        pe.wait_ge(lv_free, g - 1)
                    for c in range(4 * k, 4 * k + 4):
                        last = pe.matmul(bank[6 + k][:, (c % 4) * P:(c % 4 + 1) * P], a[:, c * P:(c + 1) * P], r[:, c * P:(c + 1) * P], start=True, stop=True)
                    last.then_inc(lv_full, 1)

            level(0)
            pe.wait_ge(kl_free, 2 * h + 2)
            for k in range(2):
                for c in range(4 * k, min(4 * k + 4, NT - 1)):
                    last = pe.matmul(bank[4 + k][:, (c % 4) * P:(c % 4 + 1) * P], kl_tok[:, c, :], ri_tok[:, c, h * P:(h + 1) * P], start=True, stop=True)
                last.then_inc(u_full, 1)
            for u in range(1, 8):
                pe.wait_ge(z_ready, h * UNITS + u + 2)
                level(u)
            pe.wait_ge(lv_free, 16 * h + 16)
            pe.wait_ge(state_ready, h + 1)
            for k in range(2):
                for c in range(4 * k, 4 * k + 4):
                    pairs = [(pT_rec[:, c, :], ri_tok[:, c, h * P:(h + 1) * P])]
                    if c:
                        pairs.append((qaT[:, c * P:(c + 1) * P], states[:, c, :]))
                    last = product(bank[2 + k][:, (c % 4) * P:(c % 4 + 1) * P], pairs)
                last.then_inc(ro_full, 1)

        def gates(q):
            for j in range(4):
                one_tile(("gate", q, j), G_GATE[q] + 2 * j)

        rfq(0)
        pe.wait_ge(pj_free, G_RFQ[1])
        pe.wait_ge(sc_relu, len(SCORED) * NIH)
        token_major(1, "ri", RW)
        rfq(1)
        pe.wait_ge(pj_free, G_RFQ[1] + 4)
        pe.wait_ge(ks_read, 2 * NT)
        token_major(2, "rg", RW)
        gates(0)
        rec(0)
        rfq(2)
        gates(1)
        rec(1)
        rfq(3)
        gates(2)
        rec(2)
        gates(3)
        rec(3)
        pe.wait_ge(pj_free, G_END)
        for j in range(4, 8):
            if j >= 6:
                pe.wait_ge(mod_read, j - 1)
            ada_chunk(j, bank[j % 2])
        pe.wait_ge(lv_free, 16 * RH)
        for j in range(8, 12):
            ada_chunk(j, bank[j - 4])
        pe.wait_ge(ro_free, 2 * RH)
        pe.wait_ge(on_ready, 2)
        for n in range(2 * RH):
            h, k = divmod(n, 2)
            if n >= 2:
                pe.wait_ge(rt_lo, n - 1)
            turn4(bank[2 + n % 2], [rg_tok[:, 4 * k + c, h * P:(h + 1) * P] for c in range(4)]).then_inc(rt_full, 1)
        pe.wait_ge(rt_lo, 2 * RH)
        pe.wait_ge(grow_ready, 2)
        pe.wait_ge(mod_read, 8)
        pe.wait_ge(flip_ready, 1)
        pe.wait_ge(bias_loaded, 16)
        for j in range(4):
            if j >= 2:
                pe.wait_ge(bias_ready, j - 1)
            pe.matmul(bank[j % 2], flip, bias_rev[:, 2 * j:2 * j + 2, :], start=True, stop=True).then_inc(bias_full, 1)
        pe.wait_ge(bias_ready, 4)
        pe.wait_ge(q_loaded, 16)

        def scores(i):
            b, h = ITEMS[i]
            n, lo, kt = P * (b + 1), HD * (h % 2), kT[h // 4]
            if i >= 2:
                pe.wait_ge(s_read, i - 1)
            for c0 in range(0, n, HALF):
                c1 = min(n, c0 + HALF)
                last = pe.matmul(pp[1 + i % 2][:, c0:c1], qT[lo:lo + HD, h // 2, b * P:(b + 1) * P], kt[lo:lo + HD, c0:c1], start=True, stop=True)
            last.then_inc(s_full, 1)

        def turn(i):
            b, h = ITEMS[i]
            pe.wait_ge(p_ready, i + 1)
            for k in range((b + 4) // 4):
                g = PT_GROUPS[i] + k
                if g >= 2:
                    pe.wait_ge(pt_free, g - 1)
                turn4(bank[6 + g % 2], [p_buf[i % 2][:, c * P:(c + 1) * P] for c in range(4 * k, min(4 * k + 4, b + 1))]).then_inc(pt_full, 1)

        def weigh(i):
            b, h = ITEMS[i]
            pe.wait_ge(pt_free, PT_GROUPS[i + 1])
            turn_of = i // NH
            if h == 0 and turn_of >= 2:
                pe.wait_ge(attn_lo_ready, turn_of - 1)
            product(bank[turn_of % 2][:, h * HD:(h + 1) * HD],
                    [(pT[i % 2][:, c, :], v_tok[:, c, (h // 4) * HD:(h // 4 + 1) * HD]) for c in range(b + 1)]).then_inc(pv_full, 1)

        def attn_out(b):
            pe.wait_ge(o_read, b + 1)
            turn4(bank[b % 2], [attn_tok[:, m * P:(m + 1) * P] for m in range(4)]).then_inc(at_full, 1)

        for i in range(len(ITEMS) + 2):
            if i < len(ITEMS):
                scores(i)
            if 1 <= i <= len(ITEMS):
                turn(i - 1)
            if i >= 2:
                weigh(i - 2)
                if ITEMS[i - 2][1] == 3 and i - 2 >= NH:
                    attn_out((i - 2) // NH - 1)
        attn_out(NT - 1)
        pe.wait_ge(attn_lo_ready, NT)
        for m in range(KD):
            pe.wait_ge(lo_ready, m + 1)
            if m >= 2:
                pe.wait_ge(y_gated, m - 1)
            for r, (hi, lo) in enumerate(((attn_hi, attn_lo), (rec_hi, rec_lo))):
                for hf in range(2):
                    cols = slice(hf * HALF, (hf + 1) * HALF)
                    w = [slice((4 * r + k) * P, (4 * r + k + 1) * P) for k in range(4)]
                    last = split_product(bank[4 * (m % 2) + 2 * r + hf],
                                         [(w_hi[m % 2][:, w[k]], w_lo[m % 2][:, w[k]], hi[:, k, cols], lo[:, k, cols]) for k in range(4)])
                last.then_inc(w_used if r else y_full, 1)

        def rows(n, ah, al, full, start=False, stop=False, gated=None):
            for t in range(4):
                a = slice(t * P, (t + 1) * P)
                if gated:
                    pe.wait_ge(gated[0], gated[1] + t)
                for dh in range(2):
                    cols = slice(dh * HALF, (dh + 1) * HALF)
                    last = split_product(bank[2 * t + dh], [(ah[:, a], al[:, a], w_hi[n % 2][:, cols], w_lo[n % 2][:, cols])], start, stop)
                if t == 3:
                    last.then_inc(w_used, 1)
                elif stop:
                    last.then_inc(full, 1)

        pe.wait_ge(y_gated, KD)
        for i in range(2 * KD):
            th, k = divmod(i, KD)
            pe.wait_ge(lo_ready, S_WO + i + 1)
            pe.wait_ge(st_lo, i + 1)
            rows(S_WO + i, mix_hi[i % 2], mix_lo[i % 2], res_full, k == 0, k == KD - 1, (res_gated, 1) if i == KD else None)

        def turn_xn2(hf):
            pe.wait_ge(xn2_ready, 4 * hf + 4)
            for k in range(KD):
                g = hf * KD + k
                if g >= 4:
                    pe.wait_ge(t2_read, g - 3)
                turn4(bank[4 + g % 4], [xn2[4 * hf + t][:, k * P:(k + 1) * P] for t in range(4)]).then_inc(t2_full, 1)

        def hidden(j, m, hf, i=0):
            n = S_FF + 2 * j + m
            if hf == 0:
                pe.wait_ge(lo_ready, i * 4 + (n + 1))
            if not isinstance(i, int):
                pe.wait_ge(hid_ready, i * 4 + (2 * j + hf - 3))
            last = split_product(bank[4 * j + 2 * m + hf],
                                 [(w_hi[n % 2][:, k * P:(k + 1) * P], w_lo[n % 2][:, k * P:(k + 1) * P],
                                   h2_hi[:, k, hf * HALF:(hf + 1) * HALF], h2_lo[:, k, hf * HALF:(hf + 1) * HALF]) for k in range(KD)])
            last.then_inc(w_used if hf else (up_full if m else g_full), 1)

        pe.wait_ge(res_gated, NT)
        turn_xn2(0)
        pe.wait_ge(h2_ready, KD)
        for m in range(2):
            hidden(0, m, 0)
        turn_xn2(1)
        pe.wait_ge(h2_ready, 2 * KD)
        for m in range(2):
            hidden(0, m, 1)
        for m in range(2):
            for hf in range(2):
                hidden(1, m, hf)
        with pe.Fori(1, KF // 2) as i:
            for j in range(2):
                for m in range(2):
                    for hf in range(2):
                        hidden(j, m, hf, i)

        def down_steps(th, steps, i=0):
            for f in steps:
                n, st = S_DN + th * KF + f, ST_DN + th * KF + f
                pe.wait_ge(lo_ready, i * 4 + (n + 1))
                pe.wait_ge(st_lo, i * 4 + (st + 1))
                rows(n, hid_hi[st % 2], hid_lo[st % 2], dn_full, f == 0, f == KF - 1, (dn_gated, 1) if th and f == 0 else None)

        for th in range(2):
            down_steps(th, range(2))
            with pe.Fori(0, DN_LOOP - 1) as i:
                down_steps(th, range(2, 6), i)
            down_steps(th, range(KF - 4, KF))

    @block.vector
    def _(dve):
        steps = [0]

        def link(ins):
            steps[0] += 1
            ins.then_inc(dve_step, 1)
            dve.wait_ge(dve_step, steps[0])

        link(dve.memset(scan_gate[:, :], 1.0))
        link(dve.memset(scan_gate[:, 0:SEQ:P], 0.0))
        link(dve.memset(pT_rec, 0.0))
        dve.wait_ge(vt_full, 1)
        dve.tensor_copy(vcol[:, :], bank[7][:, 0:V_END]).then_inc(vcol_ready, 1)
        dve.wait_ge(cact_ready, 1)
        dve.tensor_copy(c_wide[:, :, :], c_act[:, :].unsqueeze(2).broadcast_to([P, KD, P])).then_inc(cwide_ready, 1)
        dve.wait_ge(mask_loaded, 16)
        link(dve.tensor_copy(lvl_mask[:, :, :], mask_wide.bitcast(I32)))
        dve.wait_ge(xsq_done, NT)
        dve.tensor_scalar(ss[:, 8:16], ss[:, 0:8], 1.0 / D, EPS, ALU.mult, ALU.add).then_inc(ssum1, 1)
        dve.wait_ge(vcol_ready, 1)
        lb0, lb1 = vcol[:, V_LB:V_LB + RH], vcol[:, V_LB + RH:V_LB + 2 * RH]
        link(dve.tensor_tensor(lb[:, :], lb0, lb1, ALU.max))
        dve.tensor_tensor(lb_e[:, 0:RH], lb0, lb[:, :], ALU.subtract)
        dve.tensor_tensor(lb_e[:, RH:2 * RH], lb1, lb[:, :], ALU.subtract).then_inc(lb_ready, 1)
        dve.wait_ge(std1_done, 1)
        link(dve.reciprocal(rstd[:, 8:16], rstd[:, 0:8]))
        for t in range(NT):
            dve.tensor_scalar(x_tok[:, t, :], x_tok[:, t, :], rstd[:, 8 + t:9 + t], None, ALU.mult).then_inc(xn_ready, 1)
        dve.wait_ge(lbe_ready, 1)
        link(dve.tensor_tensor(one_lb[:, :], lb_e[:, 0:RH], lb_e[:, RH:2 * RH], ALU.add))
        link(dve.reciprocal(one_lb[:, :], one_lb[:, :]))
        link(dve.tensor_tensor(lb[:, :], lb_e[:, 0:RH], one_lb[:, :], ALU.mult))
        dve.tensor_scalar(one_lb[:, :], lb[:, :], -1.0, 1.0, ALU.mult, ALU.add).then_inc(lb_ready, 1)
        def mod_columns(j):
            dve.wait_ge(ada_done, 4 * j + 4)
            for c in range(4):
                link(dve.tensor_tensor(vrows[:, :], bank[j if j < 4 else j % 2][:, c * P:(c + 1) * P], ident[:, :], ALU.mult))
                ins = dve.tensor_reduce(mod[:, 4 * j + c:4 * j + c + 1], vrows[:, :], AX.X, ALU.add)
                if c < 3:
                    link(ins)
            ins.then_inc(mod_read, 1)
            dve.wait_ge(mod_read, j + 1)

        dve.wait_ge(ident_ready, 1)
        for j in range(4):
            mod_columns(j)
        link(dve.tensor_tensor(mod[:, 0:16], mod[:, 0:16], vcol[:, V_BADA:V_BADA + 16], ALU.add))
        link(dve.tensor_scalar(gain1[:, :], mod[:, 8:16], 1.0, None, ALU.add))
        link(dve.tensor_tensor(gain1[:, :], gain1[:, :], vcol[:, V_N1:V_N1 + KD], ALU.mult))
        def rest_odd(g):
            k, hf = divmod(g, 2)
            cols = slice(hf * HALF, (hf + 1) * HALF)
            dve.wait_ge(hT_hi_ready, g + 1)
            dve.tensor_tensor(hT_lo[:, k, cols], h_tmp[g % 4], hT_hi[:, k, cols].bitcast(F32), ALU.subtract).then_inc(hT_lo_odd, 1)

        for g in range(16):
            k, hf = divmod(g, 2)
            dve.wait_ge(tr_full, g + 1)
            if g >= 4:
                if g % 2:
                    dve.wait_ge(hT_lo_odd, (g - 3) // 2)
                else:
                    dve.wait_ge(hT_lo_even, (g - 2) // 2)
            dve.tensor_scalar(h_tmp[g % 4], bank[2 + g % 4], gain1[:, k:k + 1], mod[:, k:k + 1], ALU.mult, ALU.add).then_inc(tr_free, 1)
            if g % 2 == 0 and g:
                rest_odd(g - 1)
        rest_odd(15)
        dve.wait_ge(ks_read, NT)
        dve.tensor_scalar(ss[:, 24:32], ss[:, 16:24], 1.0 / LORA, EPS, ALU.mult, ALU.add).then_inc(ssum2, 1)
        dve.wait_ge(std2_done, 1)
        link(dve.reciprocal(rstd[:, 24:32], rstd[:, 16:24]))
        dve.tensor_tensor(cq_tok, cq_tok, rstd[:, 24:32].unsqueeze(2).broadcast_to([P, NT, LORA]), ALU.mult).then_inc(cqn_ready, 1)
        for n in range(4):
            g = TR_CQ + n
            kk, hf = divmod(n, 2)
            dve.wait_ge(tr_full, g + 1)
            dve.tensor_scalar(cqT[:, kk, hf * HALF:(hf + 1) * HALF], bank[2 + g % 4], vcol[:, V_QN + kk:V_QN + kk + 1], None,
                              ALU.mult).then_inc(tr_free, 1)
        topk_steps = [0, 0, 0]
        i = 0
        for b in SCORED:
            n = P * (b + 1)
            for h in range(NIH):
                dve.wait_ge(sc_relu, i + 1)
                if h == 0:
                    ins = dve.tensor_scalar(W[b], relu_buf[i % 2][:, 0:n], wi[:, b, h:h + 1], None, ALU.mult)
                else:
                    dve.wait_ge(sc_added, i)
                    ins = dve.scalar_tensor_tensor(W[b], relu_buf[i % 2][:, 0:n], wi[:, b, h:h + 1], W[b], ALU.mult, ALU.add)
                ins.then_inc(sc_added, 1)
                i += 1

        def topk(blocks, first=0, last=TOPK // 8):
            for b in blocks:
                dve.wait_ge(sc_masked, b - SCORED[0] + 1)
            for r in range(first, last):
                for j, b in enumerate(blocks):
                    if topk_steps[j]:
                        dve.wait_ge(topk_step, topk_steps[j])
                    dve.max(top8[:, 8 * j:8 * j + 8], W[b]).then_inc(topk_step, 1)
                    topk_steps[2] += 1
                    topk_steps[j] = topk_steps[2]
                for j, b in enumerate(blocks):
                    dve.wait_ge(topk_step, topk_steps[j])
                    dve.match_replace(out=W[b], in_to_replace=top8[:, 8 * j:8 * j + 8], in_values=W[b], imm_value=PICKED).then_inc(topk_step, 1)
                    topk_steps[2] += 1
                    topk_steps[j] = topk_steps[2]
            if last < TOPK // 8:
                return
            for j, b in enumerate(blocks):
                dve.wait_ge(topk_step, topk_steps[j])
                dve.tensor_scalar(W[b], W[b], (PICKED + NONCAUSAL) / 2, MASKED, ALU.is_gt, ALU.mult).then_inc(topk_done, 1)

        def cumulate(h):
            dve.wait_ge(g_ready, h + 1)
            if h:
                dve.wait_ge(ro_full, 2 * h)
            dve.tensor_tensor_scan(cumT, scan_gate[:, :], sgT[h % 2], 0.0, ALU.mult, ALU.add).then_inc(cum_ready, 1)

        def rec(h):
            q, nz = rqT[h % 2], 8 * h

            def weigh(u):
                n = h * UNITS + u
                dve.wait_ge(exp_ready, n + 1)
                e = expT[n % 2]
                if u == 0:
                    if h:
                        dve.wait_ge(ro_full, 2 * h)
                    else:
                        dve.wait_ge(pj_free, G_RFQ[h] + 4)
                    dve.tensor_tensor(qaT, q, e, ALU.mult).then_inc(z_ready, 1)
                    return
                z = zT[(nz + u - 1) % 2]
                if u == 1:
                    dve.wait_ge(kk_ready, h + 1)
                    if h:
                        dve.wait_ge(lv_full, 16 * h)
                    dve.tensor_tensor(z, kkT, e, ALU.mult).then_inc(z_ready, 1)
                    return
                if u == 3:
                    dve.wait_ge(kl_full, 2 * h + 2)
                elif u > 3:
                    dve.wait_ge(lv_full, 16 * h + 2 * (u - 2))
                m = P >> (u - 1)
                z4, e4, k4, q4 = (a.rearrange("p (b two m) -> p b two m", two=2, m=m) for a in (z, e, kkT, q))
                dve.tensor_tensor(z4[:, :, 0, :], k4[:, :, 0, :], e4[:, :, 0, :], ALU.mult)
                dve.tensor_tensor(z4[:, :, 1, :], q4[:, :, 1, :], e4[:, :, 1, :], ALU.mult).then_inc(z_ready, 1)

            def place(u):
                for k in range(2):
                    g = 16 * h + 2 * u + k
                    dve.wait_ge(lv_full, g + 1)
                    dve.copy_predicated(pT_rec[:, 4 * k:4 * k + 4, :], lvl_mask[:, u, :].unsqueeze(1).broadcast_to([P, 4, P]),
                                        bank[6 + k].rearrange("p (c t) -> p c t", t=P)).then_inc(lv_free, 1)

            for u in range(3):
                weigh(u)
            weigh(3)
            place(0)
            for c in range(NT - 1):
                if c % 4 == 0:
                    dve.wait_ge(u_full, 2 * h + c // 4 + 1)
                add = bank[4 + c // 4][:, (c % 4) * P:(c % 4 + 1) * P]
                if c == 0:
                    link(dve.tensor_copy(states[:, 1, :], add))
                else:
                    ins = dve.scalar_tensor_tensor(states[:, c + 1, :], states[:, c, :], decay[:, c:c + 1], add, ALU.mult, ALU.add)
                    if c < NT - 2:
                        link(ins)
                    else:
                        ins.then_inc(state_ready, 1)
            for u in range(4, UNITS):
                place(u - 3)
                weigh(u)
            place(6)
            place(7)

        topk((2, 3))
        cumulate(0)
        topk((4, 5))
        rec(0)
        cumulate(1)
        topk((6, 7), 0, 14)
        rec(1)
        cumulate(2)
        topk((6, 7), 14, 28)
        rec(2)
        cumulate(3)
        topk((6, 7), 28)
        rec(3)
        dve.wait_ge(osq_ready, 1)
        link(dve.tensor_reduce(ss[:, 32:64], o_sq.rearrange("p (n c) -> p n c", c=P), AX.X, ALU.add))
        dve.tensor_scalar(ss[:, 32:64], ss[:, 32:64], 1.0 / P, EPS, ALU.mult, ALU.add).then_inc(ssum3, 1)
        dve.wait_ge(std3_done, 1)
        link(dve.reciprocal(rstd[:, 32:64], rstd[:, 32:64]))
        o3 = at(F0, NT * RH, P)
        dve.tensor_tensor(o3, o3, rstd[:, 32:64].unsqueeze(2).broadcast_to([P, NT * RH, P]), ALU.mult).then_inc(on_ready, 1)
        dve.wait_ge(on_ready, 1)
        dve.wait_ge(rg_loaded, 16)
        dve.tensor_tensor(rg_tok, ri_tok, rg_tok, ALU.mult).then_inc(on_ready, 1)
        for j in range(4, 8):
            mod_columns(j)
        dve.wait_ge(gb_loaded, 32)
        dve.wait_ge(ada_done, 48)
        dve.tensor_tensor(g1_row, pp[2][:, :], gb_rows[:, 0, :], ALU.add).then_inc(grow_ready, 1)
        dve.tensor_tensor(g2_row, pp[3][:, :], gb_rows[:, 1, :], ALU.add).then_inc(grow_ready, 1)
        dve.wait_ge(on_ready, 2)
        for n in range(2 * RH):
            h, k = divmod(n, 2)
            cols = slice(k * HALF, (k + 1) * HALF)
            dve.wait_ge(rt_free, n + 1)
            dve.scalar_tensor_tensor(rec_lo[:, h, cols], bank[2 + n % 2], vcol[:, V_RN:V_RN + 1], rec_hi[:, h, cols].bitcast(F32),
                                     ALU.mult, ALU.subtract).then_inc(rt_lo, 1)
        link(dve.tensor_tensor(mod[:, 16:32], mod[:, 16:32], vcol[:, V_BADA + 24:V_BADA + 40], ALU.add))
        link(dve.tensor_scalar(gain2[:, :], mod[:, 24:32], 1.0, None, ALU.add))
        link(dve.tensor_tensor(gain2[:, :], gain2[:, :], vcol[:, V_N2:V_N2 + KD], ALU.mult))

        def read_scores(i):
            b, h = ITEMS[i]
            n = P * (b + 1)
            far = max(0, n - 256)
            dve.wait_ge(s_full, i + 1)
            dve.wait_ge(near_ready, i + 1)
            if i >= 2:
                dve.wait_ge(p_ready, i - 1)
            top = nmax[:, i % 16:i % 16 + 1]
            start = 3.0e38
            if far:
                start = far_max[:, i % 2:i % 2 + 1]
                dve.tensor_tensor_reduce(out=s_buf[i % 2][:, 0:far], in0=pp[1 + i % 2][:, 0:far], in1=W[b][:, 0:far], scale=-(HD ** -0.5),
                                         scalar=3.0e38, op0=ALU.add, op1=ALU.min, accum_out=start).then_inc(far_done, 1)
                dve.wait_ge(far_done, sum(bb >= 2 for bb, _ in ITEMS[:i + 1]))
            dve.tensor_tensor_reduce(out=s_buf[i % 2][:, far:n], in0=pp[1 + i % 2][:, far:n], in1=near[i % 2][:, 0:n - far], scale=-(HD ** -0.5),
                                     scalar=start, op0=ALU.add, op1=ALU.min, accum_out=top).then_inc(s_read, 1)

        def attn_norm(b):
            dve.wait_ge(pv_full, NH * (b + 1))
            if b:
                dve.wait_ge(at_full, b)
            link(dve.reciprocal(rinv[:, :], rsum[:, NH * (b % 2):NH * (b % 2) + NH]))
            dve.tensor_tensor(attn_tok.rearrange("p (h c) -> p h c", c=HD), bank[b % 2].rearrange("p (h c) -> p h c", c=HD),
                              rinv[:, :].unsqueeze(2).broadcast_to([P, NH, HD]), ALU.mult).then_inc(o_read, 1)

        def attn_rest(b):
            dve.wait_ge(attn_hi_ready, b + 1)
            cols = slice(ORDER[b] * P, (ORDER[b] + 1) * P)
            dve.tensor_tensor(attn_lo[:, :, cols], bank[b % 2].rearrange("p (c t) -> p c t", t=P), attn_hi[:, :, cols].bitcast(F32),
                              ALU.subtract).then_inc(attn_lo_ready, 1)

        for i in range(len(ITEMS)):
            read_scores(i)
            if i >= NH and i % NH == 7:
                attn_rest(i // NH - 1)
            if i >= NH and i % NH == 3:
                attn_norm(i // NH - 1)
        attn_norm(NT - 1)
        attn_rest(NT - 1)
        split_lo(dve, 0)
        split_lo(dve, 1)
        for m in range(KD):
            dve.wait_ge(gin_loaded[m % 2], 16 * (m // 2 + 1))
            if m:
                dve.wait_ge(mix_ready, m)
            for r in range(2):
                dve.wait_ge(w_used if r else y_full, m + 1)
                ins = dve.tensor_tensor(y_tmp[:, r, :], pp[2 * (m % 2) + r][:, :], gate_in[m % 2][:, r, :], ALU.mult)
            ins.then_inc(y_gated, 1)
            dve.wait_ge(y_gated, m + 1)
            dve.tensor_tensor(mixT[:, m * SEQ:(m + 1) * SEQ], y_tmp[:, 0, :], y_tmp[:, 1, :], ALU.add).then_inc(mix_ready, 1)
            split_lo(dve, m + 2)

        def stationary_lo(st, src, i=0):
            hi, lo = (mix_hi, mix_lo) if st < ST_DN else (hid_hi, hid_lo)
            dve.wait_ge(st_hi, i * 4 + (st + 1))
            dve.tensor_tensor(lo[st % 2][:, :], src, hi[st % 2][:, :].bitcast(F32), ALU.subtract).then_inc(st_lo, 1)

        def gate_rows(t, full, last_step, tmp, gate, gated, added):
            if t % 4 == 3:
                dve.wait_ge(w_used, last_step)
            else:
                dve.wait_ge(full, 3 * (t // 4) + t % 4 + 1)
            if t >= 2:
                dve.wait_ge(added, t - 1)
            dve.tensor_tensor(tmp[t % 2], pp[t % 4][:, :], gate, ALU.mult).then_inc(gated, 1)

        def gate_res(t):
            gate_rows(t, res_full, S_WO + KD * (t // 4 + 1), res_tmp, g1_row, res_gated, x1_ready)

        def norm2(hf):
            dve.wait_ge(sq4_done, 4 * hf + 4)
            dve.tensor_scalar(ss[:, 8 + 4 * hf:12 + 4 * hf], ss[:, 4 * hf:4 * hf + 4], 1.0 / D, EPS, ALU.mult, ALU.add).then_inc(ssum4, 1)
            dve.wait_ge(std4_done, hf + 1)
            link(dve.reciprocal(rstd[:, 8 + 4 * hf:12 + 4 * hf], rstd[:, 4 * hf:4 * hf + 4]))
            if hf == 0:
                dve.wait_ge(x1_stored[0], 16 * 4)
            for t in range(4 * hf, 4 * hf + 4):
                dve.tensor_scalar(xn2[t], x1[:, t, :], rstd[:, 8 + t:9 + t], None, ALU.mult).then_inc(xn2_ready, 1)

        for i in range(2 * KD):
            th, k = divmod(i, KD)
            if i >= 2:
                split_lo(dve, S_WO + i)
            stationary_lo(i, mixT[:, k * SEQ + th * HALF:k * SEQ + (th + 1) * HALF])
            if i == KD:
                gate_res(0)
                gate_res(1)
            if i == KD + 1:
                gate_res(2)
                gate_res(3)
            if i == 13:
                norm2(0)
        split_lo(dve, S_FF)
        for t in range(4, NT):
            gate_res(t)
        split_lo(dve, S_FF + 1)

        def h2_read(g):
            k = g % KD
            dve.wait_ge(t2_full, g + 1)
            if g >= 2:
                dve.wait_ge(h2_ready, g - 1)
            dve.tensor_scalar(h2_tmp[g % 2], bank[4 + g % 4], gain2[:, k:k + 1], mod[:, 16 + k:17 + k], ALU.mult, ALU.add).then_inc(t2_read, 1)

        def h2_rest(g):
            hf, k = divmod(g, KD)
            cols = slice(hf * HALF, (hf + 1) * HALF)
            dve.wait_ge(h2_hi_ready, g + 1)
            dve.tensor_tensor(h2_lo[:, k, cols], h2_tmp[g % 2], h2_hi[:, k, cols].bitcast(F32), ALU.subtract).then_inc(h2_ready, 1)

        for hf in range(2):
            if hf:
                norm2(1)
            for k in range(KD):
                h2_read(hf * KD + k)
                if k:
                    h2_rest(hf * KD + k - 1)
            h2_rest(hf * KD + KD - 1)
        dve.wait_ge(x1_stored[1], 16 * 4)

        def two_hidden(i):
            for j in range(2):
                split_lo(dve, S_FF + 2 * j + 2, i, 4)
                for hf in range(2):
                    dve.wait_ge(silu_ready, i * 4 + (2 * j + hf + 1))
                    if hf:
                        dve.wait_ge(w_used, i * 4 + (S_FF + 2 * j + 2))
                    else:
                        dve.wait_ge(up_full, i * 2 + (j + 1))
                    dve.tensor_tensor(hidT[:, bass.ds(i * (2 * SEQ) + (j * SEQ + hf * HALF), HALF)], bank[4 * j + 2 + hf], silu_buf[2 * j + hf],
                                      ALU.mult).then_inc(hid_ready, 1)
                split_lo(dve, S_FF + 2 * j + 3, i, 4)

        two_hidden(0)
        with dve.Fori(1, KF // 2) as i:
            two_hidden(i)

        def down_steps(th, steps, i=0):
            for f in steps:
                if th or f >= 2:
                    split_lo(dve, S_DN + th * KF + f, i, 4)
                stationary_lo(ST_DN + th * KF + f, hidT[:, bass.ds(i * (4 * SEQ) + (f * SEQ + th * HALF), HALF)], i)

        def gate_down(t):
            gate_rows(t, dn_full, S_DN + KF * (t // 4 + 1), res2_tmp, g2_row, dn_gated, x2_ready)

        def final_norm(hf):
            dve.wait_ge(sq5_done, 4 * hf + 4)
            dve.tensor_scalar(ss[:, 24 + 4 * hf:28 + 4 * hf], ss[:, 16 + 4 * hf:20 + 4 * hf], 1.0 / D, EPS, ALU.mult, ALU.add).then_inc(ssum5, 1)
            dve.wait_ge(std5_done, hf + 1)
            link(dve.reciprocal(rstd[:, 24 + 4 * hf:28 + 4 * hf], rstd[:, 16 + 4 * hf:20 + 4 * hf]))
            for t in range(4 * hf, 4 * hf + 4):
                dve.scalar_tensor_tensor(x1b[:, t, :], x1b[:, t, :], rstd[:, 24 + t:25 + t], fin_row, ALU.mult, ALU.mult).then_inc(y_ready, 1)

        down_steps(0, range(2))
        with dve.Fori(0, DN_LOOP) as i:
            down_steps(0, range(2, 6), i)
        down_steps(1, range(1))
        gate_down(0)
        gate_down(1)
        down_steps(1, range(1, 2))
        gate_down(2)
        gate_down(3)
        with dve.Fori(0, 3) as i:
            down_steps(1, range(2, 6), i)
        dve.wait_ge(fin_loaded, 16)
        final_norm(0)
        with dve.Fori(3, DN_LOOP) as i:
            down_steps(1, range(2, 6), i)
        for t in range(4, NT):
            gate_down(t)
        final_norm(1)


def bucket_steps():
    out = np.zeros((NB, 384), np.float32)
    dist = 255 - np.arange(256)
    exact = NB // 2
    nf = np.maximum(dist, 1).astype(np.float32)
    large = exact + (np.log(nf / np.float32(exact)) / np.float32(math.log(MAXD / exact)) * np.float32(NB - exact)).astype(np.int32)
    bucket = np.where(dist < exact, dist, np.minimum(large, NB - 1))
    out[bucket, np.arange(256)] += 8.0
    out[NB - 1, 0:256] -= 8.0
    return out


def level_masks():
    s, t = np.meshgrid(np.arange(P), np.arange(P), indexing="ij")
    out = [s == t]
    m = P // 2
    while m:
        out.append((s // (2 * m) == t // (2 * m)) & (s % (2 * m) < m) & (t % (2 * m) >= m))
        m //= 2
    return np.ascontiguousarray(np.stack(out, 1).astype(np.int32).reshape(P, 8 * P))


_INS = ["x", "c", "w_ada", "b_ada", "norm1_w", "w_in", "q_norm_w", "w_uq", "w_uq_idx", "rel_bias", "lb_logits", "rec_norm_w",
        "w_branch_attn", "w_branch_rec", "w_out", "norm2_w", "w_ffn_gate", "w_ffn_up", "w_ffn_down", "final_norm_w"]


def kernel(**inputs):
    import concourse.bacc as bacc
    from concourse.bass_utils import run_bass_kernel_spmd

    nc = bacc.Bacc("TRN2", target_bir_lowering=False, num_devices=1)
    arrays = {n: np.ascontiguousarray(inputs[n]) for n in _INS}
    arrays["bucket_steps"] = bucket_steps()
    arrays["level_masks"] = level_masks()
    aps = {n: nc.dram_tensor(f"in_{n}", a.shape, mybir.dt.from_np(a.dtype), kind="ExternalInput").ap() for n, a in arrays.items()}
    aps["out"] = nc.dram_tensor("out_0", [1, SEQ, D], F32, kind="ExternalOutput").ap()
    block_kernel(nc, aps)
    r = run_bass_kernel_spmd(nc, [{f"in_{n}": a for n, a in arrays.items()}], core_ids=[0])
    return r.results[0]["out_0"]
```
